# Optimizing a Trainium2 kernel written in Bass

```python
import math, functools
import jax, jax.numpy as jnp
from jax import lax
import numpy as np

D_MODEL = 1024
BATCH = 1
SEQ = 1024
DEPTH = 1
DEC_BATCH = 8
DEC_SEQ = 8
PAST_LEN = 256
PAGE_SIZE = 128

ATT_WIDTH = D_MODEL // 2
SSM_WIDTH = D_MODEL - ATT_WIDTH
HEAD_DIM = 64
V_DIM = 2 * HEAD_DIM
N_HEADS = ATT_WIDTH // V_DIM
SSM_GROUP = 16
N_SSM_GROUPS = SSM_WIDTH // SSM_GROUP
SSM_STATE = 64
N_EXPERTS = 16
N_EXPERT_GROUPS = 4
EXPERTS_PER_GROUP = N_EXPERTS // N_EXPERT_GROUPS
TOP_K = 2
D_EXPERT = 512
Q_BLOCK = 128
DN_ALPHA = (2 * DEPTH) ** 0.25
DN_BETA = (8 * DEPTH) ** -0.25
LN_EPS = 1e-5
RMS_EPS = 1e-5

kernel_name = "hymba_s5_diffattn_moe_deepnorm_step"

def layer_norm(x, g, b):
    xf = x.astype(jnp.float32)
    mu = jnp.mean(xf, -1, keepdims=True)
    var = jnp.mean(jnp.square(xf - mu), -1, keepdims=True)
    return ((xf - mu) * lax.rsqrt(var + LN_EPS) * g.astype(jnp.float32) + b.astype(jnp.float32)).astype(x.dtype)

def alibi_slopes():
    return 2.0 ** (-8.0 * jnp.arange(1, N_HEADS + 1, dtype=jnp.float32) / N_HEADS)

def diff_attend(q1, q2, k1, k2, v, q_pos, k_pos, lam):
    scale = HEAD_DIM ** -0.5
    dist = (q_pos[:, None] - k_pos[None, :]).astype(jnp.float32)
    bias = jnp.where(dist >= 0, -alibi_slopes()[:, None, None] * dist, -jnp.inf)
    s1 = jnp.einsum('nqhd,nkhd->nhqk', q1, k1, preferred_element_type=jnp.float32) * scale + bias
    s2 = jnp.einsum('nqhd,nkhd->nhqk', q2, k2, preferred_element_type=jnp.float32) * scale + bias
    w = jax.nn.softmax(s1, axis=-1) - lam * jax.nn.softmax(s2, axis=-1)
    return jnp.einsum('nhqk,nkhv->nqhv', w.astype(v.dtype), v)

def attn_prompt(q1, q2, k, v, lam):
    n, s = q1.shape[:2]
    nb = s // Q_BLOCK
    k1, k2 = k[..., :HEAD_DIM], k[..., HEAD_DIM:]
    k_pos = jnp.arange(s)
    to_blocks = lambda q: q.reshape(n, nb, Q_BLOCK, N_HEADS, HEAD_DIM).swapaxes(0, 1)

    def block(args):
        i, qb1, qb2 = args
        q_pos = i * Q_BLOCK + jnp.arange(Q_BLOCK)
        return diff_attend(qb1, qb2, k1, k2, v, q_pos, k_pos, lam)

    out = lax.map(block, (jnp.arange(nb), to_blocks(q1), to_blocks(q2)))
    return out.swapaxes(0, 1).reshape(n, s, N_HEADS, V_DIM)

def attn_sample(q1, q2, k, v, lam, k_pages, v_pages, page_table):
    n, t = q1.shape[:2]
    past = page_table.shape[1] * PAGE_SIZE
    k_past = k_pages[page_table].reshape(n, past, N_HEADS, 2 * HEAD_DIM)
    v_past = v_pages[page_table].reshape(n, past, N_HEADS, V_DIM)
    k_all = jnp.concatenate([k_past, k.astype(k_past.dtype)], axis=1)
    v_all = jnp.concatenate([v_past, v.astype(v_past.dtype)], axis=1)
    q_pos = past + jnp.arange(t)
    k_pos = jnp.arange(past + t)
    return diff_attend(q1, q2, k_all[..., :HEAD_DIM], k_all[..., HEAD_DIM:], v_all, q_pos, k_pos, lam)

def complex_affine_combine(e1, e2):
    a1r, a1i, b1r, b1i = e1
    a2r, a2i, b2r, b2i = e2
    return (a2r * a1r - a2i * a1i,
            a2r * a1i + a2i * a1r,
            a2r * b1r - a2i * b1i + b2r,
            a2r * b1i + a2i * b1r + b2i)

def s5_mixer(u, h0_re, h0_im, lam_re, lam_im, log_dt, b_re, b_im, c_re, c_im, d_skip, w_glu, b_glu):
    n, t, _ = u.shape
    f32 = jnp.float32
    uf = u.astype(f32)
    ug = uf.reshape(n, t, N_SSM_GROUPS, SSM_GROUP)
    lr, li = lam_re.astype(f32), lam_im.astype(f32)
    dt = jnp.exp(log_dt.astype(f32))[:, None]
    mag = jnp.exp(lr * dt)
    a_re, a_im = mag * jnp.cos(li * dt), mag * jnp.sin(li * dt)
    den = lr * lr + li * li
    nr = a_re - 1.0
    coef_re = (nr * lr + a_im * li) / den
    coef_im = (a_im * lr - nr * li) / den
    br, bi = b_re.astype(f32), b_im.astype(f32)
    bb_re = coef_re[..., None] * br - coef_im[..., None] * bi
    bb_im = coef_re[..., None] * bi + coef_im[..., None] * br
    bu_re = jnp.einsum('ntgc,gpc->ntgp', ug, bb_re)
    bu_im = jnp.einsum('ntgc,gpc->ntgp', ug, bb_im)
    shp = bu_re.shape
    elems = (jnp.broadcast_to(a_re, shp), jnp.broadcast_to(a_im, shp), bu_re, bu_im)
    A_re, A_im, H_re, H_im = lax.associative_scan(complex_affine_combine, elems, axis=1)
    h0r = h0_re.astype(f32)[:, None]
    h0i = h0_im.astype(f32)[:, None]
    h_re = H_re + A_re * h0r - A_im * h0i
    h_im = H_im + A_re * h0i + A_im * h0r
    y = (jnp.einsum('ntgp,gcp->ntgc', h_re, c_re.astype(f32))
         - jnp.einsum('ntgp,gcp->ntgc', h_im, c_im.astype(f32)))
    y = y.reshape(n, t, SSM_WIDTH) + d_skip.astype(f32) * uf
    g = jax.nn.gelu(y)
    out = g * jax.nn.sigmoid(g @ w_glu.astype(f32) + b_glu.astype(f32))
    return out.astype(u.dtype), h_re[:, -1], h_im[:, -1]

def route(x2d, router_w, router_bias):
    scores = jax.nn.sigmoid(jnp.dot(x2d, router_w, preferred_element_type=jnp.float32))
    sel = scores + router_bias.astype(jnp.float32)
    grp = sel.reshape(-1, N_EXPERT_GROUPS, EXPERTS_PER_GROUP)
    grp_score = jnp.sum(lax.top_k(grp, TOP_K)[0], axis=-1)
    g_idx = jnp.argmax(grp_score, axis=-1)
    in_grp = (jnp.arange(N_EXPERTS) // EXPERTS_PER_GROUP)[None, :] == g_idx[:, None]
    _, e_idx = lax.top_k(jnp.where(in_grp, sel, -jnp.inf), TOP_K)
    w = jnp.take_along_axis(scores, e_idx, axis=-1)
    w = w / jnp.sum(w, axis=-1, keepdims=True)
    return jnp.sum(jax.nn.one_hot(e_idx, N_EXPERTS, dtype=jnp.float32) * w[..., None], axis=1)

def moe(x, router_w, router_bias, w_gate, w_up, w_down):
    x2 = x.reshape(-1, D_MODEL)
    gates = route(x2, router_w, router_bias)
    out = jnp.zeros(x2.shape, jnp.float32)
    for e in range(N_EXPERTS):
        h = jax.nn.silu(x2 @ w_gate[e]) * (x2 @ w_up[e])
        out = out + gates[:, e:e + 1] * (h @ w_down[e]).astype(jnp.float32)
    return out.astype(x.dtype).reshape(x.shape)

def layer_step(x, attn_fn, h0_re, h0_im, lp, router_w, router_bias, layer_idx):
    n, t, _ = x.shape
    f32 = jnp.float32
    proj = x @ lp['w_in']
    u = proj[..., :SSM_WIDTH]
    q = proj[..., SSM_WIDTH:SSM_WIDTH + ATT_WIDTH].reshape(n, t, N_HEADS, 2, HEAD_DIM)
    k = proj[..., SSM_WIDTH + ATT_WIDTH:SSM_WIDTH + 2 * ATT_WIDTH].reshape(n, t, N_HEADS, 2 * HEAD_DIM)
    v = proj[..., SSM_WIDTH + 2 * ATT_WIDTH:].reshape(n, t, N_HEADS, V_DIM)
    lam_init = 0.8 - 0.6 * math.exp(-0.3 * layer_idx)
    lam = (jnp.exp(jnp.sum(lp['lq1'].astype(f32) * lp['lk1'].astype(f32)))
           - jnp.exp(jnp.sum(lp['lq2'].astype(f32) * lp['lk2'].astype(f32))) + lam_init)
    a = attn_fn(q[..., 0, :], q[..., 1, :], k, v, lam).astype(f32)
    a = a * lax.rsqrt(jnp.mean(a * a, axis=-1, keepdims=True) + RMS_EPS) * lp['subln_g'].astype(f32) * (1.0 - lam_init)
    a = a.reshape(n, t, ATT_WIDTH).astype(x.dtype)
    s, h_re, h_im = s5_mixer(u, h0_re, h0_im, lp['lam_re'], lp['lam_im'], lp['log_dt'], lp['b_re'], lp['b_im'],
                             lp['c_re'], lp['c_im'], lp['d'], lp['w_glu'], lp['b_glu'])
    mix = jnp.concatenate([a, s], axis=-1) @ lp['w_out']
    x = layer_norm(DN_ALPHA * x + mix, lp['ln1_g'], lp['ln1_b'])
    x = layer_norm(DN_ALPHA * x + moe(x, router_w, router_bias, lp['w_gate'], lp['w_up'], lp['w_down']),
                   lp['ln2_g'], lp['ln2_b'])
    return x, k, v, h_re, h_im

def setup_inputs(seed: int = 0) -> dict:
    key = jax.random.key(seed)
    ks = jax.random.split(key, 40)
    f32 = jnp.float32
    nrm = lambda kk, shape, s: s * jax.random.normal(kk, shape, f32)
    n_pages = PAST_LEN // PAGE_SIZE
    n_pool = (DEC_BATCH * n_pages * 5) // 4
    qk_cols = SSM_WIDTH + 2 * ATT_WIDTH
    w_in = jnp.concatenate([nrm(ks[7], (DEPTH, D_MODEL, qk_cols), D_MODEL ** -0.5),
                            nrm(ks[8], (DEPTH, D_MODEL, ATT_WIDTH), DN_BETA * D_MODEL ** -0.5)], axis=-1)
    lam_im = (math.pi * jnp.arange(SSM_STATE, dtype=f32))[None, None, :] + nrm(ks[20], (DEPTH, N_SSM_GROUPS, SSM_STATE), 0.01)
    return {
        "x_prompt": nrm(ks[0], (BATCH, SEQ, D_MODEL), 1.0),
        "x_sample": nrm(ks[1], (DEC_BATCH, DEC_SEQ, D_MODEL), 1.0),
        "cache_k": nrm(ks[2], (DEPTH, n_pool, PAGE_SIZE, N_HEADS, 2 * HEAD_DIM), 1.0),
        "cache_v": nrm(ks[3], (DEPTH, n_pool, PAGE_SIZE, N_HEADS, V_DIM), 1.0),
        "state_ssm_re": nrm(ks[4], (DEPTH, DEC_BATCH, N_SSM_GROUPS, SSM_STATE), 0.5),
        "state_ssm_im": nrm(ks[5], (DEPTH, DEC_BATCH, N_SSM_GROUPS, SSM_STATE), 0.5),
        "page_table": jax.random.permutation(ks[6], n_pool)[:DEC_BATCH * n_pages].reshape(DEC_BATCH, n_pages).astype(jnp.int32),
        "w_in": w_in,
        "w_out": nrm(ks[9], (DEPTH, D_MODEL, D_MODEL), DN_BETA * D_MODEL ** -0.5),
        "ln1_g": 1.0 + nrm(ks[10], (DEPTH, D_MODEL), 0.02),
        "ln1_b": nrm(ks[11], (DEPTH, D_MODEL), 0.02),
        "ln2_g": 1.0 + nrm(ks[12], (DEPTH, D_MODEL), 0.02),
        "ln2_b": nrm(ks[13], (DEPTH, D_MODEL), 0.02),
        "lambda_q1": nrm(ks[14], (DEPTH, HEAD_DIM), 0.1),
        "lambda_k1": nrm(ks[15], (DEPTH, HEAD_DIM), 0.1),
        "lambda_q2": nrm(ks[16], (DEPTH, HEAD_DIM), 0.1),
        "lambda_k2": nrm(ks[17], (DEPTH, HEAD_DIM), 0.1),
        "subln_g": 1.0 + nrm(ks[18], (DEPTH, V_DIM), 0.02),
        "ssm_lambda_re": -0.5 + nrm(ks[19], (DEPTH, N_SSM_GROUPS, SSM_STATE), 0.01),
        "ssm_lambda_im": lam_im,
        "ssm_log_dt": jax.random.uniform(ks[21], (DEPTH, N_SSM_GROUPS), f32, math.log(0.001), math.log(0.1)),
        "ssm_b_re": nrm(ks[22], (DEPTH, N_SSM_GROUPS, SSM_STATE, SSM_GROUP), (2 * SSM_GROUP) ** -0.5),
        "ssm_b_im": nrm(ks[23], (DEPTH, N_SSM_GROUPS, SSM_STATE, SSM_GROUP), (2 * SSM_GROUP) ** -0.5),
        "ssm_c_re": nrm(ks[24], (DEPTH, N_SSM_GROUPS, SSM_GROUP, SSM_STATE), SSM_STATE ** -0.5),
        "ssm_c_im": nrm(ks[25], (DEPTH, N_SSM_GROUPS, SSM_GROUP, SSM_STATE), SSM_STATE ** -0.5),
        "ssm_d": nrm(ks[26], (DEPTH, SSM_WIDTH), 1.0),
        "ssm_w_glu": nrm(ks[27], (DEPTH, SSM_WIDTH, SSM_WIDTH), SSM_WIDTH ** -0.5),
        "ssm_b_glu": nrm(ks[28], (DEPTH, SSM_WIDTH), 0.01),
        "router_w": nrm(ks[29], (D_MODEL, N_EXPERTS), D_MODEL ** -0.5),
        "router_bias": nrm(ks[30], (N_EXPERTS,), 0.01),
        "moe_w_gate": nrm(ks[31], (DEPTH, N_EXPERTS, D_MODEL, D_EXPERT), D_MODEL ** -0.5),
        "moe_w_up": nrm(ks[32], (DEPTH, N_EXPERTS, D_MODEL, D_EXPERT), DN_BETA * D_MODEL ** -0.5),
        "moe_w_down": nrm(ks[33], (DEPTH, N_EXPERTS, D_EXPERT, D_MODEL), DN_BETA * D_EXPERT ** -0.5),
    }

def reference(x_prompt, x_sample, cache_k, cache_v, state_ssm_re, state_ssm_im, page_table,
              w_in, w_out, ln1_g, ln1_b, ln2_g, ln2_b, lambda_q1, lambda_k1, lambda_q2, lambda_k2,
              subln_g, ssm_lambda_re, ssm_lambda_im, ssm_log_dt, ssm_b_re, ssm_b_im, ssm_c_re, ssm_c_im,
              ssm_d, ssm_w_glu, ssm_b_glu, router_w, router_bias, moe_w_gate, moe_w_up, moe_w_down):
    yp, ys = x_prompt, x_sample
    kp, vp, hrp, hip = [], [], [], []
    kss, vss, hrs, his = [], [], [], []
    for l in range(DEPTH):
        lp = dict(w_in=w_in[l], w_out=w_out[l], ln1_g=ln1_g[l], ln1_b=ln1_b[l], ln2_g=ln2_g[l], ln2_b=ln2_b[l],
                  lq1=lambda_q1[l], lk1=lambda_k1[l], lq2=lambda_q2[l], lk2=lambda_k2[l], subln_g=subln_g[l],
                  lam_re=ssm_lambda_re[l], lam_im=ssm_lambda_im[l], log_dt=ssm_log_dt[l],
                  b_re=ssm_b_re[l], b_im=ssm_b_im[l], c_re=ssm_c_re[l], c_im=ssm_c_im[l], d=ssm_d[l],
                  w_glu=ssm_w_glu[l], b_glu=ssm_b_glu[l],
                  w_gate=moe_w_gate[l], w_up=moe_w_up[l], w_down=moe_w_down[l])
        zeros = jnp.zeros((yp.shape[0], N_SSM_GROUPS, SSM_STATE), jnp.float32)
        yp, k_p, v_p, hr_p, hi_p = layer_step(yp, attn_prompt, zeros, zeros, lp, router_w, router_bias, l)
        sample_attn = functools.partial(attn_sample, k_pages=cache_k[l], v_pages=cache_v[l], page_table=page_table)
        ys, k_s, v_s, hr_s, hi_s = layer_step(ys, sample_attn, state_ssm_re[l], state_ssm_im[l], lp,
                                              router_w, router_bias, l)
        kp.append(k_p); vp.append(v_p); hrp.append(hr_p); hip.append(hi_p)
        kss.append(k_s); vss.append(v_s); hrs.append(hr_s); his.append(hi_s)
    return (yp, ys, jnp.stack(kp), jnp.stack(vp), jnp.stack(hrp), jnp.stack(hip),
            jnp.stack(kss), jnp.stack(vss), jnp.stack(hrs), jnp.stack(his))


_drawn_inputs = setup_inputs


def setup_inputs(seed=0):
    import zlib

    import numpy as np

    out = dict(_drawn_inputs(seed))
    spreads = {}
    factors = {'ln2_g': 23.995,
     'ln2_b': 22.827,
     'lambda_q1': 4.243,
     'subln_g': 11.479,
     'ssm_lambda_re': 61.004,
     'ssm_b_glu': 139.921,
     'ssm_c_re': 3.912,
     'ssm_c_im': 3.855}
    for name, (base, spread) in spreads.items():
        noise = np.random.default_rng([zlib.crc32(name.encode()), seed]).standard_normal(out[name].shape)
        drawn = base * np.exp(spread * noise) if base else spread * noise
        out[name] = __import__('jax').numpy.asarray(drawn.astype(out[name].dtype))
    for name, factor in factors.items():
        out[name] = (out[name] * factor).astype(out[name].dtype)
    return out
```

```python
from contextlib import ExitStack

import numpy as np

import concourse.bass as bass
from concourse import mybir

F32 = mybir.dt.float32
I32 = mybir.dt.int32
U32 = mybir.dt.uint32
ALU = mybir.AluOpType
ACT = mybir.ActivationFunctionType
AX = mybir.AxisListType

P = 128
D = 1024
KD = D // P
SEQ = 1024
NB_DEC, T_DEC = 8, 8
NS = NB_DEC * T_DEC
N = SEQ + NS
QB = SEQ // P
NBLK = QB + 1
H = 4
DH = 64
W = 512
PAGE = 128
NPG = 2
PAST = NPG * PAGE
NPOOL = 20
L = 8
CH = SEQ // L
NC = CH + 1 + NB_DEC
G, GC, ST = 32, 16, 64
PR = G // 2
E, EG = 16, 4
FE = 512
KF = FE // P
NEG = -1.0e30
EPS = 1e-5
ALPHA = 2.0 ** 0.25
LAM_INIT = 0.8 - 0.6
SLOTB = 128
NSB = (2 * N) // SLOTB + E + 3
USED_PAIRS = (2 * N) // SLOTB // 2


WCOLS = KD * FE * 2 + KF * D
GATE_AT, UP_AT, DOWN_AT = 0, KD * FE, 2 * KD * FE


def rows(b):
    return P if b < QB else NS


def semaphores(nc, stage):
    taken = []
    stage.callback(nc.all_engine_barrier, sem_only=True)
    stage.callback(lambda: nc.clear_and_free_semaphores(taken))

    def sem(name):
        taken.append(nc.alloc_semaphore(name))
        return taken[-1]

    return sem


class Chain:

    def __init__(self, eng, sem):
        self.eng, self.sem, self.n = eng, sem, 0

    def __call__(self, ins):
        self.n += 1
        ins.then_inc(self.sem, 1)
        self.eng.wait_ge(self.sem, self.n)


def project(nc, io, s):
    spans = [(0, 512), (512, 512), (SEQ, NS)]
    tiles = ([("u", t) for t in range(L)] + [("us", 0)]
             + [("q", h, n) for h in range(H) for n in range(3)]
             + [("k", h, n) for h in range(H) for n in range(3)]
             + [("v", b) for b in range(NBLK)] + [("kn", b) for b in range(NBLK)])
    first_kn = len(tiles) - NBLK

    def tile_rows(i):
        kind = tiles[i]
        if kind[0] == "us":
            return NS
        return rows(kind[1]) if kind[0] in ("v", "kn") else P

    def tile_cols(i):
        return spans[tiles[i][2]][1] if tiles[i][0] in "qk" else W

    with ExitStack() as c:
        sb = lambda n, sh, dt=F32: c.enter_context(nc.sbuf_tensor(n, sh, dt))
        sem = semaphores(nc, c)
        xn = [sb(f"xn{i}", [P, D]) for i in range(3)]
        xT = sb("xT", [P, KD, N])
        wi = [sb(f"wi{i}", [P, KD, W]) for i in range(3)]
        kn = [sb(f"kn{i}", [P, W]) for i in range(2)]
        bank = [c.enter_context(nc.psum_tensor(f"pa{i}", [P, 512], F32)) for i in range(8)]
        x_in = [sem(f"x_in{i}") for i in range(3)]
        w_in = [sem(f"w_in{i}") for i in range(4)]
        xt_made, xt_kept = sem("xt_made"), sem("xt_kept")
        tile_made, v_kept, a_kept = sem("tile_made"), sem("v_kept"), sem("a_kept")
        out_sent, id_in = sem("out_sent"), sem("id_in")
        kn_sent = [sem(f"kn_sent{i}") for i in range(2)]

        def kept(i):
            return (v_kept, a_kept)[i % 2], i // 2 + 1

        def empty(eng, i, copy):
            kind, r = tiles[i], tile_rows(i)
            src = bank[i % 8][0:r, 0:tile_cols(i)]
            eng.wait_ge(tile_made, i + 1)
            if kind[0] == "u":
                dst = s.uc[:, :, kind[1], :]
                src = src.rearrange("p (g c) -> p g c", g=G)
            elif kind[0] == "us":
                dst = s.us[:, :]
            elif kind[0] == "q":
                a, n = spans[kind[2]]
                return copy(s.qT[:, kind[1], a:a + n], src, DH ** -0.5)
            elif kind[0] == "k":
                a, n = spans[kind[2]]
                dst = s.kT[:, kind[1], a:a + n]
            elif kind[0] == "v":
                dst = s.v[0:r, kind[1], :]
            else:
                if kind[1] >= 2:
                    eng.wait_ge(kn_sent[kind[1] % 2], 16 * (kind[1] // 2))
                dst = kn[kind[1] % 2][0:r, :]
            return copy(dst, src, 1.0)

        with nc.Block() as block:
            @block.sync
            def _(sp):
                sp.dma_start(s.ident[:, :], io["c_ident"]).then_inc(id_in, 16)
                for b in range(NBLK):
                    if b >= 3:
                        sp.wait_ge(xt_made, b - 2)
                    src = io["x_prompt"][0, b * P:(b + 1) * P, :] if b < QB else \
                        io["x_sample"].rearrange("b t d -> (b t) d")
                    sp.dma_start(xn[b % 3][0:rows(b), :], src).then_inc(x_in[b % 3], 16)
                wv = io["w_in"][0].rearrange("(p k) n -> p k n", k=KD)
                sp.wait_ge(tile_made, L + 1)
                sp.dma_start(wi[0][:, :, :], wv[:, :, 3 * W:4 * W]).then_inc(w_in[3], 16)
                vo = io["new_v_prompt"][0, 0].rearrange("t h d -> t (h d)")
                ko = io["new_k_prompt"][0, 0].rearrange("t h d -> t (h d)")
                vs = io["new_v_sample"][0].rearrange("b t h d -> (b t) (h d)")
                ks = io["new_k_sample"][0].rearrange("b t h d -> (b t) (h d)")
                for i, kind in enumerate(tiles):
                    if kind[0] in ("v", "kn"):
                        b, r = kind[1], tile_rows(i)
                        prompt, sample = (vo, vs) if kind[0] == "v" else (ko, ks)
                        dst = prompt[b * P:(b + 1) * P, :] if b < QB else sample
                        src = s.v[0:r, b, :] if kind[0] == "v" else kn[b % 2][0:r, :]
                        sp.wait_ge(*kept(i))
                        if kind[0] == "v":
                            sp.dma_start(dst, src).then_inc(out_sent, 16)
                        else:
                            sp.dma_start(dst, src).then_inc(kn_sent[b % 2], 16)
                sp.wait_ge(out_sent, 16 * NBLK)
                sp.wait_ge(kn_sent[0], 16 * (NBLK - NBLK // 2))
                sp.wait_ge(kn_sent[1], 16 * (NBLK // 2))

            @block.tensor
            def _(pe):
                pe.wait_ge(id_in, 16)
                for b in range(NBLK):
                    pe.wait_ge(x_in[b % 3], 16 * (b // 3 + 1))
                    if b >= 4:
                        pe.wait_ge(xt_kept, b - 3)
                    r = rows(b)
                    xv = xn[b % 3][0:r, :].rearrange("t (p k) -> t k p", k=KD)
                    for k in range(KD):
                        last = pe.transpose(bank[2 * (b % 4) + k // 4][:, (k % 4) * P:(k % 4) * P + r],
                                            xv[:, k, :], s.ident[0:r, 0:r])
                    last.then_inc(xt_made, 1)
                pe.wait_ge(xt_kept, NBLK)
                for i, kind in enumerate(tiles):
                    if i >= 8:
                        pe.wait_ge(*kept(i - 8))
                    out = bank[i % 8][0:tile_rows(i), 0:tile_cols(i)]
                    if kind[0] == "kn":
                        if kind[1] == 0:
                            last_k = max(j for j, t in enumerate(tiles) if t[0] == "k")
                            pe.wait_ge(*kept(last_k))
                            pe.wait_ge(*kept(last_k - 1))
                        a, r = kind[1] * P, tile_rows(i)
                        for h in range(H):
                            last = pe.transpose(bank[i % 8][0:r, h * P:(h + 1) * P],
                                                s.kT[:, h, a:a + r], s.ident[:, :])
                        last.then_inc(tile_made, 1)
                        continue
                    col = {"u": 0, "us": 0, "q": 1, "k": 2, "v": 3}[kind[0]]
                    pe.wait_ge(w_in[col], 16)
                    for k in range(KD):
                        if kind[0] == "u":
                            ops = xT[:, k, kind[1]:SEQ:L], wi[0][:, k, :]
                        elif kind[0] == "us":
                            ops = xT[:, k, SEQ:N], wi[0][:, k, :]
                        elif kind[0] == "v":
                            ops = xT[:, k, kind[1] * P:kind[1] * P + rows(kind[1])], wi[0][:, k, :]
                        else:
                            a, n = spans[kind[2]]
                            ops = wi[col][:, k, kind[1] * P:(kind[1] + 1) * P], xT[:, k, a:a + n]
                        last = pe.matmul(out, *ops, start=(k == 0), stop=(k == KD - 1))
                    last.then_inc(tile_made, 1)

            @block.vector
            def _(dve):
                for b in range(NBLK):
                    dve.wait_ge(xt_made, b + 1)
                    r = rows(b)
                    for half in range(2):
                        src = bank[2 * (b % 4) + half][:, :].rearrange("p (k t) -> p k t", k=4)[:, :, 0:r]
                        last = nc.vector.tensor_copy(xT[:, 4 * half:4 * half + 4, b * P:b * P + r], src)
                    last.then_inc(xt_kept, 1)
                for i in range(0, len(tiles), 2):
                    empty(dve, i, lambda o, a, m: nc.vector.tensor_scalar(o, a, m, None, ALU.mult)) \
                        .then_inc(v_kept, 1)

            @block.scalar
            def _(act):
                wv = io["w_in"][0].rearrange("(p k) n -> p k n", k=KD)
                for g in range(3):
                    act.dma_start(wi[g][:, :, :], wv[:, :, g * W:(g + 1) * W]).then_inc(w_in[g], 16)
                for i in range(1, len(tiles), 2):
                    empty(act, i, lambda o, a, m: nc.scalar.activation(o, a, ACT.Copy, scale=m)) \
                        .then_inc(a_kept, 1)


def attend(nc, io, s):
    steps = [(h, i) for h in range(H) for i in range(QB)]
    with ExitStack() as c:
        sb = lambda n, sh, dt=F32: c.enter_context(nc.sbuf_tensor(n, sh, dt))
        sem = semaphores(nc, c)
        bias = sb("bias", [P, H, SEQ])
        S = [[sb(f"S{k}{j}", [P, SEQ]) for j in range(2)] for k in range(2)]
        Ex = [[sb(f"Ex{k}{j}", [P, SEQ]) for j in range(2)] for k in range(2)]
        w = [sb(f"w{k}", [P, SEQ]) for k in range(2)]
        wT = [sb(f"wT{k}", [P, SEQ]) for k in range(2)]
        mx = sb("mx", [P, len(steps), 2])
        nm = sb("nm", [P, len(steps), 2])
        l = sb("l", [P, len(steps), 2])
        rl = sb("rl", [P, len(steps), 2])
        cf = sb("cf", [P, len(steps)])
        lmv = sb("lmv", [P, 4, DH])
        lmp = sb("lmp", [P, 2, DH])
        lms = sb("lms", [P, 2])
        lme = sb("lme", [P, 2])
        sq = sb("sq", [P, P])
        psS = [c.enter_context(nc.psum_tensor(f"psS{k}", [P, SEQ], F32)) for k in range(2)]
        psT = c.enter_context(nc.psum_tensor("psT", [P, SEQ], F32))
        psO = [c.enter_context(nc.psum_tensor(f"psO{k}", [P, 512], F32)) for k in range(2)]
        bias_in = [sem(f"bias_in{h}") for h in range(H)]
        lm_in, lm_sum, lm_exp, tab_in, k_in = sem("lm_in"), sem("lm_sum"), sem("lm_exp"), sem("tab_in"), sem("kc_in")
        scored, biased, negated, exped, lam_seq = sem("scored"), sem("biased"), sem("negated"), sem("exped"), sem("lam_seq")
        mixed, turned, turned_kept, summed, out_kept, squared, r_seq = (sem(n) for n in (
            "mixed", "turned", "turned_kept", "summed", "out_kept", "squared", "r_seq"))

        with nc.Block() as block:
            @block.sync
            def _(sp):
                sp.dma_start(s.ptab[:, :], io["page_table"].rearrange("(o b) n -> o (b n)", o=1)).then_inc(tab_in, 16)
                for n, name in enumerate(("lambda_q1", "lambda_k1", "lambda_q2", "lambda_k2")):
                    sp.dma_start(lmv[:, n, :], io[name].to_broadcast([P, DH])).then_inc(lm_in, 16)
                for h in range(H):
                    sp.dma_start(bias[:, h, :], io["c_bias"][:, h, :]).then_inc(bias_in[h], 16)
                sp.wait_ge(tab_in, 16)
                load_pages(sp, io, s, "cache_k", s.kc, k_in)
                sp.wait_ge(k_in, 16 * NB_DEC * NPG)

            def scores(pe, n):
                h, i = steps[n]
                nk = (i + 1) * P
                for j in range(2):
                    if n >= 1:
                        pe.wait_ge(biased, 2 * (n - 1) + j + 1)
                    for a in range(0, nk, 512):
                        m = min(512, nk - a)
                        last = pe.matmul(psS[j][:, a:a + m], s.qT[DH * j:DH * j + DH, h, i * P:(i + 1) * P],
                                         s.kT[DH * j:DH * j + DH, h, a:a + m], start=True, stop=True)
                    last.then_inc(scored, 1)

            def turn(pe, n):
                h, i = steps[n]
                pe.wait_ge(mixed, n + 1)
                if n >= 1:
                    pe.wait_ge(turned_kept, n)
                for j in range(i + 1):
                    last = pe.transpose(psT[:, j * P:(j + 1) * P], w[n % 2][:, j * P:(j + 1) * P], s.ident[:, :])
                last.then_inc(turned, 1)

            def values(pe, n):
                h, i = steps[n]
                pe.wait_ge(turned_kept, n + 1)
                if n >= 2:
                    pe.wait_ge(out_kept, n - 1)
                for j in range(i + 1):
                    last = pe.matmul(psO[n % 2][:, 0:P], wT[n % 2][:, j * P:(j + 1) * P],
                                     s.v[:, j, h * P:(h + 1) * P], start=(j == 0), stop=(j == i))
                last.then_inc(summed, 1)

            @block.tensor
            def _(pe):
                scores(pe, 0)
                scores(pe, 1)
                for n in range(len(steps)):
                    if n + 2 < len(steps):
                        scores(pe, n + 2)
                    turn(pe, n)
                    if n >= 1:
                        values(pe, n - 1)
                values(pe, len(steps) - 1)

            @block.vector
            def _(dve):
                dve.wait_ge(lm_in, 64)
                for j in range(2):
                    last = nc.vector.tensor_tensor(lmp[:, j, :], lmv[:, 2 * j, :], lmv[:, 2 * j + 1, :], ALU.mult)
                last.then_inc(lam_seq, 1)
                dve.wait_ge(lam_seq, 1)
                nc.vector.tensor_reduce(lms[:, :], lmp[:, :, :], AX.X, ALU.add).then_inc(lm_sum, 1)
                dve.wait_ge(lm_exp, 1)
                nc.vector.tensor_tensor(s.nlam[:, :], lme[:, 1:2], lme[:, 0:1], ALU.subtract).then_inc(lam_seq, 1)
                dve.wait_ge(lam_seq, 2)
                nc.vector.tensor_scalar(s.nlam[:, :], s.nlam[:, :], LAM_INIT, None, ALU.subtract).then_inc(lam_seq, 1)
                dve.wait_ge(lam_seq, 3)
                def add_bias(n):
                    h, i = steps[n]
                    nk = (i + 1) * P
                    if i == 0:
                        dve.wait_ge(bias_in[h], 16)
                    for j in range(2):
                        dve.wait_ge(scored, 2 * n + j + 1)
                        if n >= 2:
                            dve.wait_ge(exped, 2 * (n - 2) + j + 1)
                        nc.vector.tensor_tensor_reduce(
                            S[n % 2][j][:, 0:nk], psS[j][:, 0:nk], bias[:, h, (QB - 1 - i) * P:], 1.0, NEG,
                            ALU.add, ALU.max, mx[:, n, j:j + 1]).then_inc(biased, 1)
                    dve.wait_ge(biased, 2 * n + 2)
                    nc.vector.tensor_scalar(nm[:, n, :], mx[:, n, :], -1.0, None, ALU.mult).then_inc(negated, 1)

                def mix(n):
                    h, i = steps[n]
                    nk = (i + 1) * P
                    dve.wait_ge(exped, 2 * n + 2)
                    nc.vector.reciprocal(rl[:, n, :], l[:, n, :]).then_inc(r_seq, 1)
                    dve.wait_ge(r_seq, 2 * n + 1)
                    nc.vector.scalar_tensor_tensor(cf[:, n:n + 1], rl[:, n, 1:2], s.nlam[:, 0:1], l[:, n, 0:1],
                                                   ALU.mult, ALU.mult).then_inc(r_seq, 1)
                    dve.wait_ge(r_seq, 2 * n + 2)
                    if n >= 2:
                        dve.wait_ge(turned, n - 1)
                    nc.vector.scalar_tensor_tensor(w[n % 2][:, 0:nk], Ex[n % 2][1][:, 0:nk], cf[:, n:n + 1],
                                                   Ex[n % 2][0][:, 0:nk], ALU.mult, ALU.add).then_inc(mixed, 1)

                def keep_out(n):
                    h, i = steps[n]
                    dve.wait_ge(summed, n + 1)
                    nc.vector.tensor_scalar(s.o[:, i, h * P:(h + 1) * P], psO[n % 2][:, 0:P], rl[:, n, 0:1], None,
                                            ALU.mult).then_inc(out_kept, 1)

                add_bias(0)
                add_bias(1)
                for n in range(len(steps)):
                    mix(n)
                    if n + 2 < len(steps):
                        add_bias(n + 2)
                    if n >= 2:
                        keep_out(n - 2)
                keep_out(len(steps) - 2)
                keep_out(len(steps) - 1)

            def square(act, n):
                h, i = steps[n]
                act.wait_ge(out_kept, n + 1)
                if n >= 1:
                    act.wait_ge(squared, n)
                nc.scalar.activation(sq[:, :], s.o[:, i, h * P:(h + 1) * P], ACT.Square,
                                     accum_out=s.ss[:, i, h:h + 1]).then_inc(squared, 1)

            @block.scalar
            def _(act):
                act.wait_ge(lm_sum, 1)
                nc.scalar.activation(lme[:, :], lms[:, :], ACT.Exp).then_inc(lm_exp, 1)

                def exps(n):
                    h, i = steps[n]
                    nk = (i + 1) * P
                    act.wait_ge(negated, n + 1)
                    if n >= 2:
                        act.wait_ge(mixed, n - 1)
                    for j in range(2):
                        nc.scalar.activation(Ex[n % 2][j][:, 0:nk], S[n % 2][j][:, 0:nk], ACT.Exp,
                                             bias=nm[:, n, j:j + 1], accum_out=l[:, n, j:j + 1]).then_inc(exped, 1)

                def keep_turned(n):
                    h, i = steps[n]
                    act.wait_ge(turned, n + 1)
                    if n >= 2:
                        act.wait_ge(summed, n - 1)
                    nc.scalar.activation(wT[n % 2][:, 0:(i + 1) * P], psT[:, 0:(i + 1) * P], ACT.Copy) \
                        .then_inc(turned_kept, 1)

                exps(0)
                exps(1)
                for n in range(len(steps)):
                    keep_turned(n)
                    if n + 2 < len(steps):
                        exps(n + 2)
                    if n >= 2:
                        square(act, n - 2)
                square(act, len(steps) - 2)
                square(act, len(steps) - 1)


def load_pages(sp, io, s, cache, dst, done):
    for n in range(NB_DEC * NPG):
        page = sp.value_load(s.ptab[0:1, n:n + 1], min_val=0, max_val=NPOOL - 1)
        src = io[cache][0].rearrange("n p h d -> n p (h d)")[bass.ds(page, 1), :, :]
        sp.dma_start(dst[:, n, :], src.rearrange("o p c -> p (o c)")).then_inc(done, 16)


def sample(nc, io, s):
    KC = PAST + NS
    with ExitStack() as c:
        sb = lambda n, sh, dt=F32: c.enter_context(nc.sbuf_tensor(n, sh, dt))
        sem = semaphores(nc, c)
        kc = s.kc
        vc = sb("vc", [P, NB_DEC * NPG, W])
        kcT = sb("kcT", [P, NB_DEC * NPG * P])
        bs = sb("bs", [P, H, KC])
        two = sb("two", [P, NS])
        sel = sb("sel", [P, 2])
        sg = sb("sg", [P, 1])
        qf = sb("qf", [P, H, P])
        qm = sb("qm", [P, H, NB_DEC, P])
        S = sb("sS", [P, KC])
        Ex = sb("sE", [P, KC])
        PT = [sb(f"sPT{k}", [P, 3 * NS]) for k in range(2)]
        oT = [sb(f"soT{k}", [P, NS]) for k in range(2)]
        st = sb("sst", [P, H, 4])
        sq = sb("ssq", [NS, P])
        psK = [c.enter_context(nc.psum_tensor(f"psK{k}", [P, 512], F32)) for k in range(4)]
        psS = c.enter_context(nc.psum_tensor("spS", [P, 512], F32))
        psP = c.enter_context(nc.psum_tensor("spP", [P, 512], F32))
        psO = c.enter_context(nc.psum_tensor("spO", [P, 512], F32))
        psN = c.enter_context(nc.psum_tensor("spN", [P, 512], F32))
        names = ("consts_in v_in zeroed q_ready sg_ready k_turned k_kept scored biased negated exped "
                 "scaled recip pairs pairs_kept summed o_kept o_turned o_out squared").split()
        m = {n: sem("s_" + n) for n in names}

        with nc.Block() as block:
            @block.sync
            def _(sp):
                sp.dma_start(two[:, :], io["c_two"]).then_inc(m["consts_in"], 16)
                sp.dma_start(sel[:, :], io["c_sel"]).then_inc(m["consts_in"], 16)
                sp.dma_start(bs[:, :, :], io["c_bias_s"]).then_inc(m["consts_in"], 16)
                load_pages(sp, io, s, "cache_v", vc, m["v_in"])

            @block.gpsimd
            def _(pool):
                nc.gpsimd.memset(qf[:, :, :], 0.0).then_inc(m["zeroed"], 1)
                nc.gpsimd.memset(qm[:, :, :, :], 0.0).then_inc(m["zeroed"], 1)

            @block.tensor
            def _(pe):
                def keys(h):
                    for g in range(4):
                        if h >= 1:
                            pe.wait_ge(m["k_kept"], 4 * (h - 1) + g + 1)
                        for j in range(4):
                            n = 4 * g + j
                            last = pe.transpose(psK[g][:, j * P:(j + 1) * P], kc[:, n, h * P:(h + 1) * P], s.ident[:, :])
                        last.then_inc(m["k_turned"], 1)

                def scores(h):
                    pe.wait_ge(m["k_kept"], 4 * (h + 1))
                    if h == 0:
                        pe.wait_ge(m["q_ready"], 2 * H + 4 * H)
                    else:
                        pe.wait_ge(m["biased"], h)
                    for b in range(NB_DEC):
                        pe.matmul(psS[:, 0:PAST], qm[:, h, b, :], kcT[:, b * PAST:(b + 1) * PAST],
                                  start=(b == 0), stop=(b == NB_DEC - 1))
                    pe.matmul(psS[:, PAST:KC], qf[:, h, :], s.kT[:, h, SEQ:N], start=True, stop=True) \
                        .then_inc(m["scored"], 1)

                keys(0)
                for h in range(H):
                    scores(h)
                    if h + 1 < H:
                        keys(h + 1)
                    pe.wait_ge(m["scaled"], h + 1)
                    if h == 0:
                        pe.wait_ge(m["consts_in"], 48)
                    else:
                        pe.wait_ge(m["pairs_kept"], h)
                    for j in range(3):
                        n = P if j < 2 else NS
                        last = pe.matmul(psP[0:n, j * NS:(j + 1) * NS], Ex[:, j * P:j * P + n], two[:, :],
                                         start=True, stop=True)
                    last.then_inc(m["pairs"], 1)
                    pe.wait_ge(m["pairs_kept"], h + 1)
                    if h == 0:
                        pe.wait_ge(m["v_in"], 16 * NB_DEC * NPG)
                    else:
                        pe.wait_ge(m["o_kept"], h)
                    pe.matmul(psO[:, 0:NS], s.v[0:NS, QB, h * P:(h + 1) * P], PT[h % 2][0:NS, 2 * NS:3 * NS],
                              start=True, stop=False, skip_group_check=True)
                    for b in range(NB_DEC):
                        for j in range(NPG):
                            last = pe.matmul(psO[:, b * T_DEC:(b + 1) * T_DEC], vc[:, NPG * b + j, h * P:(h + 1) * P],
                                             PT[h % 2][:, j * NS + b * T_DEC:j * NS + (b + 1) * T_DEC],
                                             start=False, stop=(b == NB_DEC - 1 and j == NPG - 1), skip_group_check=True)
                    last.then_inc(m["summed"], 1)
                    pe.wait_ge(m["o_kept"], h + 1)
                    if h >= 1:
                        pe.wait_ge(m["o_out"], h)
                    pe.transpose(psN[0:NS, 0:P], oT[h % 2][:, :], s.ident[:, :]).then_inc(m["o_turned"], 1)

            @block.vector
            def _(dve):
                dve.wait_ge(m["zeroed"], 2)
                for h in range(H):
                    for j in range(2):
                        r = slice(DH * j, DH * j + DH)
                        nc.vector.tensor_copy(qf[r, h, NS * j:NS * j + NS], s.qT[r, h, SEQ:N]).then_inc(m["q_ready"], 1)
                dve.wait_ge(m["consts_in"], 48)
                nc.vector.scalar_tensor_tensor(sg[:, :], sel[:, 1:2], s.nlam[:, 0:1], sel[:, 0:1],
                                               ALU.mult, ALU.add).then_inc(m["sg_ready"], 1)
                for h in range(H):
                    dve.wait_ge(m["scored"], h + 1)
                    if h >= 1:
                        dve.wait_ge(m["exped"], h)
                    nc.vector.tensor_tensor_reduce(S[:, :], psS[:, 0:KC], bs[:, h, :], 1.0, NEG, ALU.add,
                                                   ALU.max, st[:, h, 0:1]).then_inc(m["biased"], 1)
                    dve.wait_ge(m["biased"], h + 1)
                    nc.vector.tensor_scalar(st[:, h, 1:2], st[:, h, 0:1], -1.0, None, ALU.mult).then_inc(m["negated"], 1)
                    dve.wait_ge(m["exped"], h + 1)
                    nc.vector.reciprocal(st[:, h, 3:4], st[:, h, 2:3]).then_inc(m["recip"], 1)
                    dve.wait_ge(m["recip"], h + 1)
                    dve.wait_ge(m["sg_ready"], 1)
                    nc.vector.tensor_scalar(Ex[:, :], Ex[:, :], st[:, h, 3:4], sg[:, 0:1], ALU.mult,
                                            ALU.mult).then_inc(m["scaled"], 1)
                    dve.wait_ge(m["pairs"], h + 1)
                    if h >= 2:
                        dve.wait_ge(m["summed"], h - 1)
                    nc.vector.tensor_copy(PT[h % 2][:, 0:2 * NS], psP[:, 0:2 * NS])
                    nc.vector.tensor_copy(PT[h % 2][0:NS, 2 * NS:3 * NS], psP[0:NS, 2 * NS:3 * NS]) \
                        .then_inc(m["pairs_kept"], 1)
                    dve.wait_ge(m["summed"], h + 1)
                    if h >= 2:
                        dve.wait_ge(m["o_turned"], h - 1)
                    nc.vector.tensor_copy(oT[h % 2][:, :], psO[:, 0:NS]).then_inc(m["o_kept"], 1)
                    dve.wait_ge(m["o_turned"], h + 1)
                    nc.vector.tensor_copy(s.o[0:NS, QB, h * P:(h + 1) * P], psN[0:NS, 0:P]).then_inc(m["o_out"], 1)

            @block.scalar
            def _(act):
                act.wait_ge(m["zeroed"], 2)
                for h in range(H):
                    for j in range(2):
                        r = slice(DH * j, DH * j + DH)
                        for bh in range(2):
                            at = NS * j + T_DEC * 4 * bh
                            dst = bass_diag(qm, r, h, 4 * bh, at)
                            nc.scalar.activation(dst, s.qT[r, h, SEQ + 32 * bh:SEQ + 32 * bh + 32]
                                                 .rearrange("p (b t) -> p b t", t=T_DEC), ACT.Copy).then_inc(m["q_ready"], 1)
                def keep_keys(h):
                    for g in range(4):
                        act.wait_ge(m["k_turned"], 4 * h + g + 1)
                        if h >= 1:
                            act.wait_ge(m["scored"], h)
                        nc.scalar.activation(kcT[:, g * 512:(g + 1) * 512], psK[g][:, :], ACT.Copy) \
                            .then_inc(m["k_kept"], 1)

                keep_keys(0)
                for h in range(H):
                    if h + 1 < H:
                        keep_keys(h + 1)
                    act.wait_ge(m["negated"], h + 1)
                    if h >= 1:
                        act.wait_ge(m["pairs"], h)
                    nc.scalar.activation(Ex[:, :], S[:, :], ACT.Exp, bias=st[:, h, 1:2],
                                         accum_out=st[:, h, 2:3]).then_inc(m["exped"], 1)
                for h in range(H):
                    act.wait_ge(m["o_out"], h + 1)
                    if h >= 1:
                        act.wait_ge(m["squared"], h)
                    nc.scalar.activation(sq[:, :], s.o[0:NS, QB, h * P:(h + 1) * P], ACT.Square,
                                         accum_out=s.ss[0:NS, QB, h:h + 1]).then_inc(m["squared"], 1)


def bass_diag(qm, r, h, b0, at):
    flat = qm[r, h, :, :].rearrange("p b c -> p (b c)")
    lo = b0 * P + at
    need = 4 * (P + T_DEC)
    if lo + need <= NB_DEC * P:
        return flat[:, lo:lo + need].rearrange("p (b c) -> p b c", c=P + T_DEC)[:, :, 0:T_DEC]
    hi = NB_DEC * P - need
    return flat[:, hi:].rearrange("p (b c) -> p b c", c=P + T_DEC)[:, :, lo - hi:lo - hi + T_DEC]


def head_norm(nc, io, s):
    with ExitStack() as c:
        sb = lambda n, sh, dt=F32: c.enter_context(nc.sbuf_tensor(n, sh, dt))
        sem = semaphores(nc, c)
        rs = sb("rs", [P, NBLK * H])
        gcol = sb("gcol", [P, 1])
        an = [sb(f"an{k}", [P, W]) for k in range(2)]
        ps = [c.enter_context(nc.psum_tensor(f"psA{k}", [P, 512], F32)) for k in range(2)]
        g_in, seq, rooted, scaled, turned, kept = (sem(n) for n in "hn_g hn_seq hn_root hn_scaled hn_turned hn_kept".split())

        with nc.Block() as block:
            @block.sync
            def _(sp):
                sp.dma_start(gcol[:, :], io["subln_g"].rearrange("o v -> v o")).then_inc(g_in, 16)

            @block.vector
            def _(dve):
                ch = Chain(dve, seq)
                ssv = s.ss[:, :, :].rearrange("p b h -> p (b h)")
                ch(nc.vector.memset(s.ss[NS:P, QB, :], 1.0))
                ch(nc.vector.tensor_scalar(rs[:, :], ssv, 1.0 / P, EPS, ALU.mult, ALU.add))
                dve.wait_ge(g_in, 16)
                ch(nc.vector.tensor_scalar(gcol[:, :], gcol[:, :], 1.0 - LAM_INIT, None, ALU.mult))
                dve.wait_ge(rooted, 1)
                ch(nc.vector.reciprocal(rs[:, :], rs[:, :]))
                for b in range(NBLK):
                    r = rows(b)
                    if b >= 2:
                        dve.wait_ge(turned, b - 1)
                    for h in range(H):
                        last = nc.vector.tensor_scalar(an[b % 2][0:r, h * P:(h + 1) * P], s.o[0:r, b, h * P:(h + 1) * P],
                                                       rs[0:r, b * H + h:b * H + h + 1], None, ALU.mult)
                    last.then_inc(scaled, 1)

            @block.tensor
            def _(pe):
                for b in range(NBLK):
                    r = rows(b)
                    pe.wait_ge(scaled, b + 1)
                    if b >= 2:
                        pe.wait_ge(kept, b - 1)
                    for h in range(H):
                        last = pe.transpose(ps[b % 2][:, h * P:h * P + r], an[b % 2][0:r, h * P:(h + 1) * P],
                                            s.ident[0:r, 0:r])
                    last.then_inc(turned, 1)

            @block.scalar
            def _(act):
                act.wait_ge(seq, 3)
                nc.scalar.activation(rs[:, :], rs[:, :], ACT.Sqrt).then_inc(rooted, 1)
                for b in range(NBLK):
                    r = rows(b)
                    act.wait_ge(turned, b + 1)
                    nc.scalar.activation(s.aT[:, :, b * P:b * P + r],
                                         ps[b % 2][:, :].rearrange("p (h t) -> p h t", h=H)[:, :, 0:r],
                                         ACT.Copy, scale=gcol[:, 0:1]).then_inc(kept, 1)


MAGIC = 1.5 * 2.0 ** 23
TWO_PI = 6.283185307179586
PI_HI, PI_MID = 6.28125, 0.0019350051879882812
PI_LO = TWO_PI - PI_HI - PI_MID


def wide(ap, n):
    return ap.unsqueeze(2).to_broadcast([ap.shape[0], ap.shape[1], n])


def mid(ap, n):
    return ap.unsqueeze(1).to_broadcast([ap.shape[0], n, ap.shape[1]])


def ssm_tables(nc, io, s):
    with ExitStack() as c:
        sb = lambda n, sh, dt=F32: c.enter_context(nc.sbuf_tensor(n, sh, dt))
        sem = semaphores(nc, c)
        par = sb("par", [P, 3, PR])
        th = sb("th", [P, 2, PR])
        kk = sb("kk", [P, 2, PR])
        rr = sb("rr", [P, 2, PR])
        ra = sb("ra", [P, 2, PR])
        cs = sb("cs", [P, 2, 2, PR])
        mg = sb("mg", [P, 2, PR])
        dt_ = sb("dt_", [P, PR])
        ld = sb("ld", [P, PR])
        ar, ai, nr, den, t1, t2, cr, ci = (sb("z" + n, [P, PR]) for n in "ar ai nr den t1 t2 cr ci".split())
        half_pi = sb("half_pi", [P, 1])
        bre, bim, cre, cim = (sb("b_" + n, [P, PR, GC]) for n in "bre bim cre cim".split())
        u1, u2, u3, u4 = (sb(f"u{n}", [P, PR, GC]) for n in range(4))
        g1, g2, g3, g4 = (sb(f"g{n}", [P, PR, GC]) for n in range(4))
        cbr = sb("cbr", [P, PR, 2 * GC])
        cbi = sb("cbi", [P, PR, 2 * GC])
        pr, pi = (s.work[n][:, :, :].rearrange("p q (b c) -> p q b c", c=GC) for n in (2, 3))
        kd = sb("kd", [P, W])
        kcol = sb("kcol", [P, W])
        bk = [c.enter_context(nc.psum_tensor(f"pt{k}", [P, 512], F32)) for k in range(8)]
        (p_in, e_in, c_in, seq, dts, angles, exps, absd, sines, zeroed, b_ready, cseq, neg_c, t_made, t_kept,
         v_made, v_kept, cb_in, a_ready, us_in, pad_zeroed, u_made, u_kept, kd_in, k_made, k_kept, t_zeroed) = (
            sem("st_" + n) for n in (
            "p e c seq dts angles exps absd sines zeroed b_ready cseq neg_c t_made t_kept v_made v_kept cb_in a_ready "
            "us pad u_made u_kept kd k_made k_kept t_zeroed").split())

        with nc.Block() as block:
            @block.sync
            def _(sp):
                sp.dma_start(par[:, :, :], io["l_par"]).then_inc(p_in, 16)
                for t in range(T_DEC):
                    sp.dma_start(s.us8[:, :, t, :], s.us[t:NS:T_DEC, :].rearrange("b (g c) -> b g c", g=G)) \
                        .then_inc(us_in, 16)
                sp.dma_start(bre[:, :, :], io["l_bre"]).then_inc(e_in, 16)
                sp.dma_start(bim[:, :, :], io["l_bim"]).then_inc(e_in, 16)
                sp.dma_start(cre[:, :, :], io["l_cre"]).then_inc(c_in, 16)
                sp.dma_start(cim[:, :, :], io["l_cim"]).then_inc(c_in, 16)
                sp.dma_start(cbr[:, :, :], io["l_cbr"]).then_inc(cb_in, 16)
                sp.dma_start(cbi[:, :, :], io["l_cbi"]).then_inc(cb_in, 16)
                sp.dma_start(kd[:, :], io["l_d"]).then_inc(kd_in, 16)

            @block.scalar
            def _(act):
                act.wait_ge(p_in, 16)
                nc.scalar.activation(dt_[:, :], par[:, 2, :], ACT.Exp).then_inc(dts, 1)
                act.wait_ge(angles, 1)
                nc.scalar.activation(mg[:, 0, :], ld[:, :], ACT.Exp).then_inc(exps, 1)
                nc.scalar.activation(mg[:, 1, :], ld[:, :], ACT.Exp, scale=float(L)).then_inc(exps, 1)
                act.wait_ge(absd, 1)
                nc.scalar.activation(cs[:, 1, :, :], rr[:, :, :], ACT.Sin).then_inc(sines, 1)
                nc.scalar.activation(cs[:, 0, :, :], ra[:, :, :], ACT.Sin, scale=-1.0, bias=half_pi[:, 0:1]) \
                    .then_inc(sines, 1)
                for g in range(0, G, 4):
                    act.wait_ge(u_made, g // 4 + 1)
                    nc.scalar.activation(s.U[:, g:g + 4, 0:CH], bk[(g // 4) % 4][:, :].rearrange("p (g n) -> p g n", g=4),
                                         ACT.Copy).then_inc(u_kept, 1)
                act.wait_ge(u_made, G // 4 + 1)
                nc.scalar.activation(s.U[:, :, CH + 1:], bk[4][:, 0:G * NB_DEC].rearrange("p (g n) -> p g n", g=G),
                                     ACT.Copy).then_inc(u_kept, 1)
                act.wait_ge(t_zeroed, 1)
                for t in range(L):
                    n = (t + 1) * GC
                    act.wait_ge(t_made, t + 1)
                    nc.scalar.activation(s.T[0:n, :, t * GC:n], bk[t % 4][0:n, :].rearrange("p (g c) -> p g c", g=G),
                                         ACT.Copy).then_inc(t_kept, 1)

            @block.gpsimd
            def _(pool):
                nc.gpsimd.memset(half_pi[:, :], TWO_PI / 4).then_inc(zeroed, 1)
                nc.gpsimd.memset(s.U[:, :, CH:CH + 1], 0.0).then_inc(pad_zeroed, 1)
                ch = Chain(pool, cseq)
                tt = nc.gpsimd.tensor_tensor
                pool.wait_ge(cb_in, 32)
                ch(nc.gpsimd.tensor_scalar(cbi[:, :, :], cbi[:, :, :], -1.0, None, ALU.mult))
                pool.wait_ge(c_in, 32)
                ch(nc.gpsimd.tensor_scalar(cim[:, :, :], cim[:, :, :], -1.0, None, ALU.mult))
                pool.wait_ge(a_ready, 1)
                for t in range(L):
                    re0 = cre[:, :, :] if t == 0 else s.CAr[:, :, t - 1, :]
                    im0 = cim[:, :, :] if t == 0 else s.CAi[:, :, t - 1, :]
                    tt(g1[:, :, :], re0, wide(ar[:, :], GC), ALU.mult)
                    tt(g2[:, :, :], im0, wide(ai[:, :], GC), ALU.mult)
                    tt(g3[:, :, :], im0, wide(ar[:, :], GC), ALU.mult)
                    ch(tt(g4[:, :, :], re0, wide(ai[:, :], GC), ALU.mult))
                    tt(s.CAr[:, :, t, :], g1[:, :, :], g2[:, :, :], ALU.add)
                    ch(tt(s.CAi[:, :, t, :], g3[:, :, :], g4[:, :, :], ALU.subtract))
                    if t == 0:
                        nc.gpsimd.memset(s.T[:, :, :], 0.0).then_inc(t_zeroed, 1)

            @block.vector
            def _(dve):
                ch = Chain(dve, seq)
                ts, tt = nc.vector.tensor_scalar, nc.vector.tensor_tensor
                dve.wait_ge(dts, 1)
                lr, li = par[:, 0, :], par[:, 1, :]
                tt(ld[:, :], lr, dt_[:, :], ALU.mult).then_inc(angles, 1)
                ch(tt(th[:, 0, :], li, dt_[:, :], ALU.mult))
                ch(ts(th[:, 1, :], th[:, 0, :], float(L), None, ALU.mult))
                ch(ts(kk[:, :, :], th[:, :, :], 1.0 / TWO_PI, None, ALU.mult))
                ch(ts(kk[:, :, :], kk[:, :, :], MAGIC, None, ALU.add))
                ch(ts(kk[:, :, :], kk[:, :, :], MAGIC, None, ALU.subtract))
                stt = nc.vector.scalar_tensor_tensor
                ch(stt(rr[:, :, :], kk[:, :, :], -PI_HI, th[:, :, :], ALU.mult, ALU.add))
                ch(stt(rr[:, :, :], kk[:, :, :], -PI_MID, rr[:, :, :], ALU.mult, ALU.add))
                ch(stt(rr[:, :, :], kk[:, :, :], -PI_LO, rr[:, :, :], ALU.mult, ALU.add))
                ch(ts(rr[:, :, :], rr[:, :, :], 3.1415925, -3.1415925, ALU.min, ALU.max))
                ch(ts(ra[:, :, :], rr[:, :, :], -1.0, None, ALU.mult))
                dve.wait_ge(zeroed, 1)
                ch(tt(ra[:, :, :], rr[:, :, :], ra[:, :, :], ALU.max))
                dve.sem_inc(absd, 1)
                dve.wait_ge(exps, 2)
                dve.wait_ge(sines, 2)
                tt(ar[:, :], mg[:, 0, :], cs[:, 0, 0, :], ALU.mult)
                ch(tt(ai[:, :], mg[:, 0, :], cs[:, 1, 0, :], ALU.mult))
                dve.sem_inc(a_ready, 1)
                tt(s.a8[:, 0, :], mg[:, 1, :], cs[:, 0, 1, :], ALU.mult)
                tt(s.a8[:, 1, :], mg[:, 1, :], cs[:, 1, 1, :], ALU.mult)
                ch(ts(nr[:, :], ar[:, :], 1.0, None, ALU.subtract))
                tt(t1[:, :], lr, lr, ALU.mult)
                ch(tt(t2[:, :], li, li, ALU.mult))
                ch(tt(den[:, :], t1[:, :], t2[:, :], ALU.add))
                ch(nc.vector.reciprocal(den[:, :], den[:, :]))
                tt(t1[:, :], nr[:, :], lr, ALU.mult)
                ch(tt(t2[:, :], ai[:, :], li, ALU.mult))
                ch(tt(cr[:, :], t1[:, :], t2[:, :], ALU.add))
                tt(t1[:, :], ai[:, :], lr, ALU.mult)
                ch(tt(t2[:, :], nr[:, :], li, ALU.mult))
                ch(tt(ci[:, :], t1[:, :], t2[:, :], ALU.subtract))
                tt(cr[:, :], cr[:, :], den[:, :], ALU.mult)
                ch(tt(ci[:, :], ci[:, :], den[:, :], ALU.mult))
                dve.wait_ge(e_in, 32)

                def cmul(re_out, im_out, re, im, xr, xi, n):
                    tt(u1[:, :, :], re, wide(xr, n), ALU.mult)
                    tt(u2[:, :, :], im, wide(xi, n), ALU.mult)
                    tt(u3[:, :, :], im, wide(xr, n), ALU.mult)
                    ch(tt(u4[:, :, :], re, wide(xi, n), ALU.mult))
                    tt(re_out, u1[:, :, :], u2[:, :, :], ALU.subtract)
                    ch(tt(im_out, u3[:, :, :], u4[:, :, :], ALU.add))

                cmul(pr[:, :, L - 1, :], pi[:, :, L - 1, :], bre[:, :, :], bim[:, :, :], cr[:, :], ci[:, :], GC)
                for b in range(L - 2, -1, -1):
                    cmul(pr[:, :, b, :], pi[:, :, b, :], pr[:, :, b + 1, :], pi[:, :, b + 1, :], ar[:, :], ai[:, :], GC)
                dve.sem_inc(b_ready, 1)
                dve.wait_ge(kd_in, 16)
                dve.wait_ge(k_made, 1)
                nc.vector.tensor_tensor(kcol[:, :], bk[5][:, :], kd[:, :], ALU.add).then_inc(k_kept, 1)
                for q in range(0, PR, 2):
                    dve.wait_ge(v_made, q // 2 + 1)
                    src = bk[6 + (q // 2) % 2][:, :].rearrange("p (j k n) -> p j k n", j=2, k=2)
                    nc.vector.tensor_copy(s.VTr[:, q:q + 2, :], src[:, :, 0, :])
                    nc.vector.tensor_copy(s.VTi[:, q:q + 2, :], src[:, :, 1, :]).then_inc(v_kept, 1)
                nc.vector.memset(s.Er[:, :, 0:1], 1.0)
                nc.vector.memset(s.Ei[:, :, 0:1], 0.0)
                nc.vector.tensor_copy(s.Er[:, :, 1:2], cs[:, 0, 1, :].unsqueeze(2))
                ch(nc.vector.tensor_copy(s.Ei[:, :, 1:2], cs[:, 1, 1, :].unsqueeze(2)))
                w1, w2, w3, w4 = (s.work[n // 2][:, :, CH // 2 * (n % 2):] for n in range(4))
                m = 1
                while m < CH:
                    n = min(m, CH - 1 - m)
                    if n <= 0:
                        break
                    for dst, a, b in ((w1, s.Er, s.Er), (w2, s.Ei, s.Ei), (w3, s.Er, s.Ei), (w4, s.Ei, s.Er)):
                        last = tt(dst[:, :, 0:n], a[:, :, 1:n + 1], wide(b[:, :, m], n), ALU.mult)
                    ch(last)
                    tt(s.Er[:, :, m + 1:m + 1 + n], w1[:, :, 0:n], w2[:, :, 0:n], ALU.subtract)
                    ch(tt(s.Ei[:, :, m + 1:m + 1 + n], w3[:, :, 0:n], w4[:, :, 0:n], ALU.add))
                    m *= 2
                nc.vector.tensor_copy(s.m8[:, :], mg[:, 1, :])

            @block.tensor
            def _(pe):
                for g in range(G):
                    k = (g // 4) % 4
                    if g % 4 == 0 and g >= 16:
                        pe.wait_ge(u_kept, g // 4 - 3)
                    src = s.uc[:, g, :, :].rearrange("p t c -> p (t c)")
                    last = pe.transpose(bk[k][:, (g % 4) * P:(g % 4 + 1) * P], src, s.ident[:, :])
                    if g % 4 == 3:
                        last.then_inc(u_made, 1)
                pe.wait_ge(us_in, 16 * T_DEC)
                for g in range(G):
                    last = pe.transpose(bk[4][:, g * NB_DEC:(g + 1) * NB_DEC],
                                        s.us8[:, g, :, :].rearrange("p t c -> p (t c)"), s.ident[0:NB_DEC, 0:NB_DEC])
                last.then_inc(u_made, 1)
                pe.wait_ge(b_ready, 1)
                pe.wait_ge(cseq, 1)
                flat = lambda t, q: t[:, q, :, :].rearrange("p b c -> p (b c)")
                for q in range(PR):
                    out = bk[5][:, q * 2 * GC:(q + 1) * 2 * GC]
                    pe.matmul(out, flat(pr, q), cbr[:, q, :], start=True, stop=False)
                    last = pe.matmul(out, flat(pi, q), cbi[:, q, :], start=False, stop=True)
                last.then_inc(k_made, 1)
                for q in range(PR):
                    if q % 2 == 0 and q >= 4:
                        pe.wait_ge(v_kept, (q - 4) // 2 + 1)
                    at = 256 * (q % 2)
                    pe.transpose(bk[6 + (q // 2) % 2][:, at:at + P], flat(pr, q), s.ident[:, :])
                    last = pe.transpose(bk[6 + (q // 2) % 2][:, at + P:at + 2 * P], flat(pi, q), s.ident[:, :])
                    if q % 2:
                        last.then_inc(v_made, 1)
                pe.wait_ge(u_kept, G // 4 + 1)
                pe.wait_ge(k_kept, 1)
                for t in range(L):
                    if t >= 4:
                        pe.wait_ge(t_kept, t - 3)
                    n = (t + 1) * GC
                    pe.matmul(bk[t % 4][0:n, :], s.ident[:, P - n:P], kcol[:, :], start=True, stop=True).then_inc(t_made, 1)


def ssm_scan(nc, io, s):
    with ExitStack() as c:
        sb = lambda n, sh, dt=F32: c.enter_context(nc.sbuf_tensor(n, sh, dt))
        sem = semaphores(nc, c)
        QP = PR // 4
        U = s.U
        Vr = sb("Vr", [P, PR, NC])
        Vi = sb("Vi", [P, PR, NC])
        Gr, Gi, w1, w2 = s.work
        Hr, Hi = Vr, Vi
        h0 = sb("h0", [P, 2, PR, NB_DEC])
        hn = sb("hn", [P, 2, PR, NB_DEC])
        hw = [Gr[:, :, NB_DEC * k:NB_DEC * (k + 1)] for k in range(4)]
        fin = sb("fin", [P, 2, PR])
        part = [wk[:, 4 * k:4 * k + 4, :].rearrange("p q j -> p (q j)") for wk in s.work for k in range(4)]
        ty, tz, tw, gl = part[0:4], part[4:8], part[8:12], part[12:16]
        bk = [c.enter_context(nc.psum_tensor(f"pv{k}", [P, 512], F32)) for k in range(8)]
        (h_in, v_made, v_kept, seq, hs_ready, fin_ready, hn_ready, sent, y_made, ya_kept, yv_kept, us_back, squared,
         cubed, tanhed, gelued, turned, g_kept, scanned) = (sem("sc_" + n) for n in (
            "h v_made v_kept seq hs fin hn sent y_made ya_kept yv_kept us_back squared cubed tanhed gelued turned "
            "g_kept scanned").split())
        YB = G // 4

        def y_place(j):
            u = s.us8 if j < YB else s.uc
            g0 = 8 * (j % YB // 2) + j % 2
            return u[:, g0:g0 + 7:2, :, :].rearrange("p g t c -> p g (t c)")

        def y_bank(j):
            return bk[j % 4][0:NB_DEC if j < YB else P, :].rearrange("p (g n) -> p g n", g=4)

        gc = lambda ap: ap.rearrange("p (g c) -> p g c", g=G)
        tile = lambda n: s.uc[:, :, n, :] if n < L else gc(s.us[:, :])
        rows_of = lambda n: P if n < L else NS

        with nc.Block() as block:
            @block.sync
            def _(sp):
                sp.dma_start(h0[:, 0, :, :], io["l_h0r"]).then_inc(h_in, 16)
                sp.dma_start(h0[:, 1, :, :], io["l_h0i"]).then_inc(h_in, 16)
                sp.wait_ge(ya_kept, YB)
                for t in range(T_DEC):
                    sp.dma_start(s.us[t:NS:T_DEC, :].rearrange("b (g c) -> b g c", g=G), s.us8[:, :, t, :]) \
                        .then_inc(us_back, 16)
                sp.wait_ge(fin_ready, 1)
                sp.dma_start(io["h_prompt"], fin[:, :, :]).then_inc(sent, 16)
                sp.wait_ge(hn_ready, 1)
                sp.dma_start(io["h_sample"], hn[:, :, :, :]).then_inc(sent, 16)
                sp.wait_ge(sent, 32)

            @block.tensor
            def _(pe):
                for q in range(PR):
                    k = 4 + q % 4
                    if q >= 4:
                        pe.wait_ge(v_kept, q - 3)
                    for r in range(2):
                        rows_ = slice(ST * r, ST * r + ST)
                        pe.matmul(bk[k][rows_, 0:NC], s.VTr[:, q, rows_], U[:, 2 * q + r, :], start=True, stop=True)
                        last = pe.matmul(bk[k][rows_, 256:256 + NC], s.VTi[:, q, rows_], U[:, 2 * q + r, :],
                                         start=True, stop=True)
                    last.then_inc(v_made, 1)
                pe.wait_ge(h_in, 32)
                for j in range(2 * YB):
                    sampled = j < YB
                    if j >= 4:
                        pe.wait_ge(*((ya_kept, j - 3) if j - 4 < YB else (yv_kept, j - 3 - YB)))
                    if not sampled and j % 2 == 0:
                        pe.wait_ge(hs_ready, (j - YB) // 2 + 1)
                    m = NB_DEC if sampled else P
                    for gg in range(4):
                        g = 8 * (j % YB // 2) + 2 * gg + j % 2
                        q, r = g // 2, slice(ST * (g % 2), ST * (g % 2) + ST)
                        out = bk[j % 4][0:m, gg * P:(gg + 1) * P]
                        cols = slice(CH + 1, CH + 1 + NB_DEC) if sampled else slice(0, CH)
                        hr = h0[r, 0, q, :] if sampled else Hr[r, q, 0:CH]
                        hi = h0[r, 1, q, :] if sampled else Hi[r, q, 0:CH]
                        pe.matmul(out, U[:, g, cols], s.T[:, g, :], start=True, stop=False)
                        pe.matmul(out, hr, s.CAr[r, q, :, :].rearrange("p t c -> p (t c)"), start=False, stop=False)
                        last = pe.matmul(out, hi, s.CAi[r, q, :, :].rearrange("p t c -> p (t c)"),
                                         start=False, stop=True)
                    last.then_inc(y_made, 1)
                pe.wait_ge(v_kept, PR)
                for n in range(L + 1):
                    m = rows_of(n)
                    pe.wait_ge(gelued, n + 1)
                    if n >= 4:
                        pe.wait_ge(g_kept, n - 3)
                    for k in range(4):
                        last = pe.transpose(bk[4 + n % 4][:, k * P:k * P + m], gl[n % 4][0:m, k * P:(k + 1) * P],
                                            s.ident[0:m, 0:m])
                    last.then_inc(turned, 1)

            @block.vector
            def _(dve):
                ch = Chain(dve, seq)
                tt = nc.vector.tensor_tensor
                dve.wait_ge(v_kept, PR)
                for k in range(4):
                    a = QP * k
                    full = (slice(None), slice(a, a + QP), slice(0, CH))
                    tt(w1[full], s.Er[full], Vr[full], ALU.mult)
                    tt(w2[full], s.Ei[full], Vi[full], ALU.mult)
                    tt(Gr[full], s.Er[full], Vi[full], ALU.mult)
                    ch(tt(Gi[full], s.Ei[full], Vr[full], ALU.mult))
                    tt(w1[full], w1[full], w2[full], ALU.add)
                    ch(tt(Gr[full], Gr[full], Gi[full], ALU.subtract))
                    for q in range(a, a + QP):
                        m8 = s.m8[:, q:q + 1].to_broadcast([P, CH])
                        nc.vector.tensor_tensor_scan(w2[:, q, :], m8, w1[:, q, :], 0.0, ALU.mult, ALU.add)
                        last = nc.vector.tensor_tensor_scan(Gi[:, q, :], m8, Gr[:, q, :], 0.0, ALU.mult, ALU.add)
                    ch(last)
                    nxt = (slice(None), slice(a, a + QP), slice(1, CH + 1))
                    nc.vector.memset(Hr[:, a:a + QP, 0:1], 0.0)
                    nc.vector.memset(Hi[:, a:a + QP, 0:1], 0.0)
                    tt(w1[full], s.Er[full], w2[full], ALU.mult)
                    ch(tt(Gr[full], s.Ei[full], Gi[full], ALU.mult))
                    ch(tt(Hr[nxt], w1[full], Gr[full], ALU.subtract))
                    tt(w1[full], s.Er[full], Gi[full], ALU.mult)
                    ch(tt(Gr[full], s.Ei[full], w2[full], ALU.mult))
                    tt(Hi[nxt], w1[full], Gr[full], ALU.add).then_inc(hs_ready, 1)
                dve.wait_ge(hs_ready, 4)
                nc.vector.tensor_copy(fin[:, 0, :], Hr[:, :, CH])
                nc.vector.tensor_copy(fin[:, 1, :], Hi[:, :, CH]).then_inc(fin_ready, 1)
                dve.wait_ge(h_in, 32)
                r8, i8 = wide(s.a8[:, 0, :], NB_DEC), wide(s.a8[:, 1, :], NB_DEC)
                tt(hw[0], h0[:, 0, :, :], r8, ALU.mult)
                tt(hw[1], h0[:, 1, :, :], i8, ALU.mult)
                tt(hw[2], h0[:, 1, :, :], r8, ALU.mult)
                ch(tt(hw[3], h0[:, 0, :, :], i8, ALU.mult))
                tt(hw[0], hw[0], hw[1], ALU.subtract)
                ch(tt(hw[2], hw[2], hw[3], ALU.add))
                tt(hn[:, 0, :, :], hw[0], Vr[:, :, CH + 1:], ALU.add)
                tt(hn[:, 1, :, :], hw[2], Vi[:, :, CH + 1:], ALU.add).then_inc(hn_ready, 1)
                for j in range(YB, 2 * YB):
                    dve.wait_ge(y_made, j + 1)
                    nc.vector.tensor_copy(y_place(j), y_bank(j)).then_inc(yv_kept, 1)
                for n in range(L + 2):
                    if n <= L:
                        m = rows_of(n)
                        dve.wait_ge(squared, n + 1)
                        if n >= 4:
                            dve.wait_ge(tanhed, n - 3)
                        nc.vector.scalar_tensor_tensor(gc(tz[n % 4])[0:m], gc(ty[n % 4])[0:m], 1.0, tile(n),
                                                       ALU.add, ALU.mult).then_inc(cubed, 1)
                    if n >= 1:
                        o, m = n - 1, rows_of(n - 1)
                        dve.wait_ge(tanhed, o + 1)
                        if o >= 4:
                            dve.wait_ge(turned, o - 3)
                        nc.vector.scalar_tensor_tensor(gc(gl[o % 4])[0:m], gc(tw[o % 4])[0:m], 1.0, tile(o),
                                                       ALU.add, ALU.mult).then_inc(gelued, 1)

            @block.scalar
            def _(act):
                for q in range(PR):
                    act.wait_ge(v_made, q + 1)
                    nc.scalar.activation(Vr[:, q, :], bk[4 + q % 4][:, 0:NC], ACT.Copy)
                    nc.scalar.activation(Vi[:, q, :], bk[4 + q % 4][:, 256:256 + NC], ACT.Copy).then_inc(v_kept, 1)
                for j in range(YB):
                    act.wait_ge(y_made, j + 1)
                    nc.scalar.activation(y_place(j), y_bank(j), ACT.Copy).then_inc(ya_kept, 1)
                act.wait_ge(yv_kept, YB)
                act.wait_ge(hn_ready, 1)
                for n in range(L + 3):
                    if n <= L:
                        m = rows_of(n)
                        if n == L:
                            act.wait_ge(us_back, 16 * T_DEC)
                        if n >= 4:
                            act.wait_ge(cubed, n - 3)
                        nc.scalar.activation(gc(ty[n % 4])[0:m], tile(n), ACT.Square, scale=0.044715 ** 0.5) \
                            .then_inc(squared, 1)
                    if 1 <= n <= L + 1:
                        o, m = n - 1, rows_of(n - 1)
                        act.wait_ge(cubed, o + 1)
                        if o >= 4:
                            act.wait_ge(gelued, o - 3)
                        nc.scalar.activation(tw[o % 4][0:m, :], tz[o % 4][0:m, :], ACT.Tanh,
                                             scale=0.7978845608028654).then_inc(tanhed, 1)
                    if n >= 2:
                        o, m = n - 2, rows_of(n - 2)
                        act.wait_ge(turned, o + 1)
                        src = bk[4 + o % 4][:, :].rearrange("p (k j) -> p k j", k=4)[:, :, 0:m]
                        dst = s.gT[:, :, o:SEQ:L] if o < L else s.gT[:, :, SEQ:N]
                        nc.scalar.activation(dst, src, ACT.Copy, scale=0.25).then_inc(g_kept, 1)


def layer_norm(ch, nc, r, out, g, b, st, mv, root):
    n = r.shape[0]
    nc.vector.bn_stats(st[0:n, 0, :], r[:, 0:512])
    ch(nc.vector.bn_stats(st[0:n, 1, :], r[:, 512:D]))
    ch(nc.vector.bn_aggr(mv[0:n, 0:2], st[0:n, :, :].rearrange("p a b -> p (a b)")))
    ch(nc.vector.tensor_scalar(mv[0:n, 2:3], mv[0:n, 1:2], EPS, None, ALU.add))
    root(mv[0:n, 2:3])
    ch(nc.vector.reciprocal(mv[0:n, 3:4], mv[0:n, 2:3]))
    ch(nc.vector.tensor_scalar(r, r, mv[0:n, 0:1], mv[0:n, 3:4], ALU.subtract, ALU.mult))
    ch(nc.vector.tensor_tensor(r, r, g[0:n, :], ALU.mult))
    return nc.vector.tensor_tensor(out, r, b[0:n, :], ALU.add)


def mix(nc, io, s):
    spans = [(0, 512), (512, 512), (SEQ, NS)]
    glu = [(k, n) for k in range(W // P) for n in range(3)]
    with ExitStack() as c:
        sb = lambda n, sh, dt=F32: c.enter_context(nc.sbuf_tensor(n, sh, dt))
        sem = semaphores(nc, c)
        place = iter(np.cumsum([WCOLS, W // P * W, KD * D, D, D]).tolist())
        a, b, e, f, g = place
        wg = s.wt[:, a:b].rearrange("p (k n) -> p k n", n=W)
        wo = s.wt[:, b:e].rearrange("p (k n) -> p k n", n=D)
        lg, lb = s.wt[:, e:f], s.wt[:, f:g]
        wr = sb("wr", [P, KD, E])
        bh = sb("bh", [P, W // P])
        sT = sb("sT", [P, W // P, N])
        tg = [sb(f"tg{k}", [P, 512]) for k in range(2)]
        xn = [sb(f"mx{k}", [P, D]) for k in range(2)]
        rr = [sb(f"mr{k}", [P, D]) for k in range(2)]
        xT = [sb(f"mt{k}", [P, KD, P]) for k in range(2)]
        st, mv = sb("mst", [P, 2, 6]), sb("mmv", [P, 4])
        bk = [c.enter_context(nc.psum_tensor(f"pm{k}", [P, 512], F32)) for k in range(8)]
        (wg_in, wo_in, wr_in, b_in, l_in, seq, z_made, z_used, tanhed, s_made, m_made, m_used, normed, var_ready,
         rooted, turned, t_kept, l_made, l_kept, b_halved, first_in) = (sem("mi_" + n) for n in (
            "wg wo wr b l seq z_made z_used tanhed s_made m_made m_used normed var_ready rooted turned t_kept "
            "l_made l_kept b_halved first_in").split())
        x_in = [sem(f"mi_x{k}") for k in range(2)]
        x_out = [sem(f"mi_xo{k}") for k in range(2)]

        with nc.Block() as block:
            @block.sync
            def _(sp):
                sp.dma_start(wg[:, :, :], io["ssm_w_glu"][0].rearrange("(k p) n -> p k n", p=P)).then_inc(wg_in, 16)
                sp.dma_start(bh[:, :], io["l_bglu"]).then_inc(b_in, 16)
                for b in range(2):
                    sp.dma_start(xn[b][:, :], io["x_prompt"][0, b * P:(b + 1) * P, :]).then_inc(x_in[b], 16)
                sp.dma_start(wo[:, :, :], io["w_out"][0].rearrange("(k p) n -> p k n", p=P)).then_inc(wo_in, 16)
                sp.dma_start(wr[:, :, :], io["router_w"].rearrange("(p k) e -> p k e", k=KD)).then_inc(wr_in, 16)
                sp.dma_start(lg[:, :], io["ln1_g"].to_broadcast([P, D])).then_inc(l_in, 16)
                sp.dma_start(lb[:, :], io["ln1_b"].to_broadcast([P, D])).then_inc(l_in, 16)
                for at, n, src in expert_weights(io, 0):
                    sp.dma_start(s.wt[:, at:at + n], src).then_inc(first_in, 16)
                for b in range(NBLK):
                    r = rows(b)
                    sp.wait_ge(normed, b + 1)
                    sp.dma_start(s.x1d[b * P:b * P + r, :], rr[b % 2][0:r, :]).then_inc(x_out[b % 2], 16)
                    if b + 2 < NBLK:
                        src = io["x_prompt"][0, (b + 2) * P:(b + 3) * P, :] if b + 2 < QB else \
                            io["x_sample"].rearrange("b t d -> (b t) d")
                        sp.wait_ge(m_used, b + 1)
                        sp.dma_start(xn[b % 2][0:rows(b + 2), :], src).then_inc(x_in[b % 2], 16)
                sp.wait_ge(x_out[0], 16 * (NBLK - NBLK // 2))
                sp.wait_ge(x_out[1], 16 * (NBLK // 2))
                sp.wait_ge(first_in, 16 * 4)

            @block.tensor
            def _(pe):
                pe.wait_ge(wg_in, 16)
                for i, (k, n) in enumerate(glu):
                    if i >= 4:
                        pe.wait_ge(tanhed, i - 3)
                    a, m = spans[n]
                    for j in range(W // P):
                        last = pe.matmul(bk[i % 4][:, 0:m], wg[:, j, k * P:(k + 1) * P], s.gT[:, j, a:a + m],
                                         start=(j == 0), stop=(j == W // P - 1))
                    last.then_inc(z_made, 1)
                pe.wait_ge(s_made, len(glu))
                pe.wait_ge(tanhed, len(glu))
                pe.wait_ge(wo_in, 16)
                pe.wait_ge(wr_in, 16)

                def project_out(b):
                    if b >= 2:
                        pe.wait_ge(m_used, b - 1)
                    r = rows(b)
                    for half in range(2):
                        for k in range(KD):
                            lhs = s.aT[:, k, b * P:b * P + r] if k < H else sT[:, k - H, b * P:b * P + r]
                            last = pe.matmul(bk[2 * (b % 2) + half][0:r, :], lhs, wo[:, k, half * 512:(half + 1) * 512],
                                             start=(k == 0), stop=(k == KD - 1))
                    last.then_inc(m_made, 1)

                def logits(b):
                    r = rows(b)
                    pe.wait_ge(normed, b + 1)
                    if b >= 1:
                        pe.wait_ge(t_kept, b)
                    xv = rr[b % 2][0:r, :].rearrange("t (p k) -> t k p", k=KD)
                    for k in range(KD):
                        last = pe.transpose(bk[4 + k // 4][:, (k % 4) * P:(k % 4) * P + r], xv[:, k, :],
                                            s.ident[0:r, 0:r])
                    last.then_inc(turned, 1)
                    pe.wait_ge(t_kept, b + 1)
                    if b >= 2:
                        pe.wait_ge(l_kept, b - 1)
                    for k in range(KD):
                        last = pe.matmul(bk[6 + b % 2][0:r, 0:E], xT[b % 2][:, k, 0:r], wr[:, k, :],
                                         start=(k == 0), stop=(k == KD - 1))
                    last.then_inc(l_made, 1)

                project_out(0)
                for b in range(NBLK):
                    if b + 1 < NBLK:
                        project_out(b + 1)
                    logits(b)

            @block.gpsimd
            def _(pool):
                pool.wait_ge(b_in, 16)
                nc.gpsimd.tensor_scalar(bh[:, :], bh[:, :], 0.5, None, ALU.mult).then_inc(b_halved, 1)

            @block.vector
            def _(dve):
                for i, (k, n) in enumerate(glu):
                    a, m = spans[n]
                    dve.wait_ge(tanhed, i + 1)
                    nc.vector.scalar_tensor_tensor(sT[:, k, a:a + m], tg[i % 2][:, 0:m], 1.0, s.gT[:, k, a:a + m],
                                                   ALU.add, ALU.mult).then_inc(s_made, 1)
                ch = Chain(dve, seq)
                ch(nc.vector.memset(s.lgt[:, QB, :], 0.0))
                dve.wait_ge(l_in, 32)
                roots = [0]
                for b in range(NBLK):
                    r = rows(b)
                    dve.wait_ge(m_made, b + 1)
                    dve.wait_ge(x_in[b % 2], 16 * (b // 2 + 1))
                    if b >= 2:
                        dve.wait_ge(x_out[b % 2], 16 * (b // 2))
                        dve.wait_ge(turned, b - 1)
                    for half in range(2):
                        cols = slice(512 * half, 512 * half + 512)
                        last = nc.vector.scalar_tensor_tensor(rr[b % 2][0:r, cols], xn[b % 2][0:r, cols], ALPHA,
                                                              bk[2 * (b % 2) + half][0:r, :], ALU.mult, ALU.add)
                    last.then_inc(m_used, 1)
                    dve.wait_ge(m_used, b + 1)

                    def root(ap, b=b):
                        dve.sem_inc(var_ready, 1)
                        dve.wait_ge(rooted, b + 1)

                    x = rr[b % 2][0:r, :]
                    layer_norm(ch, nc, x, x, lg, lb, st, mv, root).then_inc(normed, 1)
                    dve.wait_ge(l_made, b + 1)
                    nc.vector.tensor_copy(s.lgt[0:r, b, :], bk[6 + b % 2][0:r, 0:E]).then_inc(l_kept, 1)

            @block.scalar
            def _(act):
                act.wait_ge(b_halved, 1)
                for i, (k, n) in enumerate(glu):
                    a, m = spans[n]
                    act.wait_ge(z_made, i + 1)
                    if i >= 2:
                        act.wait_ge(s_made, i - 1)
                    nc.scalar.activation(tg[i % 2][:, 0:m], bk[i % 4][:, 0:m], ACT.Tanh, bias=bh[:, k:k + 1]) \
                        .then_inc(tanhed, 1)
                for b in range(NBLK):
                    r = rows(b)
                    act.wait_ge(var_ready, b + 1)
                    nc.scalar.activation(mv[0:r, 2:3], mv[0:r, 2:3], ACT.Sqrt).then_inc(rooted, 1)
                    act.wait_ge(turned, b + 1)
                    if b >= 2:
                        act.wait_ge(l_made, b - 1)
                    for half in range(2):
                        src = bk[4 + half][:, :].rearrange("p (k t) -> p k t", k=4)[:, :, 0:r]
                        last = nc.scalar.activation(xT[b % 2][:, 4 * half:4 * half + 4, 0:r], src, ACT.Copy)
                    last.then_inc(t_kept, 1)


def route(nc, io, s):
    with ExitStack() as c:
        sb = lambda n, sh, dt=F32: c.enter_context(nc.sbuf_tensor(n, sh, dt))
        sem = semaphores(nc, c)
        rb = sb("rb", [P, E])
        before = sb("before", [P, P])
        ones = sb("ones", [P, P])
        lower = sb("lower", [P, EG, EG])
        tok = sb("tok", [P, NBLK])
        count = sb("count", [P, P])
        same = sb("same", [P, 2 * NBLK, P])
        holds = sb("holds", [P, 2 * NBLK, NSB + 1])
        place, blk = sb("place", [P, 2, NBLK]), sb("blk", [P, 2, NBLK])
        past = sb("past", [1, NSB, E])
        cmp_, tie = sb("cmp", [P, NBLK * EG, EG * EG]), sb("tie", [P, NBLK * EG, EG * EG])
        big = lambda n: sb(n, [P, NBLK, E])
        sc, sel, M, gate, rank, eq, slot, lo = (big("r_" + n) for n in "sc sel M gate rank eq slot lo".split())
        grp = lambda n: sb(n, [P, NBLK, EG])
        h1, h2, l1, l2, m1, m2, gs, ig, fg, cm = (grp("r_" + n) for n in "h1 h2 l1 l2 m1 m2 gs ig fg cm".split())
        one = lambda n: sb(n, [P, NBLK])
        gm, tk, ws, sa, sz = (one("r_" + n) for n in "gm tk ws sa sz".split())
        tot, nb, end, beg = (sb("r_" + n, [P, E]) for n in "tot nb end beg".split())
        eb, w0, w1, w2 = (sb("r_" + n, [1, NSB]) for n in "eb w0 w1 w2".split())
        cnt = c.enter_context(nc.psum_tensor("cnt", [P, 512], F32))
        held = c.enter_context(nc.psum_tensor("ps_held", [P, NSB + 1], F32))
        (c_in, seq, tanhed, ones_set, m_ready, counted, slots_ready, placed) = (
            sem("ro_" + n) for n in "c_in seq tanhed ones m_ready counted slots placed".split())

        with nc.Block() as block:
            @block.sync
            def _(sp):
                sp.dma_start(rb[:, :], io["router_bias"].rearrange("(o e) -> o e", o=1).to_broadcast([P, E])).then_inc(c_in, 16)
                sp.dma_start(before[:, :], io["c_before"]).then_inc(c_in, 16)
                sp.dma_start(tok[:, :], io["c_tok"]).then_inc(c_in, 16)
                sp.dma_start(count[:, :], io["c_count"]).then_inc(c_in, 16)
                sp.dma_start(lower[:, :, :], io["c_lower"]).then_inc(c_in, 16)

            @block.scalar
            def _(act):
                nc.scalar.activation(sc[:, :, :], s.lgt[:, :, :], ACT.Tanh, scale=0.5).then_inc(tanhed, 1)

            @block.gpsimd
            def _(pool):
                nc.gpsimd.memset(ones[:, :], 1.0).then_inc(ones_set, 1)

            @block.tensor
            def _(pe):
                pe.wait_ge(c_in, 80)
                pe.wait_ge(ones_set, 1)
                pe.wait_ge(m_ready, 1)
                for b in range(NBLK + 1):
                    out = cnt[:, b * E:(b + 1) * E]
                    for a in range(min(b, NBLK)):
                        last = pe.matmul(out, ones[:, :], M[:, a, :], start=(a == 0), stop=(b == NBLK and a == NBLK - 1))
                    if b < NBLK:
                        last = pe.matmul(out, before[:, :], M[:, b, :], start=(b == 0), stop=True)
                last.then_inc(counted, 1)
                pe.wait_ge(slots_ready, 1)
                for i in range(2 * NBLK):
                    last = pe.matmul(held[:, :], same[:, i, :], holds[:, i, :], start=(i == 0), stop=(i == 2 * NBLK - 1))
                last.then_inc(placed, 1)

            @block.vector
            def _(dve):
                ch = Chain(dve, seq)
                ts, tt, stt = nc.vector.tensor_scalar, nc.vector.tensor_tensor, nc.vector.scalar_tensor_tensor
                A = lambda t: t[:, :, :]
                dve.wait_ge(tanhed, 1)
                dve.wait_ge(c_in, 80)
                ch(ts(A(sc), A(sc), 0.5, 0.5, ALU.mult, ALU.add))
                ch(tt(A(sel), A(sc), mid(rb[:, :], NBLK), ALU.add))
                v = sel[:, :, :].rearrange("p b (g e) -> p b g e", e=EG)
                e = [v[:, :, :, k] for k in range(EG)]
                tt(A(h1), e[0], e[1], ALU.max)
                tt(A(l1), e[0], e[1], ALU.min)
                tt(A(h2), e[2], e[3], ALU.max)
                ch(tt(A(l2), e[2], e[3], ALU.min))
                tt(A(m1), A(h1), A(h2), ALU.max)
                tt(A(m2), A(h1), A(h2), ALU.min)
                ch(tt(A(l1), A(l1), A(l2), ALU.max))
                ch(tt(A(m2), A(m2), A(l1), ALU.max))
                ch(tt(A(gs), A(m1), A(m2), ALU.add))
                ch(nc.vector.tensor_reduce(gm[:, :], A(gs), AX.X, ALU.max))
                ch(tt(A(ig), A(gs), wide(gm[:, :], EG), ALU.is_ge))
                ch(nc.vector.memset(tk[:, :], 1.0))
                for g in range(EG):
                    ch(tt(fg[:, :, g], ig[:, :, g], tk[:, :], ALU.mult))
                    ch(tt(tk[:, :], tk[:, :], fg[:, :, g], ALU.subtract))
                sv = sel[:, :, :].rearrange("p b (g e) -> p (b g) e", e=EG)
                row = sv.unsqueeze(3).to_broadcast([P, NBLK * EG, EG, EG])
                col = sv.unsqueeze(2).to_broadcast([P, NBLK * EG, EG, EG])
                table = lambda t: t[:, :, :].rearrange("p n (i j) -> p n i j", j=EG)
                tt(table(cmp_), col, row, ALU.is_gt)
                ch(tt(table(tie), col, row, ALU.is_equal))
                ch(tt(table(tie), table(tie), lower[:, :, :].unsqueeze(1).to_broadcast([P, NBLK * EG, EG, EG]), ALU.mult))
                ch(tt(cmp_[:, :, :], cmp_[:, :, :], tie[:, :, :], ALU.add))
                ch(nc.vector.tensor_reduce(rank[:, :, :].rearrange("p b (g e) -> p (b g) e", e=EG), table(cmp_), AX.X, ALU.add))
                ch(ts(A(M), A(rank), 2.0, None, ALU.is_lt))
                mv_ = M[:, :, :].rearrange("p b (g e) -> p b g e", e=EG)
                for k in range(EG):
                    last = tt(mv_[:, :, :, k], mv_[:, :, :, k], A(fg), ALU.mult)
                ch(last)
                ch(tt(A(gate), A(sc), A(M), ALU.mult))
                ch(nc.vector.tensor_reduce(ws[:, :], A(gate), AX.X, ALU.add))
                ch(nc.vector.reciprocal(ws[:, :], ws[:, :]))
                ch(tt(A(gate), A(gate), wide(ws[:, :], E), ALU.mult))
                ch(nc.vector.memset(M[NS:P, QB, :], 0.0))
                dve.sem_inc(m_ready, 1)
                dve.wait_ge(counted, 1)
                nc.vector.tensor_copy(tot[:, :], cnt[:, NBLK * E:(NBLK + 1) * E])
                ch(nc.vector.tensor_copy(A(slot), cnt[:, 0:NBLK * E].rearrange("p (b e) -> p b e", b=NBLK)))
                ch(ts(nb[:, :], tot[:, :], 1.0 / SLOTB, (SLOTB - 1.0) / SLOTB - 0.5 + 0.5 / SLOTB, ALU.mult, ALU.add))
                ch(ts(nb[:, :], nb[:, :], MAGIC, None, ALU.add))
                ch(ts(nb[:, :], nb[:, :], MAGIC, None, ALU.subtract))
                ch(nc.vector.tensor_tensor_scan(end[:, :], ones[:, 0:E], nb[:, :], 0.0, ALU.mult, ALU.add))
                ch(tt(beg[:, :], end[:, :], nb[:, :], ALU.subtract))
                ch(ts(beg[:, :], beg[:, :], float(SLOTB), None, ALU.mult))
                ch(tt(A(slot), A(slot), mid(beg[:, :], NBLK), ALU.add))
                FAR = float(1 << 20)
                ch(ts(A(slot), A(slot), FAR, None, ALU.subtract))
                ch(tt(A(lo), A(slot), A(M), ALU.mult))
                ch(nc.vector.tensor_reduce(sa[:, :], A(lo), AX.X, ALU.min))
                ch(tt(A(eq), A(lo), wide(sa[:, :], E), ALU.is_equal))
                ch(tt(A(lo), A(slot), A(M), ALU.mult))
                ch(tt(A(rank), A(M), A(eq), ALU.subtract))
                ch(tt(A(lo), A(slot), A(rank), ALU.mult))
                ch(nc.vector.tensor_reduce(sz[:, :], A(lo), AX.X, ALU.min))
                ch(ts(sa[:, :], sa[:, :], FAR, None, ALU.add))
                ch(ts(sz[:, :], sz[:, :], FAR, None, ALU.add))
                nc.vector.tensor_copy(s.slots[:, 0, :], sa[:, :])
                ch(nc.vector.tensor_copy(s.slots[:, 1, :], sz[:, :]))
                ts(blk[:, 0, :], sa[:, :], 1.0 / SLOTB, 0.5 / SLOTB - 0.5, ALU.mult, ALU.add)
                ch(ts(blk[:, 1, :], sz[:, :], 1.0 / SLOTB, 0.5 / SLOTB - 0.5, ALU.mult, ALU.add))
                ch(ts(A(blk), A(blk), MAGIC, None, ALU.add))
                ch(ts(A(blk), A(blk), MAGIC, None, ALU.subtract))
                stt(place[:, 0, :], blk[:, 0, :], -float(SLOTB), sa[:, :], ALU.mult, ALU.add)
                ch(stt(place[:, 1, :], blk[:, 1, :], -float(SLOTB), sz[:, :], ALU.mult, ALU.add))
                flat = lambda t: t[:, :, :].rearrange("p k b -> p (k b)")
                tt(A(same), mid(count[:, :], 2 * NBLK), wide(flat(place), P), ALU.is_equal)
                ch(tt(A(holds), mid(count[:, 0:NSB + 1], 2 * NBLK), wide(flat(blk), NSB + 1), ALU.is_equal))
                hv = holds[:, :, :].rearrange("p (k b) n -> p k b n", k=2)
                for k in range(2):
                    last = tt(hv[:, k, :, :], hv[:, k, :, :], wide(tok[:, :], NSB + 1), ALU.mult)
                ch(last)
                dve.sem_inc(slots_ready, 1)
                ch(tt(A(lo), A(gate), A(eq), ALU.mult))
                ch(nc.vector.tensor_reduce(s.gates[:, 0, :], A(lo), AX.X, ALU.add))
                ch(tt(A(lo), A(gate), A(rank), ALU.mult))
                ch(nc.vector.tensor_reduce(s.gates[:, 1, :], A(lo), AX.X, ALU.add))
                ch(tt(A(past), wide(count[0:1, 0:NSB], E), mid(end[0:1, :], NSB), ALU.is_ge))
                ch(nc.vector.tensor_reduce(eb[:, :], A(past), AX.X, ALU.add))
                ch(ts(eb[:, :], eb[:, :], E - 1.0, None, ALU.min))
                ch(ts(w0[:, :], eb[:, :], 0.5, -0.25, ALU.mult, ALU.add))
                ch(ts(w0[:, :], w0[:, :], MAGIC, None, ALU.add))
                ch(ts(w0[:, :], w0[:, :], MAGIC, None, ALU.subtract))
                ch(stt(w1[:, :], w0[:, :], -1.0, eb[:, :], ALU.mult, ALU.add))
                ch(tt(w2[:, :], w1[:, :], w0[:, :], ALU.subtract))
                ts(s.wtab[:, 0, :], w2[:, :], float(WCOLS), None, ALU.mult)
                ts(s.wtab[:, 1, :], w0[:, :], 32.0, 32.0, ALU.mult, ALU.add)
                ts(s.wtab[:, 2, :], w1[:, :], 32.0, 32.0, ALU.mult, ALU.max)
                ts(s.ends[:, :], end[0:1, :], 1.0, None, ALU.add)
                ch(ts(nb[:, 0:1], end[:, E - 1:E], 0.5, 0.25, ALU.mult, ALU.add))
                ch(ts(nb[:, 0:1], nb[:, 0:1], MAGIC, None, ALU.add))
                ch(ts(nb[:, 0:1], nb[:, 0:1], MAGIC, None, ALU.subtract))
                ts(s.more_pairs[:, 0:1], nb[0:1, 0:1], 1.0, None, ALU.subtract)
                ch(ts(s.more_pairs[:, 1:2], nb[0:1, 0:1], -1.0, float(NSB // 2), ALU.mult, ALU.add))
                dve.wait_ge(placed, 1)
                nc.vector.tensor_copy(s.held[:, :], held[:, :])


def expert_weights(io, e):
    half = KF * D // 2
    for at, n, name, lo in ((GATE_AT, KD * FE, "moe_w_gate", 0), (UP_AT, KD * FE, "moe_w_up", 0),
                            (DOWN_AT, half, "moe_w_down", 0), (DOWN_AT + half, half, "moe_w_down", half)):
        v = io[name][0].rearrange("e (p k) f -> e p (k f)", p=P)
        yield at, n, v[bass.ds(e, 1), :, lo:lo + n].rearrange("o p n -> p (o n)")


def experts(nc, io, s):
    with ExitStack() as c:
        sb = lambda n, sh, dt=F32: c.enter_context(nc.sbuf_tensor(n, sh, dt))
        sem = semaphores(nc, c)
        wt = s.wt
        idxc = [sb(f"idxc{j}", [P, 1], I32) for j in range(2)]
        xg = [sb(f"xg{j}", [P, D]) for j in range(2)]
        xT = [sb(f"ext{j}", [P, KD, P]) for j in range(2)]
        th = [sb(f"eth{j}", [P, FE]) for j in range(2)]
        ha = [sb(f"eha{j}", [P, FE]) for j in range(2)]
        hh = [sb(f"ehh{j}", [P, FE]) for j in range(2)]
        hT = [sb(f"eht{j}", [P, KF, P]) for j in range(2)]
        yb = [sb(f"eyb{j}", [P, D]) for j in range(2)]
        nul = sb("enul", [P, D])
        nul_set, nul_sent = sem("ex_nul_set"), sem("ex_nul_sent")
        all_sent, idle_cleared, gather_next = sem("ex_all_sent"), sem("ex_idle_cleared"), sem("ex_gather_next")
        psG = c.enter_context(nc.psum_tensor("psG", [P, FE], F32))
        psU = c.enter_context(nc.psum_tensor("psU", [P, FE], F32))
        psY = c.enter_context(nc.psum_tensor("psY", [P, D], F32))
        psX = c.enter_context(nc.psum_tensor("psX", [P, D], F32))
        psH = c.enter_context(nc.psum_tensor("psH", [P, FE], F32))
        (idx_kept, x_turned, x_kept, gu_made, tanhed, halfway, act_done, h_turned, h_kept, y_made, y_kept) = (
            sem("ex_" + n) for n in "idx_kept x_turned x_kept gu_made tanhed halfway act_done h_turned h_kept "
            "y_made y_kept".split())
        gathered = [sem(f"ex_gathered{j}") for j in range(2)]
        y_sent = [sem(f"ex_sent{j}") for j in range(2)]
        gu_in = [sem(f"ex_gu{j}") for j in range(2)]
        d_in = [sem(f"ex_d{j}") for j in range(2)]

        def over_pairs(eng, pair):
            more = eng.value_load(s.more_pairs[0:1, 0:1], min_val=USED_PAIRS - 1, max_val=NSB // 2 - 2)
            pair(0, True)
            pair(1, False)
            with eng.Fori(2, NSB // 2) as bb:
                with eng.If(bb <= more):
                    pair(bb, False)
            return more

        with nc.Block() as block:
            @block.sync
            def _(sp):
                def load(e, j, free):
                    for i, (at, n, src) in enumerate(expert_weights(io, e)):
                        if free is not None and i % 2 == 0:
                            sp.wait_ge((gu_made, y_made)[i // 2], free)
                        sp.dma_start(wt[:, j * WCOLS + at:j * WCOLS + at + n], src).then_inc((gu_in, d_in)[i // 2][j], 16)

                sp.sem_inc(gu_in[0], 32)
                sp.sem_inc(d_in[0], 32)
                load(1, 1, None)
                with sp.Fori(1, E // 2) as ee:
                    for j in range(2):
                        free = sp.value_load(s.ends[0:1, bass.ds(2 * ee - 2 + j, 1)], min_val=1, max_val=NSB)
                        load(2 * ee + j, j, free)
                more = sp.value_load(s.more_pairs[0:1, 0:1], min_val=USED_PAIRS - 1, max_val=NSB // 2 - 2)
                idle = sp.value_load(s.more_pairs[0:1, 1:2], min_val=1, max_val=NSB // 2 - USED_PAIRS)
                sp.wait_ge(nul_set, 1)
                with sp.Fori(1, NSB // 2) as bb:
                    with sp.If(bb > more):
                        dst = s.yd[bass.ds(bb * (2 * SLOTB), 2 * SLOTB), :].rearrange("(j p) d -> p j d", p=P)
                        sp.dma_start(dst, nul[:, :].unsqueeze(1).to_broadcast([P, 2, D])).then_inc(nul_sent, 16)
                sp.wait_ge(nul_sent, 16 * idle)
                sp.sem_inc(idle_cleared, 1)
                sp.wait_ge(idle_cleared, 1)
                for j in range(2):
                    sp.wait_ge(gu_in[j], 32 * E // 2)
                    sp.wait_ge(d_in[j], 32 * E // 2)

            @block.gpsimd
            def _(pool):
                nc.gpsimd.memset(nul[:, :], 0.0).then_inc(nul_set, 1)

                def gather(b, j):
                    nc.gpsimd.tensor_copy(idxc[j][:, :], s.held[:, bass.ds(b, 1)]).then_inc(idx_kept, 1)
                    pool.wait_ge(idx_kept, b + 1)
                    pool.sem_inc(gather_next, 1)
                    pool.wait_ge(nul_set, 1)
                    nc.gpsimd.indirect_dma_start(xg[j][:, :], None, s.x1d,
                                                 bass.IndirectOffsetOnAxis(ap=idxc[j][:, 0:1], axis=0)) \
                        .then_inc(gathered[j], 16)

                gather(0, 0)

                def pair(bb, first):
                    for j in range(2):
                        b = 2 * bb + j
                        if not (first and j == 0):
                            pool.wait_ge(x_turned, b)
                        gather(b + 1, 1 - j)

                more = over_pairs(pool, pair)
                pool.wait_ge(gathered[0], 16 * more + 32)
                pool.wait_ge(gathered[1], 16 * more + 16)

            @block.tensor
            def _(pe):
                def weights(b):
                    off = pe.value_load(s.wtab[0:1, 0, bass.ds(b, 1)], min_val=0, max_val=WCOLS)
                    n0 = pe.value_load(s.wtab[0:1, 1, bass.ds(b, 1)], min_val=32, max_val=32 * E)
                    n1 = pe.value_load(s.wtab[0:1, 2, bass.ds(b, 1)], min_val=32, max_val=32 * E)
                    return off, n0, n1

                def turn_x(b, j, loads):
                    pe.wait_ge(gathered[j], 16 * loads)
                    xv = xg[j][:, :].rearrange("t (p k) -> t k p", k=KD)
                    for k in range(KD):
                        last = pe.transpose(psX[:, k * P:(k + 1) * P], xv[:, k, :], s.ident[:, :])
                    last.then_inc(x_turned, 1)

                def gate_up(b, j, first):
                    off, n0, n1 = weights(b)
                    pe.wait_ge(gu_in[0], n0)
                    if not (first and j == 0):
                        pe.wait_ge(gu_in[1], n1)
                    pe.wait_ge(x_kept, b + 1)
                    if not (first and j == 0):
                        pe.wait_ge(act_done, b)
                    for ps, at in ((psG, GATE_AT), (psU, UP_AT)):
                        for k in range(KD):
                            last = pe.matmul(ps[:, :], xT[j][:, k, :], wt[:, bass.ds(off + (at + k * FE), FE)],
                                             start=(k == 0), stop=(k == KD - 1))
                    last.then_inc(gu_made, 1)

                def turn_h(b, j, first):
                    pe.wait_ge(act_done, b + 1)
                    if not (first and j == 0):
                        pe.wait_ge(h_kept, b)
                    hv = hh[j][:, :].rearrange("t (p k) -> t k p", k=KF)
                    for k in range(KF):
                        last = pe.transpose(psH[:, k * P:(k + 1) * P], hv[:, k, :], s.ident[:, :])
                    last.then_inc(h_turned, 1)

                def down(b, j, old):
                    off, n0, n1 = weights(b)
                    pe.wait_ge(d_in[0], n0)
                    if type(b) is not int or b > 0:
                        pe.wait_ge(d_in[1], n1)
                    pe.wait_ge(h_kept, b + 1)
                    if old:
                        pe.wait_ge(y_kept, b)
                    for half in range(2):
                        for k in range(KF):
                            at = DOWN_AT + k * D + half * 512
                            last = pe.matmul(psY[:, half * 512:half * 512 + 512], hT[j][:, k, :],
                                             wt[:, bass.ds(off + at, 512)], start=(k == 0), stop=(k == KF - 1))
                    last.then_inc(y_made, 1)

                pe.sem_inc(gu_made, 1)
                pe.sem_inc(y_made, 1)
                turn_x(0, 0, 1)

                def pair(bb, first):
                    for j in range(2):
                        b = 2 * bb + j
                        gate_up(b, j, first)
                        if not (first and j == 0):
                            down(b - 1, 1 - j, not (first and j == 1))
                        pe.wait_ge(x_kept, b + 1)
                        turn_x(b + 1, 1 - j, bb + 1 + j)
                        turn_h(b, j, first)

                more = over_pairs(pe, pair)
                down(2 * more + 1, 1, True)

            @block.scalar
            def _(act):
                def keep_x(b, j, old):
                    act.wait_ge(x_turned, b + 1)
                    if old:
                        act.wait_ge(gu_made, b)
                    nc.scalar.activation(xT[j][:, :, :].rearrange("p k t -> p (k t)"), psX[:, :], ACT.Copy) \
                        .then_inc(x_kept, 1)

                def keep_y(b, j, bb):
                    act.wait_ge(y_made, b + 2)
                    if bb is not None:
                        act.wait_ge(y_sent[j], 16 * bb)
                    nc.scalar.activation(yb[j][:, :], psY[:, :], ACT.Copy).then_inc(y_kept, 1)
                    act.wait_ge(y_kept, b + 1)
                    act.dma_start(s.yd[bass.ds(b * P, P), :], yb[j][:, :]).then_inc(y_sent[j], 16)

                keep_x(0, 0, False)

                def pair(bb, first):
                    for j in range(2):
                        b = 2 * bb + j
                        act.wait_ge(gu_made, b + 2)
                        if not first:
                            act.wait_ge(act_done, b - 1)
                        nc.scalar.activation(th[j][:, :], psG[:, :], ACT.Tanh, scale=0.5).then_inc(tanhed, 1)
                        if not (first and j == 0):
                            keep_y(b - 1, 1 - j, bb - 1 + j if type(bb) is not int or bb - 1 + j > 0 else None)
                        keep_x(b + 1, 1 - j, not (first and j == 0))

                more = over_pairs(act, pair)
                keep_y(2 * more + 1, 1, more)
                act.wait_ge(y_sent[0], 16 * more + 16)
                act.wait_ge(y_sent[1], 16 * more + 16)
                act.sem_inc(all_sent, 1)
                act.wait_ge(all_sent, 1)

            @block.vector
            def _(dve):
                def pair(bb, first):
                    for j in range(2):
                        b = 2 * bb + j
                        dve.wait_ge(tanhed, b + 1)
                        nc.vector.scalar_tensor_tensor(ha[j][:, :], th[j][:, :], 1.0, psG[:, :], ALU.add, ALU.mult) \
                            .then_inc(halfway, 1)
                        dve.wait_ge(halfway, b + 1)
                        if not first:
                            dve.wait_ge(h_turned, b - 1)
                        nc.vector.scalar_tensor_tensor(hh[j][:, :], ha[j][:, :], 0.5, psU[:, :], ALU.mult, ALU.mult) \
                            .then_inc(act_done, 1)
                        dve.wait_ge(h_turned, b + 1)
                        if not first:
                            dve.wait_ge(y_made, b)
                        nc.vector.tensor_copy(hT[j][:, :, :].rearrange("p k t -> p (k t)"), psH[:, :]) \
                            .then_inc(h_kept, 1)

                over_pairs(dve, pair)


def combine(nc, io, s):
    with ExitStack() as c:
        sb = lambda n, sh, dt=F32: c.enter_context(nc.sbuf_tensor(n, sh, dt))
        sem = semaphores(nc, c)
        lg, lb = sb("cg", [P, D]), sb("cb", [P, D])
        ya = [[sb(f"ya{k}{j}", [P, D]) for j in range(3)] for k in range(2)]
        x1 = [sb(f"x1{j}", [P, D]) for j in range(3)]
        t = sb("ct", [P, D])
        out = [sb(f"co{j}", [P, D]) for j in range(2)]
        st, mv = sb("cst", [P, 2, 6]), sb("cmv", [P, 4])
        l_in, seq, scaled, taken, var_ready, rooted, normed = (
            sem("co_" + n) for n in "l_in seq scaled taken var rooted normed".split())
        y_in = [sem(f"co_y{j}") for j in range(3)]
        x_in = [sem(f"co_x{j}") for j in range(3)]
        o_out = [sem(f"co_o{j}") for j in range(2)]

        with nc.Block() as block:
            @block.gpsimd
            def _(pool):
                for b in range(NBLK):
                    r = rows(b)
                    if b >= 3:
                        pool.wait_ge(taken, b - 2)
                    for k in range(2):
                        nc.gpsimd.indirect_dma_start(
                            ya[k][b % 3][0:r, :], None, s.yd,
                            bass.IndirectOffsetOnAxis(ap=s.slots[0:r, k, b:b + 1], axis=0)).then_inc(y_in[b % 3], 16)

            @block.sync
            def _(sp):
                sp.dma_start(lg[:, :], io["ln2_g"].to_broadcast([P, D])).then_inc(l_in, 16)
                sp.dma_start(lb[:, :], io["ln2_b"].to_broadcast([P, D])).then_inc(l_in, 16)

                def load(b):
                    r = rows(b)
                    sp.dma_start(x1[b % 3][0:r, :], s.x1d[b * P:b * P + r, :]).then_inc(x_in[b % 3], 16)

                for b in range(3):
                    load(b)
                for b in range(NBLK):
                    r = rows(b)
                    sp.wait_ge(normed, b + 1)
                    dst = io["y_prompt"][0, b * P:(b + 1) * P, :] if b < QB else io["y_sample"].rearrange("b t d -> (b t) d")
                    sp.dma_start(dst, out[b % 2][0:r, :]).then_inc(o_out[b % 2], 16)
                    if b + 3 < NBLK:
                        sp.wait_ge(taken, b + 1)
                        load(b + 3)
                sp.wait_ge(o_out[0], 16 * (NBLK - NBLK // 2))
                sp.wait_ge(o_out[1], 16 * (NBLK // 2))

            @block.scalar
            def _(act):
                for b in range(NBLK):
                    r = rows(b)
                    act.wait_ge(y_in[b % 3], 32 * (b // 3 + 1))
                    nc.scalar.activation(ya[0][b % 3][0:r, :], ya[0][b % 3][0:r, :], ACT.Copy,
                                         scale=s.gates[0:r, 0, b:b + 1]).then_inc(scaled, 1)
                    act.wait_ge(var_ready, b + 1)
                    nc.scalar.activation(mv[0:r, 2:3], mv[0:r, 2:3], ACT.Sqrt).then_inc(rooted, 1)

            @block.vector
            def _(dve):
                ch = Chain(dve, seq)
                dve.wait_ge(l_in, 32)
                for b in range(NBLK):
                    r = rows(b)
                    a0, a1, x = ya[0][b % 3][0:r, :], ya[1][b % 3][0:r, :], x1[b % 3][0:r, :]
                    dve.wait_ge(scaled, b + 1)
                    dve.wait_ge(y_in[b % 3], 32 * (b // 3 + 1))
                    if b >= 1:
                        dve.wait_ge(normed, b)
                    ch(nc.vector.scalar_tensor_tensor(t[0:r, :], a1, s.gates[0:r, 1, b:b + 1], a0, ALU.mult, ALU.add))
                    dve.wait_ge(x_in[b % 3], 16 * (b // 3 + 1))
                    nc.vector.scalar_tensor_tensor(t[0:r, :], x, ALPHA, t[0:r, :], ALU.mult, ALU.add).then_inc(taken, 1)
                    dve.wait_ge(taken, b + 1)
                    if b >= 2:
                        dve.wait_ge(o_out[b % 2], 16 * (b // 2))

                    def root(ap, b=b):
                        dve.sem_inc(var_ready, 1)
                        dve.wait_ge(rooted, b + 1)

                    layer_norm(ch, nc, t[0:r, :], out[b % 2][0:r, :], lg, lb, st, mv, root).then_inc(normed, 1)


def constants():
    ident = np.eye(P, dtype=np.float32)
    slope = 2.0 ** (-8.0 * np.arange(1, H + 1, dtype=np.float32) / H)
    dist = np.arange(P)[:, None] - (np.arange(SEQ)[None, :] - (SEQ - P))
    bias = np.where(dist[:, None, :] >= 0, -slope[None, :, None] * dist[:, None, :], NEG)
    r = np.arange(P)
    seq, t = (r % NS) // T_DEC, r % T_DEC
    past = PAST + t[:, None] - np.arange(PAST)[None, :]
    new = t[:, None] - (np.arange(NS) % T_DEC)[None, :]
    same = seq[:, None] == (np.arange(NS) // T_DEC)[None, :]
    dist_s = np.concatenate([past, np.where(same, new, -1)], 1)
    bias_s = np.where(dist_s[:, None, :] >= 0, -slope[None, :, None] * dist_s[:, None, :], NEG)
    two = np.concatenate([np.eye(NS), np.eye(NS)], 0)
    sel = np.stack([r < NS, r >= NS], 1).astype(np.float32)
    f = lambda a: np.ascontiguousarray(a, dtype=np.float32)
    before = (r[:, None] < r[None, :])
    tok = np.arange(NBLK)[None, :] * P + r[:, None]
    return {"c_before": f(before), "c_tok": f(tok), "c_count": f(np.tile(r, (P, 1))),
            "c_lower": f(np.tile(np.tri(EG, EG, -1), (P, 1, 1))), "c_ident": ident, "c_bias": f(bias), "c_bias_s": f(bias_s), "c_two": f(two), "c_sel": f(sel)}


class Stage:
    pass


def layouts(i):
    pair = lambda a: np.asarray(a).reshape(PR, 2, ST).transpose(1, 2, 0).reshape(P, PR)
    par = np.stack([pair(i["ssm_lambda_re"][0]), pair(i["ssm_lambda_im"][0]),
                    pair(np.repeat(np.asarray(i["ssm_log_dt"][0])[:, None], ST, 1))], 1)
    out = {"l_par": par}
    for n in "re", "im":
        out["l_b" + n] = np.asarray(i["ssm_b_" + n][0]).reshape(PR, 2, ST, GC).transpose(1, 2, 0, 3).reshape(P, PR, GC)
        cc = np.asarray(i["ssm_c_" + n][0]).reshape(PR, 2, GC, ST).transpose(1, 3, 0, 2)
        out["l_c" + n] = cc.reshape(P, PR, GC)
        blk = np.zeros((2, ST, PR, 2, GC), np.float32)
        for r in range(2):
            blk[r, :, :, r, :] = cc[r]
        out["l_cb" + n[0]] = blk.reshape(P, PR, 2 * GC)
        h = np.asarray(i["state_ssm_" + n][0]).reshape(NB_DEC, PR, 2, ST).transpose(2, 3, 1, 0)
        out["l_h0" + n[0]] = h.reshape(P, PR, NB_DEC)
    d = np.asarray(i["ssm_d"][0]).reshape(G, GC)
    kd = np.zeros((P, G, GC), np.float32)
    for ch in range(GC):
        kd[P - GC + ch, :, ch] = d[:, ch]
    out["l_d"] = kd.reshape(P, W)
    out["l_bglu"] = np.asarray(i["ssm_b_glu"][0]).reshape(W // P, P).T
    return {k: np.ascontiguousarray(v) for k, v in out.items()}


def program(nc, io):
    s = Stage()
    with ExitStack() as c:
        sb = lambda n, sh, dt=F32: c.enter_context(nc.sbuf_tensor(n, sh, dt))
        s.ident = sb("ident", [P, P])
        s.lgt = sb("lgt", [P, NBLK, E])
        s.slots = sb("slots", [P, 2, NBLK], I32)
        s.gates = sb("gates", [P, 2, NBLK])
        s.wtab = sb("wtab", [1, 3, NSB], I32)
        s.ends = sb("ends", [1, E], I32)
        s.held = sb("held", [P, NSB + 1], I32)
        s.more_pairs = sb("more_pairs", [1, 2], I32)
        s.x1d = nc.dram_tensor("x1d", [N, D], F32).ap()
        s.yd = nc.dram_tensor("yd", [NSB * SLOTB, D], F32).ap()
        s.nlam = sb("nlam", [P, 1])
        s.aT = sb("aT", [P, H, N])
        s.qT = sb("qT", [P, H, N])
        s.gT = s.qT
        token_mixing(nc, io, s)
        s.wt = sb("wt", [P, 2 * WCOLS])
        mix(nc, io, s)
        route(nc, io, s)
        experts(nc, io, s)
        combine(nc, io, s)


def token_mixing(nc, io, s):
    with ExitStack() as c:
        sb = lambda n, sh, dt=F32: c.enter_context(nc.sbuf_tensor(n, sh, dt))
        s.uc = sb("uc", [P, G, L, GC])
        s.us = sb("us", [NS, W])
        with ExitStack() as a:
            sa = lambda n, sh, dt=F32: a.enter_context(nc.sbuf_tensor(n, sh, dt))
            s.v = sa("v", [P, NBLK, W])
            s.kT = sa("kT", [P, H, N])
            project(nc, io, s)
            s.o = sa("o", [P, NBLK, W])
            s.ss = sa("ss", [P, NBLK, H])
            s.ptab = sa("ptab", [1, NB_DEC * NPG], I32)
            s.kc = sa("kc", [P, NB_DEC * NPG, W])
            attend(nc, io, s)
            sample(nc, io, s)
            head_norm(nc, io, s)
        with ExitStack() as a:
            sa = lambda n, sh, dt=F32: a.enter_context(nc.sbuf_tensor(n, sh, dt))
            s.T = sa("T", [P, G, P])
            s.VTr = sa("VTr", [P, PR, P])
            s.VTi = sa("VTi", [P, PR, P])
            s.CAr = sa("CAr", [P, PR, L, GC])
            s.CAi = sa("CAi", [P, PR, L, GC])
            s.Er = sa("Er", [P, PR, CH])
            s.Ei = sa("Ei", [P, PR, CH])
            s.m8 = sa("m8", [P, PR])
            s.a8 = sa("a8", [P, 2, PR])
            s.us8 = sa("us8", [NB_DEC, G, L, GC])
            s.U = sa("U", [P, G, NC])
            s.work = [sa(f"work{n}", [P, PR, CH]) for n in range(4)]
            ssm_tables(nc, io, s)
            ssm_scan(nc, io, s)


_DIRECT = ["x_prompt", "x_sample", "cache_k", "cache_v", "page_table", "w_in", "w_out", "ln1_g", "ln1_b", "ln2_g",
           "ln2_b", "lambda_q1", "lambda_k1", "lambda_q2", "lambda_k2", "subln_g", "ssm_w_glu", "router_w",
           "router_bias", "moe_w_gate", "moe_w_up", "moe_w_down"]
_OUTS = {"y_prompt": (1, SEQ, D), "y_sample": (NB_DEC, T_DEC, D),
         "new_k_prompt": (1, 1, SEQ, H, P), "new_v_prompt": (1, 1, SEQ, H, P),
         "new_k_sample": (1, NB_DEC, T_DEC, H, P), "new_v_sample": (1, NB_DEC, T_DEC, H, P),
         "h_prompt": (P, 2, PR), "h_sample": (P, 2, PR, NB_DEC)}


def kernel(**inputs):
    import concourse.bacc as bacc
    from concourse.bass_utils import run_bass_kernel_spmd

    nc = bacc.Bacc("TRN2", target_bir_lowering=False, num_devices=1)
    given = {n: np.ascontiguousarray(inputs[n]) for n in _DIRECT}
    given.update(layouts(inputs))
    given.update(constants())
    io = {n: nc.dram_tensor("in_" + n, a.shape, mybir.dt.from_np(a.dtype), kind="ExternalInput").ap()
          for n, a in given.items()}
    for n, shape in _OUTS.items():
        io[n] = nc.dram_tensor("out_" + n, shape, F32, kind="ExternalOutput").ap()
    program(nc, io)
    got = run_bass_kernel_spmd(nc, [{"in_" + n: a for n, a in given.items()}], core_ids=[0]).results[0]
    out = {n: got["out_" + n] for n in _OUTS}
    hp = out["h_prompt"].reshape(2, ST, 2, PR).transpose(2, 3, 0, 1).reshape(2, 1, 1, G, ST)
    hs = out["h_sample"].reshape(2, ST, 2, PR, NB_DEC).transpose(2, 4, 3, 0, 1).reshape(2, 1, NB_DEC, G, ST)
    return (out["y_prompt"], out["y_sample"], out["new_k_prompt"], out["new_v_prompt"], hp[0], hp[1],
            out["new_k_sample"], out["new_v_sample"], hs[0], hs[1])
```

```python
from contextlib import ExitStack

import numpy as np

import concourse.bass as bass
from concourse import mybir

F32 = mybir.dt.float32
I32 = mybir.dt.int32
F32R = mybir.dt.float32r
ALU = mybir.AluOpType
ACT = mybir.ActivationFunctionType
AX = mybir.AxisListType

P = 128
D = 1024
KD = D // P
SEQ = 1024
NB_DEC, T_DEC = 8, 8
NS = NB_DEC * T_DEC
N = SEQ + NS
QB = SEQ // P
NBLK = QB + 1
H = 4
DH = 64
W = 512
PAGE = 128
NPG = 2
PAST = NPG * PAGE
NPOOL = 20
L = 8
CH = SEQ // L
NC = CH + 1 + NB_DEC
G, GC, ST = 32, 16, 64
PR = G // 2
E, EG = 16, 4
FE = 512
KF = FE // P
NEG = -1.0e30
EPS = 1e-5
ALPHA = 2.0 ** 0.25
LAM_INIT = 0.8 - 0.6
SLOTB = 128
NSB = (2 * N) // SLOTB + E + 3
USED_PAIRS = (2 * N) // SLOTB // 2


WCOLS = KD * FE * 2 + KF * D
GATE_AT, UP_AT, DOWN_AT = 0, KD * FE, 2 * KD * FE
PIECES = ((GATE_AT, UP_AT), (UP_AT, DOWN_AT), (DOWN_AT, WCOLS))


def rows(b):
    return P if b < QB else NS


def semaphores(nc, stage):
    taken = []
    stage.callback(nc.all_engine_barrier, sem_only=True)
    stage.callback(lambda: nc.clear_and_free_semaphores(taken))

    def sem(name):
        taken.append(nc.alloc_semaphore(name))
        return taken[-1]

    return sem


class Chain:

    def __init__(self, eng, sem):
        self.eng, self.sem, self.n = eng, sem, 0

    def __call__(self, ins):
        self.n += 1
        ins.then_inc(self.sem, 1)
        self.eng.wait_ge(self.sem, self.n)


def project(nc, io, s):
    spans = [(0, 384), (384, 352), (736, 352)]
    tiles = ([("v", b) for b in range(NBLK)] + [("u", t) for t in range(L)] + [("us", 0)]
             + [("q", h, n) for h in range(H) for n in range(3)]
             + [("k", h, n) for h in range(H) for n in range(3)] + [("kn", b) for b in range(NBLK)])
    group_of = [{"v": 0, "u": 1, "us": 1, "q": 2, "k": 3, "kn": 4}[t[0]] for t in tiles]
    last_of = [max(i for i, g in enumerate(group_of) if g == k) for k in range(4)]
    w_at = (3 * W, 0, W, 2 * W)
    bank_of = [i % 4 if i < NBLK else i % 8 for i in range(len(tiles))]

    def tile_rows(i):
        kind = tiles[i]
        if kind[0] == "us":
            return NS
        return rows(kind[1]) if kind[0] in ("v", "kn") else P

    def tile_cols(i):
        return spans[tiles[i][2]][1] if tiles[i][0] in "qk" else W

    def last_in_bank(i):
        return max((j for j in range(i) if bank_of[j] == bank_of[i]), default=None)

    with ExitStack() as c:
        sb = lambda n, sh, dt=F32: c.enter_context(nc.sbuf_tensor(n, sh, dt))
        sem = semaphores(nc, c)
        place = s.aT[:, :, :].rearrange("p h n -> p (h n)")
        xn = [place[:, i * D:(i + 1) * D] for i in range(3)]
        kn = [place[:, i * W:(i + 1) * W] for i in range(8)]
        xT = [sb(f"xT{i}", [P, KD, N], F32R) for i in range(2)]
        wi = [sb(f"wi{i}", [P, KD, W], F32R) for i in range(2)]
        raw = sb("w_raw", [P, KD, W])
        lmv = sb("lmv", [P, 4, DH])
        lmp = sb("lmp", [P, 2, DH])
        lms = sb("lms", [P, 2])
        lme = sb("lme", [P, 2])
        bank = [c.enter_context(nc.psum_tensor(f"pa{i}", [P, 512], F32)) for i in range(8)]
        lm_in, lm_sum, lm_exp, lam_seq = sem("lm_in"), sem("lm_sum"), sem("lm_exp"), sem("lam_seq")
        x_in = [sem(f"x_in{i}") for i in range(3)]
        w_in = [sem(f"w_in{i}") for i in range(4)]
        xt_made, xt_high, xt_kept = sem("xt_made"), sem("xt_high"), sem("xt_kept")
        w_free, w_high, w_split = sem("w_free"), sem("w_high"), sem("w_split")
        tile_made, v_kept, a_kept = sem("tile_made"), sem("v_kept"), sem("a_kept")
        out_sent, id_in = sem("out_sent"), sem("id_in")
        kn_sent = [sem(f"kn_sent{i}") for i in range(8)]

        def kept(i):
            return (v_kept, a_kept)[i % 2], i // 2 + 1

        def split(g, eng, step):
            for k in range(KD):
                if g >= 1 and k < KD - 1:
                    eng.wait_ge(w_free, (KD - 1) * (g - 1) + k + 1)
                elif g >= 1:
                    eng.wait_ge(tile_made, last_of[g - 1] + 1)
                step(k)

        def empty(eng, i, copy):
            kind, r = tiles[i], tile_rows(i)
            src = bank[bank_of[i]][0:r, 0:tile_cols(i)]
            eng.wait_ge(tile_made, i + 1)
            if kind[0] == "u":
                dst = s.uc[:, :, kind[1], :]
                src = src.rearrange("p (g c) -> p g c", g=G)
            elif kind[0] == "us":
                dst = s.us[:, :]
            elif kind[0] == "q":
                a, n = spans[kind[2]]
                return copy(s.qT[:, kind[1], a:a + n], src, DH ** -0.5)
            elif kind[0] == "k":
                a, n = spans[kind[2]]
                dst = s.kT[:, kind[1], a:a + n]
            elif kind[0] == "v":
                dst = s.v[0:r, kind[1], :]
            else:
                if kind[1] >= 8:
                    eng.wait_ge(kn_sent[kind[1] - 8], 16)
                dst = kn[kind[1] % 8][0:r, :]
            return copy(dst, src, 1.0)

        with nc.Block() as block:
            @block.sync
            def _(sp):
                sp.dma_start(s.ident[:, :], io["c_ident"]).then_inc(id_in, 16)
                for b in range(NBLK):
                    if b == 3:
                        for n, name in enumerate(("lambda_q1", "lambda_k1", "lambda_q2", "lambda_k2")):
                            sp.dma_start(lmv[:, n, :], io[name].to_broadcast([P, DH])).then_inc(lm_in, 16)
                    if b >= 3:
                        sp.wait_ge(xt_made, b - 2)
                    src = io["x_prompt"][0, b * P:(b + 1) * P, :] if b < QB else \
                        io["x_sample"].rearrange("b t d -> (b t) d")
                    sp.dma_start(xn[b % 3][0:rows(b), :], src).then_inc(x_in[b % 3], 16)
                wv = io["w_in"][0].rearrange("(p k) n -> p k n", k=KD)

                def load_weights(g):
                    sp.wait_ge(w_split, KD * g)
                    sp.dma_start(raw[:, :, :], wv[:, :, w_at[g]:w_at[g] + W]).then_inc(w_in[g], 16)

                load_weights(1)
                vo = io["new_v_prompt"][0, 0].rearrange("t h d -> t (h d)")
                ko = io["new_k_prompt"][0, 0].rearrange("t h d -> t (h d)")
                vs = io["new_v_sample"][0].rearrange("b t h d -> (b t) (h d)")
                ks = io["new_k_sample"][0].rearrange("b t h d -> (b t) (h d)")
                for i, kind in enumerate(tiles):
                    if kind[0] in ("v", "kn"):
                        b, r = kind[1], tile_rows(i)
                        prompt, sample = (vo, vs) if kind[0] == "v" else (ko, ks)
                        dst = prompt[b * P:(b + 1) * P, :] if b < QB else sample
                        src = s.v[0:r, b, :] if kind[0] == "v" else kn[b % 8][0:r, :]
                        if kind[0] == "v" and b == NBLK - 1:
                            load_weights(2)
                        if kind[0] == "kn" and b == 0:
                            load_weights(3)
                        sp.wait_ge(*kept(i))
                        if kind[0] == "v":
                            sp.dma_start(dst, src).then_inc(out_sent, 16)
                        else:
                            sp.dma_start(dst, src).then_inc(kn_sent[b % 8], 16)
                sp.wait_ge(out_sent, 16 * NBLK)
                for i in range(8):
                    sp.wait_ge(kn_sent[i], 32 if i + 8 < NBLK else 16)

            @block.tensor
            def _(pe):
                pe.wait_ge(id_in, 16)

                def turn(b):
                    pe.wait_ge(x_in[b % 3], 16 * (b // 3 + 1))
                    if b >= 2:
                        pe.wait_ge(xt_kept, b - 1)
                    r = rows(b)
                    xv = xn[b % 3][0:r, :].rearrange("t (p k) -> t k p", k=KD)
                    for k in range(KD):
                        last = pe.transpose(bank[4 + 2 * (b % 2) + k // 4][:, (k % 4) * P:(k % 4) * P + r],
                                            xv[:, k, :], s.ident[0:r, 0:r])
                    last.then_inc(xt_made, 1)

                turn(0)
                for i, kind in enumerate(tiles):
                    if i + 1 < NBLK:
                        turn(i + 1)
                    pe.wait_ge(xt_kept, min(i + 1, NBLK))
                    if last_in_bank(i) is not None:
                        pe.wait_ge(*kept(last_in_bank(i)))
                    out = bank[bank_of[i]][0:tile_rows(i), 0:tile_cols(i)]
                    if kind[0] == "kn":
                        if kind[1] == 0:
                            last_k = max(j for j, t in enumerate(tiles) if t[0] == "k")
                            pe.wait_ge(*kept(last_k))
                            pe.wait_ge(*kept(last_k - 1))
                        a, r = kind[1] * P, tile_rows(i)
                        for h in range(H):
                            last = pe.transpose(bank[bank_of[i]][0:r, h * P:(h + 1) * P],
                                                s.kT[:, h, a:a + r], s.ident[:, :])
                        last.then_inc(tile_made, 1)
                        continue
                    g = group_of[i]
                    for k in range(KD):
                        if i == 0 or group_of[i - 1] != g:
                            pe.wait_ge(w_split, KD * g + k + 1)

                        def ops(a, b):
                            if kind[0] == "u":
                                return xT[a][:, k, kind[1]:SEQ:L], wi[b][:, k, :]
                            if kind[0] == "us":
                                return xT[a][:, k, SEQ:N], wi[b][:, k, :]
                            if kind[0] == "v":
                                return xT[a][:, k, kind[1] * P:kind[1] * P + rows(kind[1])], wi[b][:, k, :]
                            at, n = spans[kind[2]]
                            return wi[a][:, k, kind[1] * P:(kind[1] + 1) * P], xT[b][:, k, at:at + n]

                        pe.matmul(out, *ops(0, 0), start=(k == 0), stop=False)
                        pe.matmul(out, *ops(0, 1), start=False, stop=False)
                        last = pe.matmul(out, *ops(1, 0), start=False, stop=(k == KD - 1))
                        if i == last_of[g] and k < KD - 1:
                            last.then_inc(w_free, 1)
                    last.then_inc(tile_made, 1)

            @block.vector
            def _(dve):
                def low_x(b):
                    dve.wait_ge(xt_high, b + 1)
                    r = rows(b)
                    for half in range(2):
                        src = bank[4 + 2 * (b % 2) + half][:, :].rearrange("p (k t) -> p k t", k=4)[:, :, 0:r]
                        hi, lo = (x[:, 4 * half:4 * half + 4, b * P:b * P + r] for x in xT)
                        last = nc.vector.tensor_tensor(lo, src, hi.bitcast(F32), ALU.subtract)
                    last.then_inc(xt_kept, 1)

                def low_w(g):
                    for k in range(KD):
                        dve.wait_ge(w_high, KD * g + k + 1)
                        nc.vector.tensor_tensor(wi[1][:, k, :], raw[:, k, :], wi[0][:, k, :].bitcast(F32),
                                                ALU.subtract).then_inc(w_split, 1)

                def minus_lambda():
                    dve.wait_ge(lm_in, 64)
                    for j in range(2):
                        last = nc.vector.tensor_tensor(lmp[:, j, :], lmv[:, 2 * j, :], lmv[:, 2 * j + 1, :], ALU.mult)
                    last.then_inc(lam_seq, 1)
                    dve.wait_ge(lam_seq, 1)
                    nc.vector.tensor_reduce(lms[:, :], lmp[:, :, :], AX.X, ALU.add).then_inc(lm_sum, 1)
                    dve.wait_ge(lm_exp, 1)
                    nc.vector.tensor_tensor(s.nlam[:, :], lme[:, 1:2], lme[:, 0:1], ALU.subtract).then_inc(lam_seq, 1)
                    dve.wait_ge(lam_seq, 2)
                    nc.vector.tensor_scalar(s.nlam[:, :], s.nlam[:, :], LAM_INIT, None, ALU.subtract).then_inc(lam_seq, 1)
                    dve.wait_ge(lam_seq, 3)

                low_x(0)
                low_w(0)
                for i in range(len(tiles)):
                    if i + 1 < NBLK:
                        low_x(i + 1)
                    if i == NBLK:
                        minus_lambda()
                    if i in last_of[0:3]:
                        low_w(last_of.index(i) + 1)
                    if i % 2 == 0:
                        empty(dve, i, lambda o, a, m: nc.vector.tensor_scalar(o, a, m, None, ALU.mult)) \
                            .then_inc(v_kept, 1)

            @block.scalar
            def _(act):
                wv = io["w_in"][0].rearrange("(p k) n -> p k n", k=KD)
                act.dma_start(raw[:, :, :], wv[:, :, w_at[0]:w_at[0] + W]).then_inc(w_in[0], 16)

                def high_x(b):
                    act.wait_ge(xt_made, b + 1)
                    r = rows(b)
                    for half in range(2):
                        src = bank[4 + 2 * (b % 2) + half][:, :].rearrange("p (k t) -> p k t", k=4)[:, :, 0:r]
                        last = nc.scalar.activation(xT[0][:, 4 * half:4 * half + 4, b * P:b * P + r], src, ACT.Copy)
                    last.then_inc(xt_high, 1)

                def high_w(g):
                    act.wait_ge(w_in[g], 16)
                    split(g, act, lambda k: nc.scalar.activation(wi[0][:, k, :], raw[:, k, :], ACT.Copy)
                          .then_inc(w_high, 1))

                high_x(0)
                high_w(0)
                for i in range(len(tiles)):
                    if i + 1 < NBLK:
                        high_x(i + 1)
                    if i == NBLK:
                        act.wait_ge(lm_sum, 1)
                        nc.scalar.activation(lme[:, :], lms[:, :], ACT.Exp).then_inc(lm_exp, 1)
                    if i in last_of[0:3]:
                        high_w(last_of.index(i) + 1)
                    if i % 2:
                        empty(act, i, lambda o, a, m: nc.scalar.activation(o, a, ACT.Copy, scale=m)) \
                            .then_inc(a_kept, 1)


def attend(nc, io, s):
    steps = [(h, i) for h in range(H) for i in range(QB)]
    with ExitStack() as c:
        sb = lambda n, sh, dt=F32: c.enter_context(nc.sbuf_tensor(n, sh, dt))
        sem = semaphores(nc, c)
        bias = sb("bias", [P, H, SEQ])
        S = [[sb(f"S{k}{j}", [P, SEQ]) for j in range(2)] for k in range(2)]
        Ex = [[sb(f"Ex{k}{j}", [P, SEQ]) for j in range(2)] for k in range(2)]
        w = [sb(f"w{k}", [P, SEQ]) for k in range(2)]
        wT = [sb(f"wT{k}", [P, SEQ]) for k in range(2)]
        mx = sb("mx", [P, len(steps), 2])
        nm = sb("nm", [P, len(steps), 2])
        l = sb("l", [P, len(steps), 2])
        rl = sb("rl", [P, len(steps), 2])
        cf = sb("cf", [P, len(steps)])
        sq = sb("sq", [P, P])
        psS = [c.enter_context(nc.psum_tensor(f"psS{k}", [P, SEQ], F32)) for k in range(2)]
        psT = c.enter_context(nc.psum_tensor("psT", [P, SEQ], F32))
        psO = [c.enter_context(nc.psum_tensor(f"psO{k}", [P, 512], F32)) for k in range(2)]
        bias_in = [sem(f"bias_in{h}") for h in range(H)]
        tab_in, k_in = sem("tab_in"), sem("kc_in")
        scored, biased, negated, exped = sem("scored"), sem("biased"), sem("negated"), sem("exped")
        mixed, turned, turned_kept, summed, out_kept, squared, r_seq = (sem(n) for n in (
            "mixed", "turned", "turned_kept", "summed", "out_kept", "squared", "r_seq"))

        with nc.Block() as block:
            @block.sync
            def _(sp):
                for h in range(H):
                    sp.dma_start(bias[:, h, :], io["c_bias"][:, h, :]).then_inc(bias_in[h], 16)
                sp.dma_start(s.ptab[:, :], io["page_table"].rearrange("(o b) n -> o (b n)", o=1)).then_inc(tab_in, 16)
                sp.wait_ge(tab_in, 16)
                load_pages(sp, io, s, "cache_k", s.kc, k_in)
                sp.wait_ge(k_in, 16 * NB_DEC * NPG)

            def scores(pe, n):
                h, i = steps[n]
                nk = (i + 1) * P
                for j in range(2):
                    if n >= 1:
                        pe.wait_ge(biased, 2 * (n - 1) + j + 1)
                    for a in range(0, nk, 512):
                        m = min(512, nk - a)
                        last = pe.matmul(psS[j][:, a:a + m], s.qT[DH * j:DH * j + DH, h, i * P:(i + 1) * P],
                                         s.kT[DH * j:DH * j + DH, h, a:a + m], start=True, stop=True)
                    last.then_inc(scored, 1)

            def turn(pe, n):
                h, i = steps[n]
                pe.wait_ge(mixed, n + 1)
                if n >= 1:
                    pe.wait_ge(turned_kept, n)
                for j in range(i + 1):
                    last = pe.transpose(psT[:, j * P:(j + 1) * P], w[n % 2][:, j * P:(j + 1) * P], s.ident[:, :])
                last.then_inc(turned, 1)

            def values(pe, n):
                h, i = steps[n]
                pe.wait_ge(turned_kept, n + 1)
                if n >= 2:
                    pe.wait_ge(out_kept, n - 1)
                for j in range(i + 1):
                    last = pe.matmul(psO[n % 2][:, 0:P], wT[n % 2][:, j * P:(j + 1) * P],
                                     s.v[:, j, h * P:(h + 1) * P], start=(j == 0), stop=(j == i))
                last.then_inc(summed, 1)

            @block.tensor
            def _(pe):
                scores(pe, 0)
                scores(pe, 1)
                for n in range(len(steps)):
                    if n + 2 < len(steps):
                        scores(pe, n + 2)
                    turn(pe, n)
                    if n >= 1:
                        values(pe, n - 1)
                values(pe, len(steps) - 1)

            @block.vector
            def _(dve):
                def add_bias(n):
                    h, i = steps[n]
                    nk = (i + 1) * P
                    if i == 0:
                        dve.wait_ge(bias_in[h], 16)
                    for j in range(2):
                        dve.wait_ge(scored, 2 * n + j + 1)
                        if n >= 2:
                            dve.wait_ge(exped, 2 * (n - 2) + j + 1)
                        nc.vector.tensor_tensor_reduce(
                            S[n % 2][j][:, 0:nk], psS[j][:, 0:nk], bias[:, h, (QB - 1 - i) * P:], 1.0, NEG,
                            ALU.add, ALU.max, mx[:, n, j:j + 1]).then_inc(biased, 1)
                    dve.wait_ge(biased, 2 * n + 2)
                    nc.vector.tensor_scalar(nm[:, n, :], mx[:, n, :], -1.0, None, ALU.mult).then_inc(negated, 1)

                def mix(n):
                    h, i = steps[n]
                    nk = (i + 1) * P
                    dve.wait_ge(exped, 2 * n + 2)
                    nc.vector.reciprocal(rl[:, n, :], l[:, n, :]).then_inc(r_seq, 1)
                    dve.wait_ge(r_seq, 2 * n + 1)
                    nc.vector.scalar_tensor_tensor(cf[:, n:n + 1], rl[:, n, 1:2], s.nlam[:, 0:1], l[:, n, 0:1],
                                                   ALU.mult, ALU.mult).then_inc(r_seq, 1)
                    dve.wait_ge(r_seq, 2 * n + 2)
                    if n >= 2:
                        dve.wait_ge(turned, n - 1)
                    nc.vector.scalar_tensor_tensor(w[n % 2][:, 0:nk], Ex[n % 2][1][:, 0:nk], cf[:, n:n + 1],
                                                   Ex[n % 2][0][:, 0:nk], ALU.mult, ALU.add).then_inc(mixed, 1)

                def keep_out(n):
                    h, i = steps[n]
                    dve.wait_ge(summed, n + 1)
                    nc.vector.tensor_scalar(s.o[:, i, h * P:(h + 1) * P], psO[n % 2][:, 0:P], rl[:, n, 0:1], None,
                                            ALU.mult).then_inc(out_kept, 1)

                add_bias(0)
                add_bias(1)
                for n in range(len(steps)):
                    mix(n)
                    if n + 2 < len(steps):
                        add_bias(n + 2)
                    if n >= 2:
                        keep_out(n - 2)
                keep_out(len(steps) - 2)
                keep_out(len(steps) - 1)

            def square(act, n):
                h, i = steps[n]
                act.wait_ge(out_kept, n + 1)
                if n >= 1:
                    act.wait_ge(squared, n)
                nc.scalar.activation(sq[:, :], s.o[:, i, h * P:(h + 1) * P], ACT.Square,
                                     accum_out=s.ss[:, i, h:h + 1]).then_inc(squared, 1)

            @block.scalar
            def _(act):
                def exps(n):
                    h, i = steps[n]
                    nk = (i + 1) * P
                    act.wait_ge(negated, n + 1)
                    if n >= 2:
                        act.wait_ge(mixed, n - 1)
                    for j in range(2):
                        nc.scalar.activation(Ex[n % 2][j][:, 0:nk], S[n % 2][j][:, 0:nk], ACT.Exp,
                                             bias=nm[:, n, j:j + 1], accum_out=l[:, n, j:j + 1]).then_inc(exped, 1)

                def keep_turned(n):
                    h, i = steps[n]
                    act.wait_ge(turned, n + 1)
                    if n >= 2:
                        act.wait_ge(summed, n - 1)
                    nc.scalar.activation(wT[n % 2][:, 0:(i + 1) * P], psT[:, 0:(i + 1) * P], ACT.Copy) \
                        .then_inc(turned_kept, 1)

                exps(0)
                exps(1)
                for n in range(len(steps)):
                    keep_turned(n)
                    if n + 2 < len(steps):
                        exps(n + 2)
                    if n >= 2:
                        square(act, n - 2)
                square(act, len(steps) - 2)
                square(act, len(steps) - 1)


def load_pages(sp, io, s, cache, dst, done):
    for n in range(NB_DEC * NPG):
        page = sp.value_load(s.ptab[0:1, n:n + 1], min_val=0, max_val=NPOOL - 1)
        src = io[cache][0].rearrange("n p h d -> n p (h d)")[bass.ds(page, 1), :, :]
        sp.dma_start(dst[:, n, :], src.rearrange("o p c -> p (o c)")).then_inc(done, 16)


def sample(nc, io, s):
    KC = PAST + NS
    with ExitStack() as c:
        sb = lambda n, sh, dt=F32: c.enter_context(nc.sbuf_tensor(n, sh, dt))
        sem = semaphores(nc, c)
        kc = s.kc
        vc = sb("vc", [P, NB_DEC * NPG, W])
        kcT = sb("kcT", [P, NB_DEC * NPG * P])
        bs = sb("bs", [P, H, KC])
        two = sb("two", [P, NS])
        sel = sb("sel", [P, 2])
        sg = sb("sg", [P, 1])
        qf = sb("qf", [P, H, P])
        qm = sb("qm", [P, H, NB_DEC, P])
        Ex = [sb(f"sE{k}", [P, KC]) for k in range(2)]
        PT = [sb(f"sPT{k}", [P, 3 * NS]) for k in range(2)]
        oT = [sb(f"soT{k}", [P, NS]) for k in range(2)]
        st = sb("sst", [P, H, 4])
        sq = kcT[0:NS, 0:P]
        psK = [c.enter_context(nc.psum_tensor(f"psK{k}", [P, 512], F32)) for k in range(4)]
        psS = [c.enter_context(nc.psum_tensor(f"spS{k}", [P, 512], F32)) for k in range(2)]
        psP = c.enter_context(nc.psum_tensor("spP", [P, 512], F32))
        psO = c.enter_context(nc.psum_tensor("spO", [P, 512], F32))
        psN = [psS[(h + 1) % 2][0:NS, 0:P] for h in range(H)]
        names = ("consts_in v_in zeroed q_ready sg_ready k_turned k_kept scored biased negated exped "
                 "scaled recip pairs pairs_kept summed o_kept o_turned o_out squared").split()
        m = {n: sem("s_" + n) for n in names}

        with nc.Block() as block:
            @block.sync
            def _(sp):
                sp.dma_start(two[:, :], io["c_two"]).then_inc(m["consts_in"], 16)
                sp.dma_start(sel[:, :], io["c_sel"]).then_inc(m["consts_in"], 16)
                sp.dma_start(bs[:, :, :], io["c_bias_s"]).then_inc(m["consts_in"], 16)
                load_pages(sp, io, s, "cache_v", vc, m["v_in"])

            @block.gpsimd
            def _(pool):
                nc.gpsimd.memset(qf[:, :, :], 0.0).then_inc(m["zeroed"], 1)
                nc.gpsimd.memset(qm[:, :, :, :], 0.0).then_inc(m["zeroed"], 1)

            @block.tensor
            def _(pe):
                def keys(h):
                    for g in range(4):
                        if h >= 1:
                            pe.wait_ge(m["k_kept"], 4 * (h - 1) + g + 1)
                        for j in range(4):
                            n = 4 * g + j
                            last = pe.transpose(psK[g][:, j * P:(j + 1) * P], kc[:, n, h * P:(h + 1) * P], s.ident[:, :])
                        last.then_inc(m["k_turned"], 1)

                def scores(h):
                    pe.wait_ge(m["k_kept"], 4 * (h + 1))
                    if h == 0:
                        pe.wait_ge(m["q_ready"], 2 * H + 4 * H)
                    if h >= 2:
                        pe.wait_ge(m["biased"], h - 1)
                    if h >= 3:
                        pe.wait_ge(m["o_out"], h - 2)
                    for b in range(NB_DEC):
                        pe.matmul(psS[h % 2][:, 0:PAST], qm[:, h, b, :], kcT[:, b * PAST:(b + 1) * PAST],
                                  start=(b == 0), stop=(b == NB_DEC - 1))
                    pe.matmul(psS[h % 2][:, PAST:KC], qf[:, h, :], s.kT[:, h, SEQ:N], start=True, stop=True) \
                        .then_inc(m["scored"], 1)

                def pairs(h):
                    pe.wait_ge(m["scaled"], h + 1)
                    if h == 0:
                        pe.wait_ge(m["consts_in"], 48)
                    else:
                        pe.wait_ge(m["pairs_kept"], h)
                    for j in range(3):
                        n = P if j < 2 else NS
                        last = pe.matmul(psP[0:n, j * NS:(j + 1) * NS], Ex[h % 2][:, j * P:j * P + n], two[:, :],
                                         start=True, stop=True)
                    last.then_inc(m["pairs"], 1)

                def values(h):
                    pe.wait_ge(m["pairs_kept"], h + 1)
                    if h == 0:
                        pe.wait_ge(m["v_in"], 16 * NB_DEC * NPG)
                    else:
                        pe.wait_ge(m["o_kept"], h)
                    pe.matmul(psO[:, 0:NS], s.v[0:NS, QB, h * P:(h + 1) * P], PT[h % 2][0:NS, 2 * NS:3 * NS],
                              start=True, stop=False, skip_group_check=True)
                    for b in range(NB_DEC):
                        for j in range(NPG):
                            last = pe.matmul(psO[:, b * T_DEC:(b + 1) * T_DEC], vc[:, NPG * b + j, h * P:(h + 1) * P],
                                             PT[h % 2][:, j * NS + b * T_DEC:j * NS + (b + 1) * T_DEC],
                                             start=False, stop=(b == NB_DEC - 1 and j == NPG - 1), skip_group_check=True)
                    last.then_inc(m["summed"], 1)

                def turn_o(h):
                    pe.wait_ge(m["o_kept"], h + 1)
                    pe.wait_ge(m["biased"], min(h + 2, H))
                    pe.transpose(psN[h], oT[h % 2][:, :], s.ident[:, :]).then_inc(m["o_turned"], 1)

                keys(0)
                scores(0)
                keys(1)
                for h in range(H):
                    if h + 1 < H:
                        scores(h + 1)
                    if h + 2 < H:
                        keys(h + 2)
                    pairs(h)
                    if h >= 1:
                        turn_o(h - 1)
                    values(h)
                turn_o(H - 1)

            @block.vector
            def _(dve):
                dve.wait_ge(m["zeroed"], 2)
                for h in range(H):
                    for j in range(2):
                        r = slice(DH * j, DH * j + DH)
                        nc.vector.tensor_copy(qf[r, h, NS * j:NS * j + NS], s.qT[r, h, SEQ:N]).then_inc(m["q_ready"], 1)
                dve.wait_ge(m["consts_in"], 48)
                nc.vector.scalar_tensor_tensor(sg[:, :], sel[:, 1:2], s.nlam[:, 0:1], sel[:, 0:1],
                                               ALU.mult, ALU.add).then_inc(m["sg_ready"], 1)

                def add_bias(h):
                    dve.wait_ge(m["scored"], h + 1)
                    if h >= 2:
                        dve.wait_ge(m["pairs"], h - 1)
                    nc.vector.tensor_tensor_reduce(Ex[h % 2][:, :], psS[h % 2][:, 0:KC], bs[:, h, :], 1.0, NEG, ALU.add,
                                                   ALU.max, st[:, h, 0:1]).then_inc(m["biased"], 1)
                    dve.wait_ge(m["biased"], h + 1)
                    nc.vector.tensor_scalar(st[:, h, 1:2], st[:, h, 0:1], -1.0, None, ALU.mult).then_inc(m["negated"], 1)

                def scale(h):
                    dve.wait_ge(m["exped"], h + 1)
                    nc.vector.reciprocal(st[:, h, 3:4], st[:, h, 2:3]).then_inc(m["recip"], 1)
                    dve.wait_ge(m["recip"], h + 1)
                    dve.wait_ge(m["sg_ready"], 1)
                    nc.vector.tensor_scalar(Ex[h % 2][:, :], Ex[h % 2][:, :], st[:, h, 3:4], sg[:, 0:1], ALU.mult,
                                            ALU.mult).then_inc(m["scaled"], 1)

                def keep_pairs(h):
                    dve.wait_ge(m["pairs"], h + 1)
                    if h >= 2:
                        dve.wait_ge(m["summed"], h - 1)
                    nc.vector.tensor_copy(PT[h % 2][:, 0:2 * NS], psP[:, 0:2 * NS])
                    nc.vector.tensor_copy(PT[h % 2][0:NS, 2 * NS:3 * NS], psP[0:NS, 2 * NS:3 * NS]) \
                        .then_inc(m["pairs_kept"], 1)

                def keep_o(h):
                    dve.wait_ge(m["summed"], h + 1)
                    if h >= 2:
                        dve.wait_ge(m["o_turned"], h - 1)
                    nc.vector.tensor_copy(oT[h % 2][:, :], psO[:, 0:NS]).then_inc(m["o_kept"], 1)

                def put_o(h):
                    dve.wait_ge(m["o_turned"], h + 1)
                    nc.vector.tensor_copy(s.o[0:NS, QB, h * P:(h + 1) * P], psN[h]).then_inc(m["o_out"], 1)

                add_bias(0)
                scale(0)
                for h in range(H):
                    if h + 1 < H:
                        add_bias(h + 1)
                    keep_pairs(h)
                    if h + 1 < H:
                        scale(h + 1)
                    if h >= 1:
                        put_o(h - 1)
                    keep_o(h)
                put_o(H - 1)

            @block.scalar
            def _(act):
                act.wait_ge(m["zeroed"], 2)
                for h in range(H):
                    for j in range(2):
                        r = slice(DH * j, DH * j + DH)
                        for bh in range(2):
                            at = NS * j + T_DEC * 4 * bh
                            dst = own_columns(qm, r, h, 4 * bh, at)
                            nc.scalar.activation(dst, s.qT[r, h, SEQ + 32 * bh:SEQ + 32 * bh + 32]
                                                 .rearrange("p (b t) -> p b t", t=T_DEC), ACT.Copy).then_inc(m["q_ready"], 1)

                def keep_keys(h):
                    for g in range(4):
                        act.wait_ge(m["k_turned"], 4 * h + g + 1)
                        if h >= 1:
                            act.wait_ge(m["scored"], h)
                        nc.scalar.activation(kcT[:, g * 512:(g + 1) * 512], psK[g][:, :], ACT.Copy) \
                            .then_inc(m["k_kept"], 1)

                def exp(h):
                    act.wait_ge(m["negated"], h + 1)
                    nc.scalar.activation(Ex[h % 2][:, :], Ex[h % 2][:, :], ACT.Exp, bias=st[:, h, 1:2],
                                         accum_out=st[:, h, 2:3]).then_inc(m["exped"], 1)

                keep_keys(0)
                exp(0)
                keep_keys(1)
                for h in range(1, H):
                    exp(h)
                    if h + 1 < H:
                        keep_keys(h + 1)
                for h in range(H):
                    act.wait_ge(m["o_out"], h + 1)
                    if h >= 1:
                        act.wait_ge(m["squared"], h)
                    nc.scalar.activation(sq, s.o[0:NS, QB, h * P:(h + 1) * P], ACT.Square,
                                         accum_out=s.ss[0:NS, QB, h:h + 1]).then_inc(m["squared"], 1)


def own_columns(qm, r, h, b0, at):
    flat = qm[r, h, :, :].rearrange("p b c -> p (b c)")
    lo = b0 * P + at
    need = 4 * (P + T_DEC)
    if lo + need <= NB_DEC * P:
        return flat[:, lo:lo + need].rearrange("p (b c) -> p b c", c=P + T_DEC)[:, :, 0:T_DEC]
    hi = NB_DEC * P - need
    return flat[:, hi:].rearrange("p (b c) -> p b c", c=P + T_DEC)[:, :, lo - hi:lo - hi + T_DEC]


def head_norm(nc, io, s):
    with ExitStack() as c:
        sb = lambda n, sh, dt=F32: c.enter_context(nc.sbuf_tensor(n, sh, dt))
        sem = semaphores(nc, c)
        rs = sb("rs", [P, NBLK * H])
        gcol = sb("gcol", [P, 1])
        an = [sb(f"an{k}", [P, W]) for k in range(2)]
        ps = [c.enter_context(nc.psum_tensor(f"psA{k}", [P, 512], F32)) for k in range(2)]
        g_in, seq, rooted, scaled, turned, kept = (sem(n) for n in "hn_g hn_seq hn_root hn_scaled hn_turned hn_kept".split())

        with nc.Block() as block:
            @block.sync
            def _(sp):
                sp.dma_start(gcol[:, :], io["subln_g"].rearrange("o v -> v o")).then_inc(g_in, 16)

            @block.vector
            def _(dve):
                ch = Chain(dve, seq)
                ssv = s.ss[:, :, :].rearrange("p b h -> p (b h)")
                ch(nc.vector.memset(s.ss[NS:P, QB, :], 1.0))
                ch(nc.vector.tensor_scalar(rs[:, :], ssv, 1.0 / P, EPS, ALU.mult, ALU.add))
                dve.wait_ge(g_in, 16)
                ch(nc.vector.tensor_scalar(gcol[:, :], gcol[:, :], 1.0 - LAM_INIT, None, ALU.mult))
                dve.wait_ge(rooted, 1)
                ch(nc.vector.reciprocal(rs[:, :], rs[:, :]))
                for b in range(NBLK):
                    r = rows(b)
                    if b >= 2:
                        dve.wait_ge(turned, b - 1)
                    for h in range(H):
                        last = nc.vector.tensor_scalar(an[b % 2][0:r, h * P:(h + 1) * P], s.o[0:r, b, h * P:(h + 1) * P],
                                                       rs[0:r, b * H + h:b * H + h + 1], None, ALU.mult)
                    last.then_inc(scaled, 1)

            @block.tensor
            def _(pe):
                for b in range(NBLK):
                    r = rows(b)
                    pe.wait_ge(scaled, b + 1)
                    if b >= 2:
                        pe.wait_ge(kept, b - 1)
                    for h in range(H):
                        last = pe.transpose(ps[b % 2][:, h * P:h * P + r], an[b % 2][0:r, h * P:(h + 1) * P],
                                            s.ident[0:r, 0:r])
                    last.then_inc(turned, 1)

            @block.scalar
            def _(act):
                act.wait_ge(seq, 3)
                nc.scalar.activation(rs[:, :], rs[:, :], ACT.Sqrt).then_inc(rooted, 1)
                for b in range(NBLK):
                    r = rows(b)
                    act.wait_ge(turned, b + 1)
                    nc.scalar.activation(s.aT[:, :, b * P:b * P + r],
                                         ps[b % 2][:, :].rearrange("p (h t) -> p h t", h=H)[:, :, 0:r],
                                         ACT.Copy, scale=gcol[:, 0:1]).then_inc(kept, 1)


MAGIC = 1.5 * 2.0 ** 23
TWO_PI = 6.283185307179586
PI_HI, PI_MID = 6.28125, 0.0019350051879882812
PI_LO = TWO_PI - PI_HI - PI_MID


def wide(ap, n):
    return ap.unsqueeze(2).to_broadcast([ap.shape[0], ap.shape[1], n])


def mid(ap, n):
    return ap.unsqueeze(1).to_broadcast([ap.shape[0], n, ap.shape[1]])


def ssm_tables(nc, io, s):
    with ExitStack() as c:
        sb = lambda n, sh, dt=F32: c.enter_context(nc.sbuf_tensor(n, sh, dt))
        sem = semaphores(nc, c)
        par = sb("par", [P, 3, PR])
        th = sb("th", [P, 2, PR])
        kk = sb("kk", [P, 2, PR])
        rr = sb("rr", [P, 2, PR])
        ra = sb("ra", [P, 2, PR])
        cs = sb("cs", [P, 2, 2, PR])
        mg = sb("mg", [P, 2, PR])
        dt_ = sb("dt_", [P, PR])
        ld = sb("ld", [P, PR])
        ar, ai, nr, den, t1, t2, cr, ci = (sb("z" + n, [P, PR]) for n in "ar ai nr den t1 t2 cr ci".split())
        half_pi = sb("half_pi", [P, 1])
        bre, bim, cre, cim = (sb("b_" + n, [P, PR, GC]) for n in "bre bim cre cim".split())
        u1, u2, u3, u4 = (sb(f"u{n}", [P, PR, GC]) for n in range(4))
        g1, g2, g3, g4 = (sb(f"g{n}", [P, PR, GC]) for n in range(4))
        cbr = sb("cbr", [P, PR, 2 * GC])
        cbi = sb("cbi", [P, PR, 2 * GC])
        pr, pi = (s.work[n][:, :, :].rearrange("p q (b c) -> p q b c", c=GC) for n in (2, 3))
        kd = sb("kd", [P, W])
        kcol = sb("kcol", [P, W])
        bk = [c.enter_context(nc.psum_tensor(f"pt{k}", [P, 512], F32)) for k in range(8)]
        (p_in, e_in, c_in, seq, dts, angles, exps, absd, sines, zeroed, b_ready, cseq, t_made, t_kept,
         v_made, v_kept, cb_in, a_ready, us_in, pad_zeroed, u_made, u_kept, kd_in, k_made, k_kept, t_zeroed) = (
            sem("st_" + n) for n in (
            "p e c seq dts angles exps absd sines zeroed b_ready cseq t_made t_kept v_made v_kept cb_in a_ready "
            "us pad u_made u_kept kd k_made k_kept t_zeroed").split())

        with nc.Block() as block:
            @block.sync
            def _(sp):
                sp.dma_start(par[:, :, :], io["l_par"]).then_inc(p_in, 16)
                for t in range(T_DEC):
                    sp.dma_start(s.us8[:, :, t, :], s.us[t:NS:T_DEC, :].rearrange("b (g c) -> b g c", g=G)) \
                        .then_inc(us_in, 16)
                sp.dma_start(bre[:, :, :], io["l_bre"]).then_inc(e_in, 16)
                sp.dma_start(bim[:, :, :], io["l_bim"]).then_inc(e_in, 16)
                sp.dma_start(cre[:, :, :], io["l_cre"]).then_inc(c_in, 16)
                sp.dma_start(cim[:, :, :], io["l_cim"]).then_inc(c_in, 16)
                sp.dma_start(cbr[:, :, :], io["l_cbr"]).then_inc(cb_in, 16)
                sp.dma_start(cbi[:, :, :], io["l_cbi"]).then_inc(cb_in, 16)
                sp.dma_start(kd[:, :], io["l_d"]).then_inc(kd_in, 16)

            @block.scalar
            def _(act):
                act.wait_ge(p_in, 16)
                nc.scalar.activation(dt_[:, :], par[:, 2, :], ACT.Exp).then_inc(dts, 1)
                act.wait_ge(angles, 1)
                nc.scalar.activation(mg[:, 0, :], ld[:, :], ACT.Exp).then_inc(exps, 1)
                nc.scalar.activation(mg[:, 1, :], ld[:, :], ACT.Exp, scale=float(L)).then_inc(exps, 1)
                act.wait_ge(absd, 1)
                nc.scalar.activation(cs[:, 1, :, :], rr[:, :, :], ACT.Sin).then_inc(sines, 1)
                nc.scalar.activation(cs[:, 0, :, :], ra[:, :, :], ACT.Sin, scale=-1.0, bias=half_pi[:, 0:1]) \
                    .then_inc(sines, 1)
                for g in range(0, G, 4):
                    act.wait_ge(u_made, g // 4 + 1)
                    nc.scalar.activation(s.U[:, g:g + 4, 0:CH], bk[(g // 4) % 4][:, :].rearrange("p (g n) -> p g n", g=4),
                                         ACT.Copy).then_inc(u_kept, 1)
                act.wait_ge(u_made, G // 4 + 1)
                nc.scalar.activation(s.U[:, :, CH + 1:], bk[4][:, 0:G * NB_DEC].rearrange("p (g n) -> p g n", g=G),
                                     ACT.Copy).then_inc(u_kept, 1)
                for q in range(0, PR, 2):
                    act.wait_ge(v_made, q // 2 + 1)
                    src = bk[6 + (q // 2) % 2][:, :].rearrange("p (j k n) -> p j k n", j=2, k=2)
                    nc.scalar.activation(s.VTr[:, q:q + 2, :], src[:, :, 0, :], ACT.Copy)
                    nc.scalar.activation(s.VTi[:, q:q + 2, :], src[:, :, 1, :], ACT.Copy).then_inc(v_kept, 1)
                act.wait_ge(t_zeroed, 1)
                for t in range(L):
                    n = (t + 1) * GC
                    act.wait_ge(t_made, t + 1)
                    nc.scalar.activation(s.T[0:n, :, t * GC:n], bk[t % 4][0:n, :].rearrange("p (g c) -> p g c", g=G),
                                         ACT.Copy).then_inc(t_kept, 1)

            @block.gpsimd
            def _(pool):
                nc.gpsimd.memset(half_pi[:, :], TWO_PI / 4).then_inc(zeroed, 1)
                nc.gpsimd.memset(s.U[:, :, CH:CH + 1], 0.0).then_inc(pad_zeroed, 1)
                ch = Chain(pool, cseq)
                tt = nc.gpsimd.tensor_tensor
                pool.wait_ge(cb_in, 32)
                ch(nc.gpsimd.tensor_scalar(cbi[:, :, :], cbi[:, :, :], -1.0, None, ALU.mult))
                pool.wait_ge(c_in, 32)
                ch(nc.gpsimd.tensor_scalar(cim[:, :, :], cim[:, :, :], -1.0, None, ALU.mult))
                pool.wait_ge(a_ready, 1)
                for t in range(L):
                    re0 = cre[:, :, :] if t == 0 else s.CAr[:, :, t - 1, :]
                    im0 = cim[:, :, :] if t == 0 else s.CAi[:, :, t - 1, :]
                    tt(g1[:, :, :], re0, wide(ar[:, :], GC), ALU.mult)
                    tt(g2[:, :, :], im0, wide(ai[:, :], GC), ALU.mult)
                    tt(g3[:, :, :], im0, wide(ar[:, :], GC), ALU.mult)
                    ch(tt(g4[:, :, :], re0, wide(ai[:, :], GC), ALU.mult))
                    tt(s.CAr[:, :, t, :], g1[:, :, :], g2[:, :, :], ALU.add)
                    ch(tt(s.CAi[:, :, t, :], g3[:, :, :], g4[:, :, :], ALU.subtract))
                    if t == 0:
                        nc.gpsimd.memset(s.T[:, :, :], 0.0).then_inc(t_zeroed, 1)

            @block.vector
            def _(dve):
                ch = Chain(dve, seq)
                ts, tt = nc.vector.tensor_scalar, nc.vector.tensor_tensor
                dve.wait_ge(dts, 1)
                lr, li = par[:, 0, :], par[:, 1, :]
                tt(ld[:, :], lr, dt_[:, :], ALU.mult).then_inc(angles, 1)
                ch(tt(th[:, 0, :], li, dt_[:, :], ALU.mult))
                ch(ts(th[:, 1, :], th[:, 0, :], float(L), None, ALU.mult))
                ch(ts(kk[:, :, :], th[:, :, :], 1.0 / TWO_PI, None, ALU.mult))
                ch(ts(kk[:, :, :], kk[:, :, :], MAGIC, None, ALU.add))
                ch(ts(kk[:, :, :], kk[:, :, :], MAGIC, None, ALU.subtract))
                stt = nc.vector.scalar_tensor_tensor
                ch(stt(rr[:, :, :], kk[:, :, :], -PI_HI, th[:, :, :], ALU.mult, ALU.add))
                ch(stt(rr[:, :, :], kk[:, :, :], -PI_MID, rr[:, :, :], ALU.mult, ALU.add))
                ch(stt(rr[:, :, :], kk[:, :, :], -PI_LO, rr[:, :, :], ALU.mult, ALU.add))
                ch(ts(rr[:, :, :], rr[:, :, :], 3.1415925, -3.1415925, ALU.min, ALU.max))
                ch(ts(ra[:, :, :], rr[:, :, :], -1.0, None, ALU.mult))
                dve.wait_ge(zeroed, 1)
                ch(tt(ra[:, :, :], rr[:, :, :], ra[:, :, :], ALU.max))
                dve.sem_inc(absd, 1)
                dve.wait_ge(exps, 2)
                dve.wait_ge(sines, 2)
                tt(ar[:, :], mg[:, 0, :], cs[:, 0, 0, :], ALU.mult)
                ch(tt(ai[:, :], mg[:, 0, :], cs[:, 1, 0, :], ALU.mult))
                dve.sem_inc(a_ready, 1)
                tt(s.a8[:, 0, :], mg[:, 1, :], cs[:, 0, 1, :], ALU.mult)
                tt(s.a8[:, 1, :], mg[:, 1, :], cs[:, 1, 1, :], ALU.mult)
                ch(ts(nr[:, :], ar[:, :], 1.0, None, ALU.subtract))
                tt(t1[:, :], lr, lr, ALU.mult)
                ch(tt(t2[:, :], li, li, ALU.mult))
                ch(tt(den[:, :], t1[:, :], t2[:, :], ALU.add))
                ch(nc.vector.reciprocal(den[:, :], den[:, :]))
                tt(t1[:, :], nr[:, :], lr, ALU.mult)
                ch(tt(t2[:, :], ai[:, :], li, ALU.mult))
                ch(tt(cr[:, :], t1[:, :], t2[:, :], ALU.add))
                tt(t1[:, :], ai[:, :], lr, ALU.mult)
                ch(tt(t2[:, :], nr[:, :], li, ALU.mult))
                ch(tt(ci[:, :], t1[:, :], t2[:, :], ALU.subtract))
                tt(cr[:, :], cr[:, :], den[:, :], ALU.mult)
                ch(tt(ci[:, :], ci[:, :], den[:, :], ALU.mult))
                dve.wait_ge(e_in, 32)

                def cmul(re_out, im_out, re, im, xr, xi, n):
                    tt(u1[:, :, :], re, wide(xr, n), ALU.mult)
                    tt(u2[:, :, :], im, wide(xi, n), ALU.mult)
                    tt(u3[:, :, :], im, wide(xr, n), ALU.mult)
                    ch(tt(u4[:, :, :], re, wide(xi, n), ALU.mult))
                    tt(re_out, u1[:, :, :], u2[:, :, :], ALU.subtract)
                    ch(tt(im_out, u3[:, :, :], u4[:, :, :], ALU.add))

                cmul(pr[:, :, L - 1, :], pi[:, :, L - 1, :], bre[:, :, :], bim[:, :, :], cr[:, :], ci[:, :], GC)
                for b in range(L - 2, -1, -1):
                    cmul(pr[:, :, b, :], pi[:, :, b, :], pr[:, :, b + 1, :], pi[:, :, b + 1, :], ar[:, :], ai[:, :], GC)
                dve.sem_inc(b_ready, 1)
                nc.vector.memset(s.Er[:, :, 0:1], 1.0)
                nc.vector.memset(s.Ei[:, :, 0:1], 0.0)
                nc.vector.tensor_copy(s.Er[:, :, 1:2], cs[:, 0, 1, :].unsqueeze(2))
                ch(nc.vector.tensor_copy(s.Ei[:, :, 1:2], cs[:, 1, 1, :].unsqueeze(2)))
                w1, w2, w3, w4 = (s.work[n // 2][:, :, CH // 2 * (n % 2):] for n in range(4))
                m = 1
                while m < CH:
                    n = min(m, CH - 1 - m)
                    if n <= 0:
                        break
                    for dst, a, b in ((w1, s.Er, s.Er), (w2, s.Ei, s.Ei), (w3, s.Er, s.Ei), (w4, s.Ei, s.Er)):
                        last = tt(dst[:, :, 0:n], a[:, :, 1:n + 1], wide(b[:, :, m], n), ALU.mult)
                    ch(last)
                    tt(s.Er[:, :, m + 1:m + 1 + n], w1[:, :, 0:n], w2[:, :, 0:n], ALU.subtract)
                    ch(tt(s.Ei[:, :, m + 1:m + 1 + n], w3[:, :, 0:n], w4[:, :, 0:n], ALU.add))
                    m *= 2
                nc.vector.tensor_copy(s.m8[:, :], mg[:, 1, :])
                dve.wait_ge(kd_in, 16)
                dve.wait_ge(k_made, 1)
                nc.vector.tensor_tensor(kcol[:, :], bk[5][:, :], kd[:, :], ALU.add).then_inc(k_kept, 1)

            @block.tensor
            def _(pe):
                for g in range(G):
                    k = (g // 4) % 4
                    if g % 4 == 0 and g >= 16:
                        pe.wait_ge(u_kept, g // 4 - 3)
                    src = s.uc[:, g, :, :].rearrange("p t c -> p (t c)")
                    last = pe.transpose(bk[k][:, (g % 4) * P:(g % 4 + 1) * P], src, s.ident[:, :])
                    if g % 4 == 3:
                        last.then_inc(u_made, 1)
                pe.wait_ge(us_in, 16 * T_DEC)
                for g in range(G):
                    last = pe.transpose(bk[4][:, g * NB_DEC:(g + 1) * NB_DEC],
                                        s.us8[:, g, :, :].rearrange("p t c -> p (t c)"), s.ident[0:NB_DEC, 0:NB_DEC])
                last.then_inc(u_made, 1)
                pe.wait_ge(b_ready, 1)
                pe.wait_ge(cseq, 1)
                flat = lambda t, q: t[:, q, :, :].rearrange("p b c -> p (b c)")
                for q in range(PR):
                    out = bk[5][:, q * 2 * GC:(q + 1) * 2 * GC]
                    pe.matmul(out, flat(pr, q), cbr[:, q, :], start=True, stop=False)
                    last = pe.matmul(out, flat(pi, q), cbi[:, q, :], start=False, stop=True)
                last.then_inc(k_made, 1)
                for q in range(PR):
                    if q % 2 == 0 and q >= 4:
                        pe.wait_ge(v_kept, (q - 4) // 2 + 1)
                    at = 256 * (q % 2)
                    pe.transpose(bk[6 + (q // 2) % 2][:, at:at + P], flat(pr, q), s.ident[:, :])
                    last = pe.transpose(bk[6 + (q // 2) % 2][:, at + P:at + 2 * P], flat(pi, q), s.ident[:, :])
                    if q % 2:
                        last.then_inc(v_made, 1)
                pe.wait_ge(u_kept, G // 4 + 1)
                pe.wait_ge(k_kept, 1)
                for t in range(L):
                    if t >= 4:
                        pe.wait_ge(t_kept, t - 3)
                    n = (t + 1) * GC
                    pe.matmul(bk[t % 4][0:n, :], s.ident[:, P - n:P], kcol[:, :], start=True, stop=True).then_inc(t_made, 1)


def ssm_scan(nc, io, s):
    with ExitStack() as c:
        sb = lambda n, sh, dt=F32: c.enter_context(nc.sbuf_tensor(n, sh, dt))
        sem = semaphores(nc, c)
        QP = PR // 4
        U = s.U
        Vr = sb("Vr", [P, PR, NC])
        Vi = sb("Vi", [P, PR, NC])
        Gr, Gi, w1, w2 = s.work
        Hr, Hi = Vr, Vi
        h0 = sb("h0", [P, 2, PR, NB_DEC])
        hn = sb("hn", [P, 2, PR, NB_DEC])
        hw = [Gr[:, :, NB_DEC * k:NB_DEC * (k + 1)] for k in range(4)]
        fin = sb("fin", [P, 2, PR])
        part = [wk[:, 4 * k:4 * k + 4, :].rearrange("p q j -> p (q j)") for wk in s.work for k in range(4)]
        ty, tz, tw, gl = part[0:4], part[4:8], part[8:12], part[12:16]
        bk = [c.enter_context(nc.psum_tensor(f"pv{k}", [P, 512], F32)) for k in range(8)]
        (h_in, v_made, v_kept, seq, hs_ready, fin_ready, hn_ready, sent, y_made, ya_kept, yv_kept, us_back, squared,
         cubed, tanhed, gelued, turned, g_kept) = (sem("sc_" + n) for n in (
            "h v_made v_kept seq hs fin hn sent y_made ya_kept yv_kept us_back squared cubed tanhed gelued turned "
            "g_kept").split())
        YB = G // 4

        def y_place(j):
            u = s.us8 if j < YB else s.uc
            g0 = 8 * (j % YB // 2) + j % 2
            return u[:, g0:g0 + 7:2, :, :].rearrange("p g t c -> p g (t c)")

        def y_bank(j):
            return bk[j % 4][0:NB_DEC if j < YB else P, :].rearrange("p (g n) -> p g n", g=4)

        gc = lambda ap: ap.rearrange("p (g c) -> p g c", g=G)
        tile = lambda n: s.uc[:, :, n, :] if n < L else gc(s.us[:, :])
        rows_of = lambda n: P if n < L else NS

        with nc.Block() as block:
            @block.sync
            def _(sp):
                sp.dma_start(h0[:, 0, :, :], io["l_h0r"]).then_inc(h_in, 16)
                sp.dma_start(h0[:, 1, :, :], io["l_h0i"]).then_inc(h_in, 16)
                sp.wait_ge(ya_kept, YB)
                for t in range(T_DEC):
                    sp.dma_start(s.us[t:NS:T_DEC, :].rearrange("b (g c) -> b g c", g=G), s.us8[:, :, t, :]) \
                        .then_inc(us_back, 16)
                sp.wait_ge(fin_ready, 1)
                sp.dma_start(io["h_prompt"], fin[:, :, :]).then_inc(sent, 16)
                sp.wait_ge(hn_ready, 1)
                sp.dma_start(io["h_sample"], hn[:, :, :, :]).then_inc(sent, 16)
                sp.wait_ge(sent, 32)

            @block.tensor
            def _(pe):
                for q in range(PR):
                    k = 4 + q % 4
                    if q >= 4:
                        pe.wait_ge(v_kept, q - 3)
                    for r in range(2):
                        rows_ = slice(ST * r, ST * r + ST)
                        pe.matmul(bk[k][rows_, 0:NC], s.VTr[:, q, rows_], U[:, 2 * q + r, :], start=True, stop=True)
                        last = pe.matmul(bk[k][rows_, 256:256 + NC], s.VTi[:, q, rows_], U[:, 2 * q + r, :],
                                         start=True, stop=True)
                    last.then_inc(v_made, 1)
                pe.wait_ge(h_in, 32)
                for j in range(2 * YB):
                    sampled = j < YB
                    if j >= 4:
                        pe.wait_ge(*((ya_kept, j - 3) if j - 4 < YB else (yv_kept, j - 3 - YB)))
                    if not sampled and j % 2 == 0:
                        pe.wait_ge(hs_ready, (j - YB) // 2 + 1)
                    m = NB_DEC if sampled else P
                    for gg in range(4):
                        g = 8 * (j % YB // 2) + 2 * gg + j % 2
                        q, r = g // 2, slice(ST * (g % 2), ST * (g % 2) + ST)
                        out = bk[j % 4][0:m, gg * P:(gg + 1) * P]
                        cols = slice(CH + 1, CH + 1 + NB_DEC) if sampled else slice(0, CH)
                        hr = h0[r, 0, q, :] if sampled else Hr[r, q, 0:CH]
                        hi = h0[r, 1, q, :] if sampled else Hi[r, q, 0:CH]
                        pe.matmul(out, U[:, g, cols], s.T[:, g, :], start=True, stop=False)
                        pe.matmul(out, hr, s.CAr[r, q, :, :].rearrange("p t c -> p (t c)"), start=False, stop=False)
                        last = pe.matmul(out, hi, s.CAi[r, q, :, :].rearrange("p t c -> p (t c)"),
                                         start=False, stop=True)
                    last.then_inc(y_made, 1)
                pe.wait_ge(v_kept, PR)
                for n in range(L + 1):
                    m = rows_of(n)
                    pe.wait_ge(gelued, n + 1)
                    if n >= 4:
                        pe.wait_ge(g_kept, n - 3)
                    for k in range(4):
                        last = pe.transpose(bk[4 + n % 4][:, k * P:k * P + m], gl[n % 4][0:m, k * P:(k + 1) * P],
                                            s.ident[0:m, 0:m])
                    last.then_inc(turned, 1)

            @block.vector
            def _(dve):
                ch = Chain(dve, seq)
                tt = nc.vector.tensor_tensor
                for k in range(4):
                    a = QP * k
                    dve.wait_ge(v_kept, a + QP)
                    full = (slice(None), slice(a, a + QP), slice(0, CH))
                    tt(w1[full], s.Er[full], Vr[full], ALU.mult)
                    tt(w2[full], s.Ei[full], Vi[full], ALU.mult)
                    tt(Gr[full], s.Er[full], Vi[full], ALU.mult)
                    ch(tt(Gi[full], s.Ei[full], Vr[full], ALU.mult))
                    tt(w1[full], w1[full], w2[full], ALU.add)
                    ch(tt(Gr[full], Gr[full], Gi[full], ALU.subtract))
                    for q in range(a, a + QP):
                        m8 = s.m8[:, q:q + 1].to_broadcast([P, CH])
                        nc.vector.tensor_tensor_scan(w2[:, q, :], m8, w1[:, q, :], 0.0, ALU.mult, ALU.add)
                        last = nc.vector.tensor_tensor_scan(Gi[:, q, :], m8, Gr[:, q, :], 0.0, ALU.mult, ALU.add)
                    ch(last)
                    nxt = (slice(None), slice(a, a + QP), slice(1, CH + 1))
                    nc.vector.memset(Hr[:, a:a + QP, 0:1], 0.0)
                    nc.vector.memset(Hi[:, a:a + QP, 0:1], 0.0)
                    tt(w1[full], s.Er[full], w2[full], ALU.mult)
                    ch(tt(Gr[full], s.Ei[full], Gi[full], ALU.mult))
                    ch(tt(Hr[nxt], w1[full], Gr[full], ALU.subtract))
                    tt(w1[full], s.Er[full], Gi[full], ALU.mult)
                    ch(tt(Gr[full], s.Ei[full], w2[full], ALU.mult))
                    tt(Hi[nxt], w1[full], Gr[full], ALU.add).then_inc(hs_ready, 1)
                dve.wait_ge(hs_ready, 4)
                nc.vector.tensor_copy(fin[:, 0, :], Hr[:, :, CH])
                nc.vector.tensor_copy(fin[:, 1, :], Hi[:, :, CH]).then_inc(fin_ready, 1)
                dve.wait_ge(h_in, 32)
                r8, i8 = wide(s.a8[:, 0, :], NB_DEC), wide(s.a8[:, 1, :], NB_DEC)
                tt(hw[0], h0[:, 0, :, :], r8, ALU.mult)
                tt(hw[1], h0[:, 1, :, :], i8, ALU.mult)
                tt(hw[2], h0[:, 1, :, :], r8, ALU.mult)
                ch(tt(hw[3], h0[:, 0, :, :], i8, ALU.mult))
                tt(hw[0], hw[0], hw[1], ALU.subtract)
                ch(tt(hw[2], hw[2], hw[3], ALU.add))
                tt(hn[:, 0, :, :], hw[0], Vr[:, :, CH + 1:], ALU.add)
                tt(hn[:, 1, :, :], hw[2], Vi[:, :, CH + 1:], ALU.add).then_inc(hn_ready, 1)
                for j in range(YB, 2 * YB):
                    dve.wait_ge(y_made, j + 1)
                    nc.vector.tensor_copy(y_place(j), y_bank(j)).then_inc(yv_kept, 1)
                for n in range(L + 2):
                    if n <= L:
                        m = rows_of(n)
                        dve.wait_ge(squared, n + 1)
                        if n >= 4:
                            dve.wait_ge(tanhed, n - 3)
                        nc.vector.scalar_tensor_tensor(gc(tz[n % 4])[0:m], gc(ty[n % 4])[0:m], 1.0, tile(n),
                                                       ALU.add, ALU.mult).then_inc(cubed, 1)
                    if n >= 1:
                        o, m = n - 1, rows_of(n - 1)
                        dve.wait_ge(tanhed, o + 1)
                        if o >= 4:
                            dve.wait_ge(turned, o - 3)
                        nc.vector.scalar_tensor_tensor(gc(gl[o % 4])[0:m], gc(tw[o % 4])[0:m], 1.0, tile(o),
                                                       ALU.add, ALU.mult).then_inc(gelued, 1)

            @block.scalar
            def _(act):
                for q in range(PR):
                    act.wait_ge(v_made, q + 1)
                    nc.scalar.activation(Vr[:, q, :], bk[4 + q % 4][:, 0:NC], ACT.Copy)
                    nc.scalar.activation(Vi[:, q, :], bk[4 + q % 4][:, 256:256 + NC], ACT.Copy).then_inc(v_kept, 1)
                for j in range(YB):
                    act.wait_ge(y_made, j + 1)
                    nc.scalar.activation(y_place(j), y_bank(j), ACT.Copy).then_inc(ya_kept, 1)
                act.wait_ge(yv_kept, YB)
                act.wait_ge(hn_ready, 1)
                for n in range(L + 3):
                    if n <= L:
                        m = rows_of(n)
                        if n == L:
                            act.wait_ge(us_back, 16 * T_DEC)
                        if n >= 4:
                            act.wait_ge(cubed, n - 3)
                        nc.scalar.activation(gc(ty[n % 4])[0:m], tile(n), ACT.Square, scale=0.044715 ** 0.5) \
                            .then_inc(squared, 1)
                    if 1 <= n <= L + 1:
                        o, m = n - 1, rows_of(n - 1)
                        act.wait_ge(cubed, o + 1)
                        if o >= 4:
                            act.wait_ge(gelued, o - 3)
                        nc.scalar.activation(tw[o % 4][0:m, :], tz[o % 4][0:m, :], ACT.Tanh,
                                             scale=0.7978845608028654).then_inc(tanhed, 1)
                    if n >= 2:
                        o, m = n - 2, rows_of(n - 2)
                        act.wait_ge(turned, o + 1)
                        src = bk[4 + o % 4][:, :].rearrange("p (k j) -> p k j", k=4)[:, :, 0:m]
                        dst = s.gT[:, :, o:SEQ:L] if o < L else s.gT[:, :, SEQ:N]
                        nc.scalar.activation(dst, src, ACT.Copy, scale=0.25).then_inc(g_kept, 1)


def layer_norm(ch, nc, r, out, g, b, st, mv, root):
    n = r.shape[0]
    nc.vector.bn_stats(st[0:n, 0, :], r[:, 0:512])
    ch(nc.vector.bn_stats(st[0:n, 1, :], r[:, 512:D]))
    ch(nc.vector.bn_aggr(mv[0:n, 0:2], st[0:n, :, :].rearrange("p a b -> p (a b)")))
    ch(nc.vector.tensor_scalar(mv[0:n, 2:3], mv[0:n, 1:2], EPS, None, ALU.add))
    root(mv[0:n, 2:3])
    ch(nc.vector.reciprocal(mv[0:n, 3:4], mv[0:n, 2:3]))
    ch(nc.vector.tensor_scalar(r, r, mv[0:n, 0:1], mv[0:n, 3:4], ALU.subtract, ALU.mult))
    ch(nc.vector.tensor_tensor(r, r, g[0:n, :], ALU.mult))
    return nc.vector.tensor_tensor(out, r, b[0:n, :], ALU.add)


def mix(nc, io, s):
    spans = [(0, 384), (384, 352), (736, 352)]
    glu = [(k, n) for k in range(W // P) for n in range(3)]
    with ExitStack() as c:
        sb = lambda n, sh, dt=F32: c.enter_context(nc.sbuf_tensor(n, sh, dt))
        sem = semaphores(nc, c)
        wg = sb("wg", [P, W // P, W])
        wo = [sb(f"wo{k}", [P, KD, D], F32R) for k in range(2)]
        wr = sb("wr", [P, KD, E])
        bh = sb("bh", [P, W // P])
        sT = sb("sT", [P, W // P, N])
        ap = [[sb(f"ap{k}{j}", [P, KD, P], F32R) for k in range(2)] for j in range(2)]
        tg = [sb(f"tg{k}", [P, 512]) for k in range(2)]
        rr = [sb(f"mr{k}", [P, D]) for k in range(2)]
        xT = [wg[:, 2 * k:2 * k + 2, :].rearrange("p a (k t) -> p (a k) t", t=P) for k in range(2)]
        lg, lb, xn0, xn1 = (s.raw[:, DOWN_AT + k * D:DOWN_AT + (k + 1) * D] for k in range(4))
        xn = [xn0, xn1]
        st, mv = sb("mst", [P, 2, 6]), sb("mmv", [P, 4])
        bk = [c.enter_context(nc.psum_tensor(f"pm{k}", [P, 512], F32)) for k in range(8)]
        wo_in = [sem(f"mi_wo{k}") for k in range(2)]
        w_high, w_split, a_high, a_split = (sem("mi_" + n) for n in "w_high w_split a_high a_split".split())
        (wg_in, wr_in, b_in, l_in, seq, z_made, tanhed, s_made, m_made, m_used, normed, var_ready,
         rooted, turned, t_kept, l_made, l_kept, b_halved, first_in, lgt_zeroed) = (sem("mi_" + n) for n in (
            "wg wr b l seq z_made tanhed s_made m_made m_used normed var_ready rooted turned t_kept "
            "l_made l_kept b_halved first_in lgt_zeroed").split())
        x_in = [sem(f"mi_x{k}") for k in range(2)]
        x_out = [sem(f"mi_xo{k}") for k in range(2)]

        with nc.Block() as block:
            @block.sync
            def _(sp):
                sp.dma_start(wg[:, :, :], io["ssm_w_glu"][0].rearrange("(k p) n -> p k n", p=P)).then_inc(wg_in, 16)
                sp.dma_start(bh[:, :], io["l_bglu"]).then_inc(b_in, 16)
                for b in range(2):
                    sp.dma_start(xn[b][:, :], io["x_prompt"][0, b * P:(b + 1) * P, :]).then_inc(x_in[b], 16)
                for k in range(KD):
                    if k >= 2:
                        sp.wait_ge(w_split, k - 1)
                    sp.dma_start(rr[k % 2][:, :], io["w_out"][0, k * P:(k + 1) * P, :]).then_inc(wo_in[k % 2], 16)
                sp.dma_start(wr[:, :, :], io["router_w"].rearrange("(p k) e -> p k e", k=KD)).then_inc(wr_in, 16)
                sp.dma_start(lg[:, :], io["ln1_g"].to_broadcast([P, D])).then_inc(l_in, 16)
                sp.dma_start(lb[:, :], io["ln1_b"].to_broadcast([P, D])).then_inc(l_in, 16)
                for i in range(2):
                    sp.dma_start(s.raw[:, slice(*PIECES[i])], expert_weights(io, 0, i)).then_inc(first_in, 16)
                for b in range(NBLK):
                    r = rows(b)
                    sp.wait_ge(normed, b + 1)
                    sp.dma_start(s.x1d[b * P:b * P + r, :], rr[b % 2][0:r, :]).then_inc(x_out[b % 2], 16)
                    if b + 2 < NBLK:
                        src = io["x_prompt"][0, (b + 2) * P:(b + 3) * P, :] if b + 2 < QB else \
                            io["x_sample"].rearrange("b t d -> (b t) d")
                        sp.wait_ge(m_used, b + 1)
                        sp.dma_start(xn[b % 2][0:rows(b + 2), :], src).then_inc(x_in[b % 2], 16)
                sp.wait_ge(x_out[0], 16 * (NBLK - NBLK // 2))
                sp.wait_ge(x_out[1], 16 * (NBLK // 2))
                sp.wait_ge(first_in, 16 * 2)

            @block.tensor
            def _(pe):
                pe.wait_ge(wg_in, 16)
                for i, (k, n) in enumerate(glu):
                    if i >= 4:
                        pe.wait_ge(tanhed, i - 3)
                    a, m = spans[n]
                    for j in range(W // P):
                        last = pe.matmul(bk[i % 4][:, 0:m], wg[:, j, k * P:(k + 1) * P], s.gT[:, j, a:a + m],
                                         start=(j == 0), stop=(j == W // P - 1))
                    last.then_inc(z_made, 1)
                pe.wait_ge(s_made, len(glu))
                pe.wait_ge(tanhed, len(glu))
                pe.wait_ge(w_split, KD)
                pe.wait_ge(wr_in, 16)

                def project_out(b):
                    if b >= 2:
                        pe.wait_ge(m_used, b - 1)
                    pe.wait_ge(a_split, b + 1)
                    r = rows(b)
                    for half in range(2):
                        out, cols = bk[2 * (b % 2) + half][0:r, :], slice(half * 512, (half + 1) * 512)
                        for k in range(KD):
                            hi, lo = (part[:, k, 0:r] for part in ap[b % 2])
                            pe.matmul(out, hi, wo[0][:, k, cols], start=(k == 0), stop=False)
                            pe.matmul(out, hi, wo[1][:, k, cols], start=False, stop=False)
                            last = pe.matmul(out, lo, wo[0][:, k, cols], start=False, stop=(k == KD - 1))
                    last.then_inc(m_made, 1)

                def logits(b):
                    r = rows(b)
                    pe.wait_ge(normed, b + 1)
                    if b >= 1:
                        pe.wait_ge(t_kept, b)
                    xv = rr[b % 2][0:r, :].rearrange("t (p k) -> t k p", k=KD)
                    for k in range(KD):
                        last = pe.transpose(bk[4 + k // 4][:, (k % 4) * P:(k % 4) * P + r], xv[:, k, :],
                                            s.ident[0:r, 0:r])
                    last.then_inc(turned, 1)
                    pe.wait_ge(t_kept, b + 1)
                    if b >= 2:
                        pe.wait_ge(l_kept, b - 1)
                    for k in range(KD):
                        last = pe.matmul(bk[6 + b % 2][0:r, 0:E], xT[b % 2][:, k, 0:r], wr[:, k, :],
                                         start=(k == 0), stop=(k == KD - 1))
                    last.then_inc(l_made, 1)

                project_out(0)
                for b in range(NBLK):
                    if b + 1 < NBLK:
                        project_out(b + 1)
                    logits(b)

            @block.gpsimd
            def _(pool):
                pool.wait_ge(b_in, 16)
                nc.gpsimd.tensor_scalar(bh[:, :], bh[:, :], 0.5, None, ALU.mult).then_inc(b_halved, 1)

            @block.vector
            def _(dve):
                for i, (k, n) in enumerate(glu):
                    a, m = spans[n]
                    dve.wait_ge(tanhed, i + 1)
                    nc.vector.scalar_tensor_tensor(sT[:, k, a:a + m], tg[i % 2][:, 0:m], 1.0, s.gT[:, k, a:a + m],
                                                   ALU.add, ALU.mult).then_inc(s_made, 1)
                    if i < KD:
                        dve.wait_ge(w_high, i + 1)
                        nc.vector.tensor_tensor(wo[1][:, i, :], rr[i % 2][:, :], wo[0][:, i, :].bitcast(F32),
                                                ALU.subtract).then_inc(w_split, 1)

                def low_a(b):
                    r = rows(b)
                    dve.wait_ge(a_high, b + 1)
                    hi, lo = ap[b % 2]
                    for n, src in enumerate((s.aT, sT)):
                        ks = slice(4 * n, 4 * n + 4)
                        last = nc.vector.tensor_tensor(lo[:, ks, 0:r], src[:, :, b * P:b * P + r],
                                                       hi[:, ks, 0:r].bitcast(F32), ALU.subtract)
                    last.then_inc(a_split, 1)

                low_a(0)
                low_a(1)
                ch = Chain(dve, seq)
                nc.vector.memset(s.lgt[:, QB, :], 0.0).then_inc(lgt_zeroed, 1)
                dve.wait_ge(l_in, 32)
                for b in range(NBLK):
                    r = rows(b)
                    dve.wait_ge(m_made, b + 1)
                    dve.wait_ge(x_in[b % 2], 16 * (b // 2 + 1))
                    if b >= 2:
                        dve.wait_ge(x_out[b % 2], 16 * (b // 2))
                        dve.wait_ge(turned, b - 1)
                    for half in range(2):
                        cols = slice(512 * half, 512 * half + 512)
                        last = nc.vector.scalar_tensor_tensor(rr[b % 2][0:r, cols], xn[b % 2][0:r, cols], ALPHA,
                                                              bk[2 * (b % 2) + half][0:r, :], ALU.mult, ALU.add)
                    last.then_inc(m_used, 1)
                    dve.wait_ge(m_used, b + 1)

                    def root(ap, b=b):
                        dve.sem_inc(var_ready, 1)
                        dve.wait_ge(rooted, b + 1)

                    x = rr[b % 2][0:r, :]
                    layer_norm(ch, nc, x, x, lg, lb, st, mv, root).then_inc(normed, 1)
                    if b + 2 < NBLK:
                        low_a(b + 2)

            @block.scalar
            def _(act):
                act.wait_ge(b_halved, 1)
                for i, (k, n) in enumerate(glu):
                    a, m = spans[n]
                    act.wait_ge(z_made, i + 1)
                    if i >= 2:
                        act.wait_ge(s_made, i - 1)
                    nc.scalar.activation(tg[i % 2][:, 0:m], bk[i % 4][:, 0:m], ACT.Tanh, bias=bh[:, k:k + 1]) \
                        .then_inc(tanhed, 1)
                    if i < KD:
                        act.wait_ge(wo_in[i % 2], 16 * (i // 2 + 1))
                        nc.scalar.activation(wo[0][:, i, :], rr[i % 2][:, :], ACT.Copy).then_inc(w_high, 1)

                def high_a(b):
                    r = rows(b)
                    if b >= 2:
                        act.wait_ge(m_made, b - 1)
                    else:
                        act.wait_ge(s_made, len(glu))
                    for n, src in enumerate((s.aT, sT)):
                        last = nc.scalar.activation(ap[b % 2][0][:, 4 * n:4 * n + 4, 0:r], src[:, :, b * P:b * P + r],
                                                    ACT.Copy)
                    last.then_inc(a_high, 1)

                high_a(0)
                high_a(1)
                for b in range(NBLK):
                    r = rows(b)
                    act.wait_ge(var_ready, b + 1)
                    nc.scalar.activation(mv[0:r, 2:3], mv[0:r, 2:3], ACT.Sqrt).then_inc(rooted, 1)
                    if b + 2 < NBLK:
                        high_a(b + 2)
                    act.wait_ge(turned, b + 1)
                    if b >= 2:
                        act.wait_ge(l_made, b - 1)
                    for half in range(2):
                        src = bk[4 + half][:, :].rearrange("p (k t) -> p k t", k=4)[:, :, 0:r]
                        last = nc.scalar.activation(xT[b % 2][:, 4 * half:4 * half + 4, 0:r], src, ACT.Copy)
                    last.then_inc(t_kept, 1)
                    act.wait_ge(l_made, b + 1)
                    if b == QB:
                        act.wait_ge(lgt_zeroed, 1)
                    nc.scalar.activation(s.lgt[0:r, b, :], bk[6 + b % 2][0:r, 0:E], ACT.Copy).then_inc(l_kept, 1)


def route(nc, io, s):
    with ExitStack() as c:
        sb = lambda n, sh, dt=F32: c.enter_context(nc.sbuf_tensor(n, sh, dt))
        sem = semaphores(nc, c)
        rb = sb("rb", [P, E])
        before = sb("before", [P, P])
        ones = sb("ones", [P, P])
        lower = sb("lower", [P, EG, EG])
        tok = sb("tok", [P, NBLK])
        count = sb("count", [P, P])
        same = sb("same", [P, 2 * NBLK, P])
        holds = sb("holds", [P, 2 * NBLK, NSB + 1])
        place, blk = sb("place", [P, 2, NBLK]), sb("blk", [P, 2, NBLK])
        past = sb("past", [1, NSB + 1, E])
        ne, top = sb("ne", [1, E]), sb("top", [1, 1])
        new = sb("new", [1, NSB + 1])
        cmp_, tie = sb("cmp", [P, NBLK * EG, EG * EG]), sb("tie", [P, NBLK * EG, EG * EG])
        big = lambda n: sb(n, [P, NBLK, E])
        sc, sel, M, gate, rank, eq, slot, lo = (big("r_" + n) for n in "sc sel M gate rank eq slot lo".split())
        grp = lambda n: sb(n, [P, NBLK, EG])
        h1, h2, l1, l2, m1, m2, gs, ig, fg = (grp("r_" + n) for n in "h1 h2 l1 l2 m1 m2 gs ig fg".split())
        one = lambda n: sb(n, [P, NBLK])
        gm, tk, ws, sa, sz = (one("r_" + n) for n in "gm tk ws sa sz".split())
        nb, end, beg = (sb("r_" + n, [P, E]) for n in "nb end beg".split())
        ahead = sb("r_ahead", [P, NBLK + 1, E])
        eb, w0 = (sb("r_" + n, [1, NSB + 1]) for n in "eb w0".split())
        cnt = c.enter_context(nc.psum_tensor("cnt", [P, 512], F32))
        held = c.enter_context(nc.psum_tensor("ps_held", [P, NSB + 1], F32))
        (c_in, seq, tanhed, ones_set, m_ready, counted, slots_ready, placed) = (
            sem("ro_" + n) for n in "c_in seq tanhed ones m_ready counted slots placed".split())

        with nc.Block() as block:
            @block.sync
            def _(sp):
                sp.dma_start(rb[:, :], io["router_bias"].rearrange("(o e) -> o e", o=1).to_broadcast([P, E])) \
                    .then_inc(c_in, 16)
                sp.dma_start(before[:, :], io["c_before"]).then_inc(c_in, 16)
                sp.dma_start(tok[:, :], io["c_tok"]).then_inc(c_in, 16)
                sp.dma_start(count[:, :], io["c_count"]).then_inc(c_in, 16)
                sp.dma_start(lower[:, :, :], io["c_lower"]).then_inc(c_in, 16)

            @block.scalar
            def _(act):
                nc.scalar.activation(sc[:, :, :], s.lgt[:, :, :], ACT.Tanh, scale=0.5).then_inc(tanhed, 1)

            @block.gpsimd
            def _(pool):
                nc.gpsimd.memset(ones[:, :], 1.0).then_inc(ones_set, 1)

            @block.tensor
            def _(pe):
                pe.wait_ge(c_in, 80)
                pe.wait_ge(ones_set, 1)
                pe.wait_ge(m_ready, 1)
                flat_m = M[:, :, :].rearrange("p b e -> p (b e)")
                pe.matmul(cnt[:, 0:NBLK * E], before[:, :], flat_m, start=True, stop=True)
                last = pe.matmul(cnt[:, NBLK * E:2 * NBLK * E], ones[:, :], flat_m, start=True, stop=True)
                last.then_inc(counted, 1)
                pe.wait_ge(slots_ready, 1)
                for i in range(2 * NBLK):
                    last = pe.matmul(held[:, :], same[:, i, :], holds[:, i, :], start=(i == 0), stop=(i == 2 * NBLK - 1))
                last.then_inc(placed, 1)

            @block.vector
            def _(dve):
                ch = Chain(dve, seq)
                ts, tt, stt = nc.vector.tensor_scalar, nc.vector.tensor_tensor, nc.vector.scalar_tensor_tensor
                A = lambda t: t[:, :, :]
                dve.wait_ge(tanhed, 1)
                dve.wait_ge(c_in, 80)
                ch(ts(A(sc), A(sc), 0.5, 0.5, ALU.mult, ALU.add))
                ch(tt(A(sel), A(sc), mid(rb[:, :], NBLK), ALU.add))
                v = sel[:, :, :].rearrange("p b (g e) -> p b g e", e=EG)
                e = [v[:, :, :, k] for k in range(EG)]
                tt(A(h1), e[0], e[1], ALU.max)
                tt(A(l1), e[0], e[1], ALU.min)
                tt(A(h2), e[2], e[3], ALU.max)
                ch(tt(A(l2), e[2], e[3], ALU.min))
                tt(A(m1), A(h1), A(h2), ALU.max)
                tt(A(m2), A(h1), A(h2), ALU.min)
                ch(tt(A(l1), A(l1), A(l2), ALU.max))
                ch(tt(A(m2), A(m2), A(l1), ALU.max))
                ch(tt(A(gs), A(m1), A(m2), ALU.add))
                ch(nc.vector.tensor_reduce(gm[:, :], A(gs), AX.X, ALU.max))
                ch(tt(A(ig), A(gs), wide(gm[:, :], EG), ALU.is_ge))
                ch(nc.vector.memset(tk[:, :], 1.0))
                for g in range(EG):
                    ch(tt(fg[:, :, g], ig[:, :, g], tk[:, :], ALU.mult))
                    ch(tt(tk[:, :], tk[:, :], fg[:, :, g], ALU.subtract))
                sv = sel[:, :, :].rearrange("p b (g e) -> p (b g) e", e=EG)
                row = sv.unsqueeze(3).to_broadcast([P, NBLK * EG, EG, EG])
                col = sv.unsqueeze(2).to_broadcast([P, NBLK * EG, EG, EG])
                table = lambda t: t[:, :, :].rearrange("p n (i j) -> p n i j", j=EG)
                tt(table(cmp_), col, row, ALU.is_gt)
                ch(tt(table(tie), col, row, ALU.is_equal))
                ch(tt(table(tie), table(tie), lower[:, :, :].unsqueeze(1).to_broadcast([P, NBLK * EG, EG, EG]), ALU.mult))
                ch(tt(cmp_[:, :, :], cmp_[:, :, :], tie[:, :, :], ALU.add))
                ch(nc.vector.tensor_reduce(rank[:, :, :].rearrange("p b (g e) -> p (b g) e", e=EG), table(cmp_),
                                           AX.X, ALU.add))
                ch(ts(A(M), A(rank), 2.0, None, ALU.is_lt))
                mv_ = M[:, :, :].rearrange("p b (g e) -> p b g e", e=EG)
                for k in range(EG):
                    last = tt(mv_[:, :, :, k], mv_[:, :, :, k], A(fg), ALU.mult)
                ch(last)
                ch(tt(A(gate), A(sc), A(M), ALU.mult))
                ch(nc.vector.tensor_reduce(ws[:, :], A(gate), AX.X, ALU.add))
                ch(nc.vector.reciprocal(ws[:, :], ws[:, :]))
                ch(tt(A(gate), A(gate), wide(ws[:, :], E), ALU.mult))
                ch(nc.vector.memset(M[NS:P, QB, :], 0.0))
                dve.sem_inc(m_ready, 1)
                dve.wait_ge(counted, 1)
                of_block = cnt[:, NBLK * E:2 * NBLK * E].rearrange("p (b e) -> p b e", b=NBLK)
                ch(nc.vector.memset(ahead[:, 0, :], 0.0))
                for b in range(NBLK):
                    ch(tt(ahead[:, b + 1, :], ahead[:, b, :], of_block[:, b, :], ALU.add))
                tot = ahead[:, NBLK, :]
                ch(tt(A(slot), cnt[:, 0:NBLK * E].rearrange("p (b e) -> p b e", b=NBLK), ahead[:, 0:NBLK, :], ALU.add))
                ch(ts(nb[:, :], tot, 1.0 / SLOTB, (SLOTB - 1.0) / SLOTB - 0.5 + 0.5 / SLOTB, ALU.mult, ALU.add))
                ch(ts(nb[:, :], nb[:, :], MAGIC, None, ALU.add))
                ch(ts(nb[:, :], nb[:, :], MAGIC, None, ALU.subtract))
                ch(nc.vector.tensor_tensor_scan(end[:, :], ones[:, 0:E], nb[:, :], 0.0, ALU.mult, ALU.add))
                ch(tt(beg[:, :], end[:, :], nb[:, :], ALU.subtract))
                ch(ts(beg[:, :], beg[:, :], float(SLOTB), None, ALU.mult))
                ch(tt(A(slot), A(slot), mid(beg[:, :], NBLK), ALU.add))
                FAR = float(1 << 20)
                ch(ts(A(slot), A(slot), FAR, None, ALU.subtract))
                ch(tt(A(lo), A(slot), A(M), ALU.mult))
                ch(nc.vector.tensor_reduce(sa[:, :], A(lo), AX.X, ALU.min))
                ch(tt(A(eq), A(lo), wide(sa[:, :], E), ALU.is_equal))
                ch(tt(A(lo), A(slot), A(M), ALU.mult))
                ch(tt(A(rank), A(M), A(eq), ALU.subtract))
                ch(tt(A(lo), A(slot), A(rank), ALU.mult))
                ch(nc.vector.tensor_reduce(sz[:, :], A(lo), AX.X, ALU.min))
                ch(ts(sa[:, :], sa[:, :], FAR, None, ALU.add))
                ch(ts(sz[:, :], sz[:, :], FAR, None, ALU.add))
                nc.vector.tensor_copy(s.slots[:, 0, :], sa[:, :])
                ch(nc.vector.tensor_copy(s.slots[:, 1, :], sz[:, :]))
                ts(blk[:, 0, :], sa[:, :], 1.0 / SLOTB, 0.5 / SLOTB - 0.5, ALU.mult, ALU.add)
                ch(ts(blk[:, 1, :], sz[:, :], 1.0 / SLOTB, 0.5 / SLOTB - 0.5, ALU.mult, ALU.add))
                ch(ts(A(blk), A(blk), MAGIC, None, ALU.add))
                ch(ts(A(blk), A(blk), MAGIC, None, ALU.subtract))
                stt(place[:, 0, :], blk[:, 0, :], -float(SLOTB), sa[:, :], ALU.mult, ALU.add)
                ch(stt(place[:, 1, :], blk[:, 1, :], -float(SLOTB), sz[:, :], ALU.mult, ALU.add))
                flat = lambda t: t[:, :, :].rearrange("p k b -> p (k b)")
                tt(A(same), mid(count[:, :], 2 * NBLK), wide(flat(place), P), ALU.is_equal)
                ch(tt(A(holds), mid(count[:, 0:NSB + 1], 2 * NBLK), wide(flat(blk), NSB + 1), ALU.is_equal))
                hv = holds[:, :, :].rearrange("p (k b) n -> p k b n", k=2)
                for k in range(2):
                    last = tt(hv[:, k, :, :], hv[:, k, :, :], wide(tok[:, :], NSB + 1), ALU.mult)
                ch(last)
                dve.sem_inc(slots_ready, 1)
                ch(tt(A(lo), A(gate), A(eq), ALU.mult))
                ch(nc.vector.tensor_reduce(s.gates[:, 0, :], A(lo), AX.X, ALU.add))
                ch(tt(A(lo), A(gate), A(rank), ALU.mult))
                ch(nc.vector.tensor_reduce(s.gates[:, 1, :], A(lo), AX.X, ALU.add))
                ch(ts(ne[:, :], nb[0:1, :], 0.0, None, ALU.is_gt))
                ch(nc.vector.tensor_reduce(top[:, :], ne[:, :], AX.X, ALU.add))
                ch(nc.vector.tensor_tensor_scan(w0[:, 0:E], ones[0:1, 0:E], ne[:, :], 0.0, ALU.mult, ALU.add))
                ch(ts(w0[:, 0:E], w0[:, 0:E], ne[:, 0:1], None, ALU.subtract))
                among = past[:, 0:E, :]
                ch(tt(among, wide(count[0:1, 0:E], E), mid(w0[:, 0:E], E), ALU.is_gt))
                ch(nc.vector.tensor_reduce(eb[:, 0:E], among, AX.X, ALU.add))
                ts(s.order[:, :], eb[:, 0:E], E - 1.0, None, ALU.min)
                ch(ts(w0[:, 0:1], top[:, :], 1.0, None, ALU.add))
                ch(ts(s.split_by[:, :], count[0:1, 0:E], ne[:, 0:1], w0[:, 0:1], ALU.add, ALU.min))
                ch(tt(A(past), wide(count[0:1, 0:NSB + 1], E), mid(end[0:1, :], NSB + 1), ALU.is_ge))
                ch(tt(A(past), A(past), mid(ne[:, :], NSB + 1), ALU.mult))
                ch(nc.vector.tensor_reduce(eb[:, :], A(past), AX.X, ALU.add))
                ch(ts(eb[:, :], eb[:, :], 1.0, top[:, :], ALU.add, ALU.min))
                nc.vector.tensor_copy(s.wtab[:, 1, :], eb[:, :])
                ts(s.wtab[:, 0, :], eb[:, :], 1.0, ne[:, 0:1], ALU.add, ALU.subtract)
                nc.vector.memset(new[:, 0:1], 1.0)
                ch(tt(new[:, 1:], eb[:, 1:], eb[:, 0:NSB], ALU.subtract))
                nc.vector.tensor_copy(s.wtab[:, 2, :], new[:, :])
                ch(ts(w0[:, :], eb[:, :], top[:, :], None, ALU.is_lt))
                tt(s.wtab[:, 3, :], new[:, :], w0[:, :], ALU.mult)
                ch(ts(nb[:, 0:1], end[:, E - 1:E], 0.5, 0.25, ALU.mult, ALU.add))
                ch(ts(nb[:, 0:1], nb[:, 0:1], MAGIC, None, ALU.add))
                ch(ts(nb[:, 0:1], nb[:, 0:1], MAGIC, None, ALU.subtract))
                ts(s.more_pairs[:, 0:1], nb[0:1, 0:1], 1.0, None, ALU.subtract)
                ch(ts(s.more_pairs[:, 1:2], nb[0:1, 0:1], -1.0, float(NSB // 2), ALU.mult, ALU.add))
                dve.wait_ge(placed, 1)
                nc.vector.tensor_copy(s.held[:, :], held[:, :])


def expert_weights(io, e, i):
    v = io[("moe_w_gate", "moe_w_up", "moe_w_down")[i]][0].rearrange("e (p k) f -> e p (k f)", p=P)
    return v[bass.ds(e, 1), :, :].rearrange("o p n -> p (o n)")


def experts(nc, io, s):
    with ExitStack() as c:
        sb = lambda n, sh, dt=F32: c.enter_context(nc.sbuf_tensor(n, sh, dt))
        sem = semaphores(nc, c)
        whi, wlo = sb("whi", [P, WCOLS], F32R), sb("wlo", [P, WCOLS], F32R)
        idxc = [sb(f"idxc{j}", [P, 1], I32) for j in range(2)]
        xg = [sb(f"xg{j}", [P, D]) for j in range(2)]
        xs = [[sb(f"exs{j}{i}", [P, D], F32R) for i in range(2)] for j in range(2)]
        hs = [[sb(f"ehs{j}{i}", [P, FE], F32R) for i in range(2)] for j in range(2)]
        yb = [sb(f"eyb{j}", [P, D]) for j in range(2)]
        th = [sb(f"eth{j}", [P, FE]) for j in range(2)]
        hh = [sb(f"ehh{j}", [P, FE]) for j in range(2)]
        nul = sb("enul", [P, D // 2])
        nul_set, nul_sent = sem("ex_nul_set"), sem("ex_nul_sent")
        all_sent, idle_cleared, gather_next = sem("ex_all_sent"), sem("ex_idle_cleared"), sem("ex_gather_next")
        psG = c.enter_context(nc.psum_tensor("psG", [P, FE], F32))
        psU = c.enter_context(nc.psum_tensor("psU", [P, FE], F32))
        psY = c.enter_context(nc.psum_tensor("psY", [P, D], F32))
        psX = c.enter_context(nc.psum_tensor("psX", [P, D], F32))
        psH = c.enter_context(nc.psum_tensor("psH", [P, FE], F32))
        (idx_kept, x_turned, x_kept, x_split, g_made, gu_made, tanhed, halfway, act_done, h_turned, h_kept, h_split,
         y_made, y_kept) = (sem("ex_" + n) for n in "idx_kept x_turned x_kept x_split g_made gu_made tanhed halfway "
                            "act_done h_turned h_kept h_split y_made y_kept".split())
        hi_made = [sem(f"ex_hi{i}") for i in range(3)]
        lo_made = [sem(f"ex_lo{i}") for i in range(3)]
        gathered = [sem(f"ex_gathered{j}") for j in range(2)]
        y_sent = [sem(f"ex_sent{j}") for j in range(2)]
        w_in = [sem(f"ex_w{i}") for i in range(3)]

        def over_pairs(eng, pair):
            more = eng.value_load(s.more_pairs[0:1, 0:1], min_val=USED_PAIRS - 1, max_val=NSB // 2 - 2)
            pair(0, True)
            pair(1, False)
            with eng.Fori(2, NSB // 2) as bb:
                with eng.If(bb <= more):
                    pair(bb, False)
            return more

        def entry(eng, row, b, lo, hi):
            return eng.value_load(s.wtab[0:1, row, bass.ds(b, 1)], min_val=lo, max_val=hi)

        with nc.Block() as block:
            @block.sync
            def _(sp):
                for i in range(2):
                    sp.sem_inc(w_in[i], 16)
                with sp.Fori(1, E) as r:
                    e = sp.value_load(s.order[0:1, bass.ds(r, 1)], min_val=0, max_val=E - 1)
                    free = sp.value_load(s.split_by[0:1, bass.ds(r, 1)], min_val=1, max_val=E + 1)
                    for i in range(2):
                        sp.wait_ge(w_in[i], 16 * r)
                        sp.wait_ge(lo_made[i], free)
                        sp.dma_start(s.raw[:, slice(*PIECES[i])], expert_weights(io, e, i)).then_inc(w_in[i], 16)
                more = sp.value_load(s.more_pairs[0:1, 0:1], min_val=USED_PAIRS - 1, max_val=NSB // 2 - 2)
                idle = sp.value_load(s.more_pairs[0:1, 1:2], min_val=1, max_val=NSB // 2 - USED_PAIRS)
                sp.wait_ge(nul_set, 1)
                with sp.Fori(1, NSB // 2) as bb:
                    with sp.If(bb > more):
                        for half in range(2):
                            cols = slice(half * D // 2, (half + 1) * D // 2)
                            dst = s.yd[bass.ds(bb * (2 * SLOTB), 2 * SLOTB), cols].rearrange("(j p) d -> p j d", p=P)
                            sp.dma_start(dst, nul[:, :].unsqueeze(1).to_broadcast([P, 2, D // 2])).then_inc(nul_sent, 16)
                sp.wait_ge(nul_sent, 32 * idle)
                sp.sem_inc(idle_cleared, 1)
                sp.wait_ge(idle_cleared, 1)
                for i in range(2):
                    sp.wait_ge(w_in[i], 16 * E)

            @block.gpsimd
            def _(pool):
                nc.gpsimd.memset(nul[:, :], 0.0).then_inc(nul_set, 1)

                def gather(b, j):
                    nc.gpsimd.tensor_copy(idxc[j][:, :], s.held[:, bass.ds(b, 1)]).then_inc(idx_kept, 1)
                    pool.wait_ge(idx_kept, b + 1)
                    pool.sem_inc(gather_next, 1)
                    pool.wait_ge(nul_set, 1)
                    nc.gpsimd.indirect_dma_start(xg[j][:, :], None, s.x1d,
                                                 bass.IndirectOffsetOnAxis(ap=idxc[j][:, 0:1], axis=0)) \
                        .then_inc(gathered[j], 16)

                gather(0, 0)

                def pair(bb, first):
                    for j in range(2):
                        b = 2 * bb + j
                        if not (first and j == 0):
                            pool.wait_ge(x_turned, b)
                        gather(b + 1, 1 - j)

                more = over_pairs(pool, pair)
                pool.wait_ge(gathered[0], 16 * more + 32)
                pool.wait_ge(gathered[1], 16 * more + 16)

            @block.tensor
            def _(pe):
                def turn_x(b, j, loads):
                    pe.wait_ge(gathered[j], 16 * loads)
                    xv = xg[j][:, :].rearrange("t (p k) -> t k p", k=KD)
                    for k in range(KD):
                        last = pe.transpose(psX[:, k * P:(k + 1) * P], xv[:, k, :], s.ident[:, :])
                    last.then_inc(x_turned, 1)

                def product(out, x, steps, at):
                    for k in range(steps):
                        hi, lo = (part[:, k * P:(k + 1) * P] for part in x)
                        w_hi, w_lo = (part[:, at(k):at(k) + 512] for part in (whi, wlo))
                        pe.matmul(out, hi, w_hi, start=(k == 0), stop=False)
                        pe.matmul(out, hi, w_lo, start=False, stop=False)
                        last = pe.matmul(out, lo, w_hi, start=False, stop=(k == steps - 1))
                    return last

                def gate_up(b, j, first):
                    count = entry(pe, 1, b, 1, E) + 1
                    pe.wait_ge(lo_made[0], count)
                    pe.wait_ge(x_split, b + 1)
                    if not (first and j == 0):
                        pe.wait_ge(act_done, b)
                    product(psG[:, :], xs[j], KD, lambda k: GATE_AT + k * FE).then_inc(g_made, 1)
                    pe.wait_ge(lo_made[1], count)
                    product(psU[:, :], xs[j], KD, lambda k: UP_AT + k * FE).then_inc(gu_made, 1)

                def turn_h(b, j, first):
                    pe.wait_ge(act_done, b + 1)
                    if not (first and j == 0):
                        pe.wait_ge(h_split, b)
                    hv = hh[j][:, :].rearrange("t (p k) -> t k p", k=KF)
                    for k in range(KF):
                        last = pe.transpose(psH[:, k * P:(k + 1) * P], hv[:, k, :], s.ident[:, :])
                    last.then_inc(h_turned, 1)

                def down(b, j, old):
                    count = entry(pe, 1, b, 1, E) + 1
                    pe.wait_ge(lo_made[2], count)
                    pe.wait_ge(h_split, b + 1)
                    if old:
                        pe.wait_ge(y_kept, b)
                    for half in range(2):
                        last = product(psY[:, half * 512:half * 512 + 512], hs[j], KF,
                                       lambda k: DOWN_AT + k * D + half * 512)
                    last.then_inc(y_made, 1)

                turn_x(0, 0, 1)

                def pair(bb, first):
                    for j in range(2):
                        b = 2 * bb + j
                        gate_up(b, j, first)
                        pe.wait_ge(x_split, b + 1)
                        turn_x(b + 1, 1 - j, bb + 1 + j)
                        if not (first and j == 0):
                            down(b - 1, 1 - j, not (first and j == 1))
                        turn_h(b, j, first)

                more = over_pairs(pe, pair)
                down(2 * more + 1, 1, True)

            @block.scalar
            def _(act):
                def high(b, i, after=None):
                    act.wait_ge(w_in[i], 16 * entry(act, 0, b, 1, E))
                    if after is not None:
                        act.wait_ge(*after)
                    at = slice(*PIECES[i])
                    nc.scalar.activation(whi[:, at], s.raw[:, at], ACT.Copy).then_inc(hi_made[i], 1)

                def keep_x(b, j, old):
                    act.wait_ge(x_turned, b + 1)
                    if old:
                        act.wait_ge(gu_made, b - 1)
                    nc.scalar.activation(xs[j][0][:, :], psX[:, :], ACT.Copy).then_inc(x_kept, 1)

                def keep_h(b, j, first):
                    act.wait_ge(h_turned, b + 1)
                    if not first:
                        act.wait_ge(y_made, b - 1)
                    nc.scalar.activation(hs[j][0][:, :], psH[:, :], ACT.Copy).then_inc(h_kept, 1)

                def keep_y(b, j, bb):
                    act.wait_ge(y_made, b + 1)
                    if bb is not None:
                        act.wait_ge(y_sent[j], 16 * bb)
                    nc.scalar.activation(yb[j][:, :], psY[:, :], ACT.Copy).then_inc(y_kept, 1)
                    act.wait_ge(y_kept, b + 1)
                    act.dma_start(s.yd[bass.ds(b * P, P), :], yb[j][:, :]).then_inc(y_sent[j], 16)

                def load_down(r):
                    e = act.value_load(s.order[0:1, bass.ds(r, 1)], min_val=0, max_val=E - 1)
                    act.dma_start(s.raw[:, slice(*PIECES[2])], expert_weights(io, e, 2)).then_inc(w_in[2], 16)

                high(0, 0)
                keep_x(0, 0, False)
                load_down(0)
                with act.If(entry(act, 0, 0, 1, E) > 1):
                    act.wait_ge(w_in[2], 16)
                    load_down(1)
                high(0, 1)
                high(0, 2)

                def pair(bb, first):
                    for j in range(2):
                        b = 2 * bb + j
                        new = entry(act, 2, b + 1, 0, 1)
                        with act.If(new > 0):
                            high(b + 1, 0, (g_made, b + 1))
                        act.wait_ge(g_made, b + 1)
                        if not first:
                            act.wait_ge(act_done, b - 1)
                        nc.scalar.activation(th[j][:, :], psG[:, :], ACT.Tanh, scale=0.5).then_inc(tanhed, 1)
                        if not (first and j == 0):
                            with act.If(entry(act, 3, b - 1, 0, 1) > 0):
                                r, count = entry(act, 0, b - 1, 1, E - 1), entry(act, 1, b - 1, 1, E)
                                act.wait_ge(lo_made[2], count + 1)
                                load_down(r)
                        with act.If(new > 0):
                            high(b + 1, 1, (gu_made, b + 1))
                        keep_x(b + 1, 1 - j, not (first and j == 0))
                        if not (first and j == 0):
                            keep_y(b - 1, 1 - j, bb - 1 + j if type(bb) is not int or bb - 1 + j > 0 else None)
                        keep_h(b, j, first)
                        if not (first and j == 0):
                            new = entry(act, 2, b, 0, 1)
                            with act.If(new > 0):
                                high(b, 2, (y_made, b))

                more = over_pairs(act, pair)
                keep_y(2 * more + 1, 1, more)
                loads = entry(act, 0, NSB, 1, E)
                act.wait_ge(y_sent[0], 16 * more + 16)
                act.wait_ge(y_sent[1], 16 * more + 16)
                act.wait_ge(w_in[2], 16 * loads)
                act.sem_inc(all_sent, 1)
                act.wait_ge(all_sent, 1)

            @block.vector
            def _(dve):
                def low(b, i):
                    at = slice(*PIECES[i])
                    dve.wait_ge(hi_made[i], entry(dve, 1, b, 1, E))
                    nc.vector.tensor_tensor(wlo[:, at], s.raw[:, at], whi[:, at].bitcast(F32), ALU.subtract) \
                        .then_inc(lo_made[i], 1)

                def low_x(b, j):
                    dve.wait_ge(x_kept, b + 1)
                    nc.vector.tensor_tensor(xs[j][1][:, :], psX[:, :], xs[j][0][:, :].bitcast(F32), ALU.subtract) \
                        .then_inc(x_split, 1)

                for i in range(3):
                    dve.sem_inc(lo_made[i], 1)
                low(0, 0)
                low_x(0, 0)
                low(0, 1)
                low(0, 2)

                def pair(bb, first):
                    for j in range(2):
                        b = 2 * bb + j
                        new = entry(dve, 2, b + 1, 0, 1)
                        with dve.If(new > 0):
                            low(b + 1, 0)
                        dve.wait_ge(tanhed, b + 1)
                        nc.vector.scalar_tensor_tensor(th[j][:, :], th[j][:, :], 1.0, psG[:, :], ALU.add, ALU.mult) \
                            .then_inc(halfway, 1)
                        dve.wait_ge(halfway, b + 1)
                        dve.wait_ge(gu_made, b + 1)
                        if not first:
                            dve.wait_ge(h_turned, b - 1)
                        nc.vector.scalar_tensor_tensor(hh[j][:, :], th[j][:, :], 0.5, psU[:, :], ALU.mult, ALU.mult) \
                            .then_inc(act_done, 1)
                        low_x(b + 1, 1 - j)
                        with dve.If(new > 0):
                            low(b + 1, 1)
                        dve.wait_ge(h_kept, b + 1)
                        nc.vector.tensor_tensor(hs[j][1][:, :], psH[:, :], hs[j][0][:, :].bitcast(F32), ALU.subtract) \
                            .then_inc(h_split, 1)
                        if not (first and j == 0):
                            new = entry(dve, 2, b, 0, 1)
                            with dve.If(new > 0):
                                low(b, 2)

                over_pairs(dve, pair)


def combine(nc, io, s):
    with ExitStack() as c:
        sb = lambda n, sh, dt=F32: c.enter_context(nc.sbuf_tensor(n, sh, dt))
        sem = semaphores(nc, c)
        lg, lb = sb("cg", [P, D]), sb("cb", [P, D])
        ya = [[sb(f"ya{k}{j}", [P, D]) for j in range(4)] for k in range(2)]
        x1 = [sb(f"x1{j}", [P, D]) for j in range(4)]
        t = [sb(f"ct{j}", [P, D]) for j in range(3)]
        out = [sb(f"co{j}", [P, D]) for j in range(3)]
        diag = sb("cdiag", [P, NBLK, 2, P])
        alpha = sb("calpha", [P, P])
        bk = [c.enter_context(nc.psum_tensor(f"pc{k}", [P, D], F32)) for k in range(3)]
        st, mv = sb("cst", [P, 2, 6]), sb("cmv", [P, NBLK, 5])
        l_in, seq, diag_set, taken, var_ready, rooted, stats_ready, normalised, weighted, biased = (
            sem("co_" + n) for n in "l_in seq diag taken var rooted stats normalised weighted biased".split())
        y_in = [sem(f"co_y{j}") for j in range(4)]
        x_in = [sem(f"co_x{j}") for j in range(4)]
        o_out = [sem(f"co_o{j}") for j in range(3)]

        with nc.Block() as block:
            @block.gpsimd
            def _(pool):
                def gather(b):
                    r = rows(b)
                    if b >= 4:
                        pool.wait_ge(taken, b - 3)
                    for k in range(2):
                        nc.gpsimd.indirect_dma_start(
                            ya[k][b % 4][0:r, :], None, s.yd,
                            bass.IndirectOffsetOnAxis(ap=s.slots[0:r, k, b:b + 1], axis=0)).then_inc(y_in[b % 4], 16)

                for b in range(NBLK):
                    gather(b)

            @block.sync
            def _(sp):
                sp.dma_start(lg[:, :], io["ln2_g"].to_broadcast([P, D])).then_inc(l_in, 16)
                sp.dma_start(lb[:, :], io["ln2_b"].to_broadcast([P, D])).then_inc(l_in, 16)

                def load(b):
                    r = rows(b)
                    sp.dma_start(x1[b % 4][0:r, :], s.x1d[b * P:b * P + r, :]).then_inc(x_in[b % 4], 16)

                for b in range(4):
                    load(b)
                for b in range(NBLK):
                    r = rows(b)
                    if b + 4 < NBLK:
                        sp.wait_ge(taken, b + 1)
                        load(b + 4)
                    sp.wait_ge(biased, b + 1)
                    dst = io["y_prompt"][0, b * P:(b + 1) * P, :] if b < QB else io["y_sample"].rearrange("b t d -> (b t) d")
                    sp.dma_start(dst, out[b % 3][0:r, :]).then_inc(o_out[b % 3], 16)
                for j in range(3):
                    sp.wait_ge(o_out[j], 16 * (NBLK // 3))

            @block.tensor
            def _(pe):
                pe.wait_ge(diag_set, 1)
                for b in range(NBLK):
                    r = rows(b)
                    pe.wait_ge(y_in[b % 4], 32 * (b // 4 + 1))
                    pe.wait_ge(x_in[b % 4], 16 * (b // 4 + 1))
                    if b >= 3:
                        pe.wait_ge(normalised, b - 2)
                    for half in range(2):
                        cols = slice(half * 512, half * 512 + 512)
                        out = bk[b % 3][0:r, cols]
                        pe.matmul(out, alpha[0:r, 0:r], x1[b % 4][0:r, cols], start=True, stop=False)
                        pe.matmul(out, diag[0:r, b, 0, 0:r], ya[0][b % 4][0:r, cols], start=False, stop=False)
                        last = pe.matmul(out, diag[0:r, b, 1, 0:r], ya[1][b % 4][0:r, cols], start=False, stop=True)
                    last.then_inc(taken, 1)

            @block.scalar
            def _(act):
                for b in range(NBLK):
                    r = rows(b)
                    act.wait_ge(var_ready, b + 1)
                    nc.scalar.activation(mv[0:r, b, 2:3], mv[0:r, b, 2:3], ACT.Sqrt).then_inc(rooted, 1)
                    act.wait_ge(stats_ready, b + 1)
                    if b >= 3:
                        act.wait_ge(weighted, b - 2)
                    nc.scalar.activation(t[b % 3][0:r, :], bk[b % 3][0:r, :], ACT.Identity,
                                         scale=mv[0:r, b, 3:4], bias=mv[0:r, b, 4:5]) \
                        .then_inc(normalised, 1)

            @block.vector
            def _(dve):
                ch = Chain(dve, seq)

                def weigh(b):
                    r = rows(b)
                    dve.wait_ge(normalised, b + 1)
                    if b == 0:
                        dve.wait_ge(l_in, 32)
                    if b >= 3:
                        dve.wait_ge(o_out[b % 3], 16 * (b // 3))
                    nc.vector.tensor_tensor(out[b % 3][0:r, :], t[b % 3][0:r, :], lg[0:r, :], ALU.mult) \
                        .then_inc(weighted, 1)
                    dve.wait_ge(weighted, b + 1)
                    nc.vector.tensor_tensor(out[b % 3][0:r, :], out[b % 3][0:r, :], lb[0:r, :], ALU.add) \
                        .then_inc(biased, 1)

                nc.vector.tensor_scalar(alpha[:, :], s.ident[:, :], ALPHA, None, ALU.mult)
                for b in range(NBLK):
                    for k in range(2):
                        last = nc.vector.tensor_scalar(diag[:, b, k, :], s.ident[:, :], s.gates[:, k, b:b + 1], None,
                                                       ALU.mult)
                last.then_inc(diag_set, 1)
                for b in range(NBLK):
                    r = rows(b)
                    tb, m = bk[b % 3][0:r, :], mv[0:r, b, :]
                    dve.wait_ge(taken, b + 1)
                    nc.vector.bn_stats(st[0:r, 0, :], tb[:, 0:512])
                    ch(nc.vector.bn_stats(st[0:r, 1, :], tb[:, 512:D]))
                    ch(nc.vector.bn_aggr(m[:, 0:2], st[0:r, :, :].rearrange("p a b -> p (a b)")))
                    nc.vector.tensor_scalar(m[:, 2:3], m[:, 1:2], EPS, None, ALU.add).then_inc(var_ready, 1)
                    if b >= 1:
                        weigh(b - 1)
                    dve.wait_ge(rooted, b + 1)
                    ch(nc.vector.reciprocal(m[:, 3:4], m[:, 2:3]))
                    nc.vector.tensor_scalar(m[:, 4:5], m[:, 0:1], m[:, 3:4], -1.0, ALU.mult, ALU.mult) \
                        .then_inc(stats_ready, 1)
                weigh(NBLK - 1)


def constants():
    ident = np.eye(P, dtype=np.float32)
    slope = 2.0 ** (-8.0 * np.arange(1, H + 1, dtype=np.float32) / H)
    dist = np.arange(P)[:, None] - (np.arange(SEQ)[None, :] - (SEQ - P))
    bias = np.where(dist[:, None, :] >= 0, -slope[None, :, None] * dist[:, None, :], NEG)
    r = np.arange(P)
    seq, t = (r % NS) // T_DEC, r % T_DEC
    past = PAST + t[:, None] - np.arange(PAST)[None, :]
    new = t[:, None] - (np.arange(NS) % T_DEC)[None, :]
    same = seq[:, None] == (np.arange(NS) // T_DEC)[None, :]
    dist_s = np.concatenate([past, np.where(same, new, -1)], 1)
    bias_s = np.where(dist_s[:, None, :] >= 0, -slope[None, :, None] * dist_s[:, None, :], NEG)
    two = np.concatenate([np.eye(NS), np.eye(NS)], 0)
    sel = np.stack([r < NS, r >= NS], 1).astype(np.float32)
    f = lambda a: np.ascontiguousarray(a, dtype=np.float32)
    before = r[:, None] < r[None, :]
    tok = np.arange(NBLK)[None, :] * P + r[:, None]
    return {"c_before": f(before), "c_tok": f(tok), "c_count": f(np.tile(r, (P, 1))),
            "c_lower": f(np.tile(np.tri(EG, EG, -1), (P, 1, 1))), "c_ident": ident, "c_bias": f(bias),
            "c_bias_s": f(bias_s), "c_two": f(two), "c_sel": f(sel)}


class Stage:
    pass


def layouts(i):
    pair = lambda a: np.asarray(a).reshape(PR, 2, ST).transpose(1, 2, 0).reshape(P, PR)
    par = np.stack([pair(i["ssm_lambda_re"][0]), pair(i["ssm_lambda_im"][0]),
                    pair(np.repeat(np.asarray(i["ssm_log_dt"][0])[:, None], ST, 1))], 1)
    out = {"l_par": par}
    for n in "re", "im":
        out["l_b" + n] = np.asarray(i["ssm_b_" + n][0]).reshape(PR, 2, ST, GC).transpose(1, 2, 0, 3).reshape(P, PR, GC)
        cc = np.asarray(i["ssm_c_" + n][0]).reshape(PR, 2, GC, ST).transpose(1, 3, 0, 2)
        out["l_c" + n] = cc.reshape(P, PR, GC)
        blk = np.zeros((2, ST, PR, 2, GC), np.float32)
        for r in range(2):
            blk[r, :, :, r, :] = cc[r]
        out["l_cb" + n[0]] = blk.reshape(P, PR, 2 * GC)
        h = np.asarray(i["state_ssm_" + n][0]).reshape(NB_DEC, PR, 2, ST).transpose(2, 3, 1, 0)
        out["l_h0" + n[0]] = h.reshape(P, PR, NB_DEC)
    d = np.asarray(i["ssm_d"][0]).reshape(G, GC)
    kd = np.zeros((P, G, GC), np.float32)
    for ch in range(GC):
        kd[P - GC + ch, :, ch] = d[:, ch]
    out["l_d"] = kd.reshape(P, W)
    out["l_bglu"] = np.asarray(i["ssm_b_glu"][0]).reshape(W // P, P).T
    return {k: np.ascontiguousarray(v) for k, v in out.items()}


def program(nc, io):
    s = Stage()
    with ExitStack() as c:
        sb = lambda n, sh, dt=F32: c.enter_context(nc.sbuf_tensor(n, sh, dt))
        s.ident = sb("ident", [P, P])
        s.lgt = sb("lgt", [P, NBLK, E])
        s.slots = sb("slots", [P, 2, NBLK], I32)
        s.gates = sb("gates", [P, 2, NBLK])
        s.wtab = sb("wtab", [1, 4, NSB + 1], I32)
        s.order = sb("order", [1, E], I32)
        s.split_by = sb("split_by", [1, E], I32)
        s.held = sb("held", [P, NSB + 1], I32)
        s.more_pairs = sb("more_pairs", [1, 2], I32)
        s.x1d = nc.dram_tensor("x1d", [N, D], F32).ap()
        s.yd = nc.dram_tensor("yd", [NSB * SLOTB, D], F32).ap()
        s.nlam = sb("nlam", [P, 1])
        with ExitStack() as w:
            with ExitStack() as m:
                sm = lambda n, sh, dt=F32: m.enter_context(nc.sbuf_tensor(n, sh, dt))
                s.aT = sm("aT", [P, H, N])
                s.qT = sm("qT", [P, H, N])
                s.gT = s.qT
                token_mixing(nc, io, s)
                s.raw = w.enter_context(nc.sbuf_tensor("raw", [P, WCOLS], F32, side="right"))
                mix(nc, io, s)
                route(nc, io, s)
            experts(nc, io, s)
        combine(nc, io, s)


def token_mixing(nc, io, s):
    with ExitStack() as c:
        sb = lambda n, sh, dt=F32: c.enter_context(nc.sbuf_tensor(n, sh, dt))
        s.uc = sb("uc", [P, G, L, GC])
        s.us = sb("us", [NS, W])
        with ExitStack() as a:
            sa = lambda n, sh, dt=F32: a.enter_context(nc.sbuf_tensor(n, sh, dt))
            s.v = sa("v", [P, NBLK, W])
            s.kT = sa("kT", [P, H, N])
            project(nc, io, s)
            s.o = sa("o", [P, NBLK, W])
            s.ss = sa("ss", [P, NBLK, H])
            s.ptab = sa("ptab", [1, NB_DEC * NPG], I32)
            s.kc = sa("kc", [P, NB_DEC * NPG, W])
            attend(nc, io, s)
            sample(nc, io, s)
            head_norm(nc, io, s)
        with ExitStack() as a:
            sa = lambda n, sh, dt=F32: a.enter_context(nc.sbuf_tensor(n, sh, dt))
            s.T = sa("T", [P, G, P])
            s.VTr = sa("VTr", [P, PR, P])
            s.VTi = sa("VTi", [P, PR, P])
            s.CAr = sa("CAr", [P, PR, L, GC])
            s.CAi = sa("CAi", [P, PR, L, GC])
            s.Er = sa("Er", [P, PR, CH])
            s.Ei = sa("Ei", [P, PR, CH])
            s.m8 = sa("m8", [P, PR])
            s.a8 = sa("a8", [P, 2, PR])
            s.us8 = sa("us8", [NB_DEC, G, L, GC])
            s.U = sa("U", [P, G, NC])
            s.work = [sa(f"work{n}", [P, PR, CH]) for n in range(4)]
            ssm_tables(nc, io, s)
            ssm_scan(nc, io, s)


_DIRECT = ["x_prompt", "x_sample", "cache_k", "cache_v", "page_table", "w_in", "w_out", "ln1_g", "ln1_b", "ln2_g",
           "ln2_b", "lambda_q1", "lambda_k1", "lambda_q2", "lambda_k2", "subln_g", "ssm_w_glu", "router_w",
           "router_bias", "moe_w_gate", "moe_w_up", "moe_w_down"]
_OUTS = {"y_prompt": (1, SEQ, D), "y_sample": (NB_DEC, T_DEC, D),
         "new_k_prompt": (1, 1, SEQ, H, P), "new_v_prompt": (1, 1, SEQ, H, P),
         "new_k_sample": (1, NB_DEC, T_DEC, H, P), "new_v_sample": (1, NB_DEC, T_DEC, H, P),
         "h_prompt": (P, 2, PR), "h_sample": (P, 2, PR, NB_DEC)}


def kernel(**inputs):
    import concourse.bacc as bacc
    from concourse.bass_utils import run_bass_kernel_spmd

    nc = bacc.Bacc("TRN2", target_bir_lowering=False, num_devices=1)
    given = {n: np.ascontiguousarray(inputs[n]) for n in _DIRECT}
    given.update(layouts(inputs))
    given.update(constants())
    io = {n: nc.dram_tensor("in_" + n, a.shape, mybir.dt.from_np(a.dtype), kind="ExternalInput").ap()
          for n, a in given.items()}
    for n, shape in _OUTS.items():
        io[n] = nc.dram_tensor("out_" + n, shape, F32, kind="ExternalOutput").ap()
    program(nc, io)
    got = run_bass_kernel_spmd(nc, [{"in_" + n: a for n, a in given.items()}], core_ids=[0]).results[0]
    out = {n: got["out_" + n] for n in _OUTS}
    hp = out["h_prompt"].reshape(2, ST, 2, PR).transpose(2, 3, 0, 1).reshape(2, 1, 1, G, ST)
    hs = out["h_sample"].reshape(2, ST, 2, PR, NB_DEC).transpose(2, 4, 3, 0, 1).reshape(2, 1, NB_DEC, G, ST)
    return (out["y_prompt"], out["y_sample"], out["new_k_prompt"], out["new_v_prompt"], hp[0], hp[1],
            out["new_k_sample"], out["new_v_sample"], hs[0], hs[1])
```
